# Optimizing a Trainium2 kernel written in Bass

```python
import jax, jax.numpy as jnp
from jax import lax
import numpy as np

D_MODEL = 1024
BATCH = 1
SEQ = 512
DEPTH = 2

GRID_W = 64
CTX_LEN = 256
N_Q_HEADS = 8
N_KV_HEADS = 2
Q_PER_KV = N_Q_HEADS // N_KV_HEADS
HEAD_DIM = 64
WINDOW = 128
ATTN_BLOCK = WINDOW
ROPE_THETA = 10000.0
FNET_GROUPS = 4
FNET_GROUP_DIM = 128
ATTN_WIDTH = N_Q_HEADS * HEAD_DIM
KV_WIDTH = N_KV_HEADS * HEAD_DIM
FNET_WIDTH = FNET_GROUPS * FNET_GROUP_DIM
AB_IN_WIDTH = ATTN_WIDTH + 2 * KV_WIDTH + FNET_WIDTH
AB_OUT_WIDTH = ATTN_WIDTH + FNET_WIDTH
SGU_GROUPS = 8
SGU_GROUP_DIM = 128
SGU_WIDTH = SGU_GROUPS * SGU_GROUP_DIM
SGU_CHUNK = 128
PEER_HEADS = 8
PEER_NKEYS = 128
PEER_TOPK = 16
PEER_KEY_DIM = 256
PEER_EXPERTS = PEER_NKEYS * PEER_NKEYS
PEER_BLOCK = 128
N_MOD = 6
N_EVEN = (DEPTH + 1) // 2
N_ODD = DEPTH // 2
RMS_EPS = 1e-6
NEG_INF = -1e30

kernel_name = "hybrid_dit_swa_fnet_sgu_peer"

def rmsnorm(x, w):
    x32 = x.astype(jnp.float32)
    y = x32 * lax.rsqrt(jnp.mean(x32 * x32, axis=-1, keepdims=True) + RMS_EPS)
    return (y * w.astype(jnp.float32)).astype(x.dtype)

def modulate(h, shift, scale):
    return h * (1 + scale) + shift

def ada_params(cond, w, b):
    m = jax.nn.silu(cond) @ w + b
    return jnp.split(m, N_MOD, axis=-1)

def axial_angles(n_tokens):
    rows = n_tokens // GRID_W
    r, cl = jnp.meshgrid(jnp.arange(rows), jnp.arange(GRID_W), indexing="ij")
    row = r.reshape(-1).astype(jnp.float32)
    col = cl.reshape(-1).astype(jnp.float32)
    half = HEAD_DIM // 2
    inv = ROPE_THETA ** (-jnp.arange(0, half, 2, dtype=jnp.float32) / half)
    return row[:, None] * inv, col[:, None] * inv

def rope_half(x, ang):
    h = x.shape[-1] // 2
    a, b = x[..., :h], x[..., h:]
    shape = (ang.shape[0],) + (1,) * (x.ndim - 3) + (h,)
    cos = jnp.cos(ang).reshape(shape).astype(x.dtype)
    sin = jnp.sin(ang).reshape(shape).astype(x.dtype)
    return jnp.concatenate([a * cos - b * sin, b * cos + a * sin], axis=-1)

def rope_axial(x, ang_row, ang_col):
    h = HEAD_DIM // 2
    return jnp.concatenate([rope_half(x[..., :h], ang_row), rope_half(x[..., h:], ang_col)], axis=-1)

def banded(t, nb):
    pad = [(0, 0), (ATTN_BLOCK, ATTN_BLOCK)] + [(0, 0)] * (t.ndim - 2)
    tp = jnp.pad(t, pad).reshape((t.shape[0], nb + 2, ATTN_BLOCK) + t.shape[2:])
    return jnp.concatenate([tp[:, :-2], tp[:, 1:-1], tp[:, 2:]], axis=2)

def latent_window_attention(q, k, v, k_ctx, v_ctx, sink):
    B, S = q.shape[:2]
    nb = S // ATTN_BLOCK
    scale = HEAD_DIM ** -0.5
    qb = q.reshape(B, nb, ATTN_BLOCK, N_KV_HEADS, Q_PER_KV, HEAD_DIM)
    kb = banded(k, nb)
    vb = banded(v, nb)
    qi = jnp.arange(ATTN_BLOCK)[:, None]
    kj = jnp.arange(3 * ATTN_BLOCK)[None, :] - ATTN_BLOCK
    kpos = jnp.arange(nb)[:, None, None] * ATTN_BLOCK + kj
    mask = (jnp.abs(qi - kj) <= WINDOW) & (kpos >= 0) & (kpos < S)
    s_loc = jnp.einsum("bnqhgd,bnkhd->bnhgqk", qb, kb).astype(jnp.float32) * scale
    s_loc = jnp.where(mask[None, :, None, None], s_loc, NEG_INF)
    s_ctx = jnp.einsum("bnqhgd,bchd->bnhgqc", qb, k_ctx).astype(jnp.float32) * scale
    sk = sink.astype(jnp.float32).reshape(N_KV_HEADS, Q_PER_KV)[:, :, None, None]
    m = jnp.maximum(jnp.maximum(s_loc.max(-1, keepdims=True), s_ctx.max(-1, keepdims=True)), sk)
    p_loc = jnp.exp(s_loc - m)
    p_ctx = jnp.exp(s_ctx - m)
    inv_den = 1.0 / (p_loc.sum(-1, keepdims=True) + p_ctx.sum(-1, keepdims=True) + jnp.exp(sk - m))
    o = (jnp.einsum("bnhgqk,bnkhd->bnqhgd", (p_loc * inv_den).astype(v.dtype), vb)
         + jnp.einsum("bnhgqc,bchd->bnqhgd", (p_ctx * inv_den).astype(v.dtype), v_ctx))
    return o.reshape(B, S, ATTN_WIDTH)

def context_attention(q, k, v, sink):
    B, C = q.shape[:2]
    scale = HEAD_DIM ** -0.5
    s = jnp.einsum("bqhgd,bkhd->bhgqk", q, k).astype(jnp.float32) * scale
    sk = sink.astype(jnp.float32).reshape(N_KV_HEADS, Q_PER_KV)[:, :, None, None]
    m = jnp.maximum(s.max(-1, keepdims=True), sk)
    p = jnp.exp(s - m)
    p = p / (p.sum(-1, keepdims=True) + jnp.exp(sk - m))
    o = jnp.einsum("bhgqk,bkhd->bqhgd", p.astype(v.dtype), v)
    return o.reshape(B, C, ATTN_WIDTH)

def fourier_mix(f):
    B, n = f.shape[:2]
    fg = f.reshape(B, n, FNET_GROUPS, FNET_GROUP_DIM).astype(jnp.float32)
    y = jnp.fft.fft2(fg, axes=(1, 3), norm="ortho").real
    return y.reshape(B, n, FNET_WIDTH).astype(f.dtype)

def ab_mixer(h_l, h_c, w_in, w_out, sink, ang_row, ang_col, with_ctx_out):
    B, S = h_l.shape[:2]
    C = h_c.shape[1]
    p_l = h_l @ w_in
    q_l = p_l[..., :ATTN_WIDTH].reshape(B, S, N_KV_HEADS, Q_PER_KV, HEAD_DIM)
    k_l = p_l[..., ATTN_WIDTH:ATTN_WIDTH + KV_WIDTH].reshape(B, S, N_KV_HEADS, HEAD_DIM)
    v_l = p_l[..., ATTN_WIDTH + KV_WIDTH:ATTN_WIDTH + 2 * KV_WIDTH].reshape(B, S, N_KV_HEADS, HEAD_DIM)
    f_l = p_l[..., ATTN_WIDTH + 2 * KV_WIDTH:]
    q_l = rope_axial(q_l, ang_row, ang_col)
    k_l = rope_axial(k_l, ang_row, ang_col)
    off = ATTN_WIDTH if with_ctx_out else 0
    p_c = h_c @ (w_in if with_ctx_out else w_in[:, ATTN_WIDTH:ATTN_WIDTH + 2 * KV_WIDTH])
    k_c = p_c[..., off:off + KV_WIDTH].reshape(B, C, N_KV_HEADS, HEAD_DIM)
    v_c = p_c[..., off + KV_WIDTH:off + 2 * KV_WIDTH].reshape(B, C, N_KV_HEADS, HEAD_DIM)
    a_l = latent_window_attention(q_l, k_l, v_l, k_c, v_c, sink)
    y_l = jnp.concatenate([a_l, fourier_mix(f_l)], axis=-1) @ w_out
    y_c = None
    if with_ctx_out:
        q_c = p_c[..., :ATTN_WIDTH].reshape(B, C, N_KV_HEADS, Q_PER_KV, HEAD_DIM)
        f_c = p_c[..., ATTN_WIDTH + 2 * KV_WIDTH:]
        a_c = context_attention(q_c, k_c, v_c, sink)
        y_c = jnp.concatenate([a_c, fourier_mix(f_c)], axis=-1) @ w_out
    return y_l, y_c

def sgu_mixer(h, w_in, norm_w, w_s, b_s, w_out):
    B, n = h.shape[:2]
    nc = n // SGU_CHUNK
    z = jax.nn.gelu(h @ w_in)
    u, v = z[..., :SGU_WIDTH], z[..., SGU_WIDTH:]
    v = rmsnorm(v, norm_w).reshape(B, nc, SGU_CHUNK, SGU_GROUPS, SGU_GROUP_DIM)
    sv = jnp.einsum("gpq,bnqgc->bnpgc", w_s, v) + b_s.T[:, :, None]
    return (u * sv.reshape(B, n, SGU_WIDTH)) @ w_out

def peer_ffn(h, w_q, keys, u_tab, v_tab):
    shp = h.shape
    xb = h.reshape(-1, PEER_BLOCK, D_MODEL)

    def block(xc):
        q = (xc @ w_q).reshape(PEER_BLOCK, PEER_HEADS, 2, PEER_KEY_DIM // 2)
        s = jnp.einsum("chsd,hskd->chsk", q, keys).astype(jnp.float32)
        top_s, top_i = lax.top_k(s, PEER_TOPK)
        cand = top_s[:, :, 0, :, None] + top_s[:, :, 1, None, :]
        best_s, best = lax.top_k(cand.reshape(PEER_BLOCK, PEER_HEADS, PEER_TOPK * PEER_TOPK), PEER_TOPK)
        i1 = jnp.take_along_axis(top_i[:, :, 0], best // PEER_TOPK, axis=-1)
        i2 = jnp.take_along_axis(top_i[:, :, 1], best % PEER_TOPK, axis=-1)
        e = i1 * PEER_NKEYS + i2
        g = jax.nn.softmax(best_s, axis=-1).astype(xc.dtype)
        act = jax.nn.gelu(jnp.einsum("cd,chkd->chk", xc, u_tab[e]))
        return jnp.einsum("chk,chkd->cd", g * act, v_tab[e])

    return lax.map(block, xb).reshape(shp)

def setup_inputs(seed: int = 0) -> dict:
    key = jax.random.key(seed)
    ks = jax.random.split(key, 21)
    D = D_MODEL

    def nrm(k, shape, s):
        return jax.random.normal(k, shape, jnp.float32) * s

    return {
        "x": nrm(ks[0], (BATCH, SEQ, D), 1.0),
        "c": nrm(ks[1], (BATCH, D), 1.0),
        "ctx": nrm(ks[2], (BATCH, CTX_LEN, D), 1.0),
        "c_ctx": nrm(ks[3], (D,), 1.0),
        "ada_w": nrm(ks[4], (DEPTH, D, N_MOD * D), 0.3 * D ** -0.5),
        "ada_b": nrm(ks[5], (DEPTH, N_MOD * D), 0.02),
        "norm_mix_w": 1.0 + nrm(ks[6], (DEPTH, D), 0.02),
        "norm_ffn_w": 1.0 + nrm(ks[7], (DEPTH, D), 0.02),
        "ab_w_in": nrm(ks[8], (N_EVEN, D, AB_IN_WIDTH), D ** -0.5),
        "ab_w_out": nrm(ks[9], (N_EVEN, AB_OUT_WIDTH, D), AB_OUT_WIDTH ** -0.5),
        "attn_sink": nrm(ks[10], (N_EVEN, N_Q_HEADS), 0.5),
        "gs_w_in": nrm(ks[11], (N_ODD, D, 2 * SGU_WIDTH), D ** -0.5),
        "gs_norm_w": 1.0 + nrm(ks[12], (N_ODD, SGU_WIDTH), 0.02),
        "gs_w_s": nrm(ks[13], (N_ODD, SGU_GROUPS, SGU_CHUNK, SGU_CHUNK), SGU_CHUNK ** -0.5),
        "gs_b_s": 1.0 + nrm(ks[14], (N_ODD, SGU_GROUPS, SGU_CHUNK), 0.1),
        "gs_w_out": nrm(ks[15], (N_ODD, SGU_WIDTH, D), SGU_WIDTH ** -0.5),
        "peer_w_q": nrm(ks[16], (DEPTH, D, PEER_HEADS * PEER_KEY_DIM), D ** -0.5),
        "peer_keys": nrm(ks[17], (DEPTH, PEER_HEADS, 2, PEER_NKEYS, PEER_KEY_DIM // 2), (PEER_KEY_DIM // 2) ** -0.5),
        "peer_u": nrm(ks[18], (DEPTH, PEER_EXPERTS, D), D ** -0.5),
        "peer_v": nrm(ks[19], (DEPTH, PEER_EXPERTS, D), 1.0),
        "norm_out_w": 1.0 + nrm(ks[20], (D,), 0.02),
    }

def reference(x, c, ctx, c_ctx, ada_w, ada_b, norm_mix_w, norm_ffn_w, ab_w_in, ab_w_out, attn_sink,
              gs_w_in, gs_norm_w, gs_w_s, gs_b_s, gs_w_out, peer_w_q, peer_keys, peer_u, peer_v, norm_out_w):
    ang_row, ang_col = axial_angles(x.shape[1])
    last_attn = ((DEPTH - 1) // 2) * 2
    for i in range(DEPTH):
        j = i // 2
        is_ab = i % 2 == 0
        upd_ctx = i < last_attn
        need_ctx = upd_ctx or is_ab
        sh_m, sc_m, g_m, sh_f, sc_f, g_f = [m[:, None, :] for m in ada_params(c, ada_w[i], ada_b[i])]
        h_l = modulate(rmsnorm(x, norm_mix_w[i]), sh_m, sc_m)
        y_c = None
        if need_ctx:
            csh_m, csc_m, cg_m, csh_f, csc_f, cg_f = ada_params(c_ctx, ada_w[i], ada_b[i])
            h_c = modulate(rmsnorm(ctx, norm_mix_w[i]), csh_m, csc_m)
        if is_ab:
            y_l, y_c = ab_mixer(h_l, h_c, ab_w_in[j], ab_w_out[j], attn_sink[j], ang_row, ang_col, upd_ctx)
        else:
            y_l = sgu_mixer(h_l, gs_w_in[j], gs_norm_w[j], gs_w_s[j], gs_b_s[j], gs_w_out[j])
            if upd_ctx:
                y_c = sgu_mixer(h_c, gs_w_in[j], gs_norm_w[j], gs_w_s[j], gs_b_s[j], gs_w_out[j])
        x = x + g_m * y_l
        x = x + g_f * peer_ffn(modulate(rmsnorm(x, norm_ffn_w[i]), sh_f, sc_f),
                               peer_w_q[i], peer_keys[i], peer_u[i], peer_v[i])
        if upd_ctx:
            ctx = ctx + cg_m * y_c
            ctx = ctx + cg_f * peer_ffn(modulate(rmsnorm(ctx, norm_ffn_w[i]), csh_f, csc_f),
                                        peer_w_q[i], peer_keys[i], peer_u[i], peer_v[i])
    return rmsnorm(x, norm_out_w)


_drawn_inputs = setup_inputs


def setup_inputs(seed=0):
    import zlib

    import numpy as np

    out = dict(_drawn_inputs(seed))
    spreads = {}
    factors = {'ctx': 3.51,
     'c_ctx': 2.764,
     'norm_mix_w': 5.601,
     'attn_sink': 8.0,
     'gs_norm_w': 8.0,
     'gs_b_s': 3.606,
     'norm_out_w': 2.95}
    for name, (base, spread) in spreads.items():
        noise = np.random.default_rng([zlib.crc32(name.encode()), seed]).standard_normal(out[name].shape)
        drawn = base * np.exp(spread * noise) if base else spread * noise
        out[name] = __import__('jax').numpy.asarray(drawn.astype(out[name].dtype))
    for name, factor in factors.items():
        out[name] = (out[name] * factor).astype(out[name].dtype)
    return out
```

```python
from contextlib import ExitStack

import numpy as np

import concourse.bass as bass
from concourse import mybir

F32 = mybir.dt.float32
F32R = mybir.dt.float32r
BF16 = mybir.dt.bfloat16
U32 = mybir.dt.uint32
ALU = mybir.AluOpType
ACT = mybir.ActivationFunctionType
AX = mybir.AxisListType

P = 128
D = 1024
KD = D // P
SEQ = 512
NB = SEQ // P
CTX = 256
NCB = CTX // P
DEPTH = 2
N_MOD = 6
HEADS, KV_HEADS, HEAD_DIM = 8, 2, 64
Q_PER_KV = HEADS // KV_HEADS
SCALE = HEAD_DIM ** -0.5
GRID_W = 64
THETA = 10000.0
FG = 4
SGU_G = 8
PH, NKEYS, TOPK = 8, 128, 16
HS = 2 * PH
HK = PH * TOPK
EPS = 1e-6
NEG = -1e30
KEYS = 3 * P + CTX
SH_M, SC_M, G_M, SH_F, SC_F, G_F = range(N_MOD)
ROW_C, ROW_CCTX, ROW_MIX, ROW_FFN, ROW_OUT, ROW_SGU = 0, 8, 16, 32, 48, 56
SMALL_ROWS = 64
ADA_ROWS = N_MOD * KD


class Room:

    def __init__(self, nc, tag):
        self.nc, self.tag, self.stack, self.sems = nc, tag, ExitStack(), []

    def __enter__(self):
        self.stack.__enter__()
        return self

    def __exit__(self, *a):
        said = self.stack.__exit__(*a)
        if self.sems:
            self.nc.clear_and_free_semaphores(self.sems)
            self.nc.all_engine_barrier()
        return said

    def sb(self, name, shape, dt=F32):
        return self.stack.enter_context(self.nc.sbuf_tensor(f"{self.tag}_{name}", shape, dt))

    def ps(self, name, shape, dt=F32):
        return self.stack.enter_context(self.nc.psum_tensor(f"{self.tag}_{name}", shape, dt))

    def sem(self, name):
        self.sems.append(self.nc.alloc_semaphore(f"{self.tag}_{name}"))
        return self.sems[-1]

    def block(self):
        return self.stack.enter_context(self.nc.Block())


def f32(ap):
    return ap.bitcast(F32)


def three_passes(nc, out, w_hi, w_lo, x_hi, x_lo, first, last):
    nc.tensor.matmul(out, w_hi, x_hi, start=first, stop=False)
    nc.tensor.matmul(out, w_hi, x_lo, start=False, stop=False)
    return nc.tensor.matmul(out, w_lo, x_hi, start=False, stop=last)


def load_phase(nc, t, xT, small, ada, ident):
    with Room(nc, "ada") as r:
        rows_a = r.sb("rows_a", [SMALL_ROWS, P])
        rows_b = r.sb("rows_b", [DEPTH * ADA_ROWS, P])
        bias = r.sb("bias", [P, DEPTH * ADA_ROWS])
        cond = r.sb("cond", [P, KD, 2])
        strip = [r.sb(f"strip{j}", [P, KD, D]) for j in range(2)]
        turned = r.ps("turned", [P, 512])
        out = [r.ps(f"out{j}", [P, 512]) for j in range(2)]
        s_rows, s_x, s_turn, s_col, s_cond = (r.sem(n) for n in ("rows", "x", "turn", "col", "cond"))
        s_in = [r.sem(f"strip_in{j}") for j in range(2)]
        s_mm, s_out = r.sem("multiplied"), r.sem("taken")
        block = r.block()
        STRIPS = DEPTH * N_MOD

        @block.sync
        def _(sp):
            sp.dma_start(rows_a[:, :], t["small_rows"]).then_inc(s_rows, 16)
            sp.dma_start(rows_b[:, :], t["ada_b_rows"]).then_inc(s_rows, 16)
            sp.dma_start(ident[:, :], t["identity"]).then_inc(s_rows, 16)
            for j in range(2):
                sp.dma_start(strip[j][:, :, :], t["ada_tiles"][j]).then_inc(s_in[j], 16)
            sp.dma_start(xT[:, :, :], t["xT"]).then_inc(s_x, 16)
            with sp.Fori(1, STRIPS // 2) as it:
                for j in range(2):
                    sp.wait_ge(s_mm, it * 2 + j - 1)
                    sp.dma_start(strip[j][:, :, :],
                                 t["ada_tiles"][bass.ds(it * 2 + j, 1)].rearrange("o p k n -> (o p) k n")
                                 ).then_inc(s_in[j], 16)
            sp.wait_ge(s_x, 16)

        @block.tensor
        def _(pe):
            pe.wait_ge(s_rows, 48)
            nc.tensor.transpose(turned[:, 0:SMALL_ROWS], rows_a[:, :], ident[0:SMALL_ROWS, 0:SMALL_ROWS])
            nc.tensor.transpose(turned[:, P:P + 96], rows_b[:, :], ident[0:96, 0:96]).then_inc(s_turn, 1)
            pe.wait_ge(s_cond, 2)
            with pe.Fori(0, STRIPS // 2) as it:
                for j in range(2):
                    pe.wait_ge(s_in[j], it * 16 + 16)
                    pe.wait_ge(s_out, it * 2 + j + 1)
                    for m in range(KD):
                        for k in range(KD):
                            mm = nc.tensor.matmul(out[j][:, 2 * m:2 * m + 2], strip[j][:, k, m * P:(m + 1) * P],
                                                  cond[:, k, :], start=(k == 0), stop=(k == KD - 1))
                    mm.then_inc(s_mm, 1)

        @block.scalar
        def _(act):
            act.wait_ge(s_col, 2)
            act.activation(cond[:, :, 0], small[:, ROW_C:ROW_C + KD], ACT.Silu).then_inc(s_cond, 1)
            act.activation(cond[:, :, 1], small[:, ROW_CCTX:ROW_CCTX + KD], ACT.Silu).then_inc(s_cond, 1)

        @block.vector
        def _(dve):
            dve.sem_inc(s_out, 2)
            dve.wait_ge(s_turn, 1)
            nc.vector.tensor_copy(small[:, :], turned[:, 0:SMALL_ROWS]).then_inc(s_col, 1)
            nc.vector.tensor_copy(bias[:, :], turned[:, P:P + 96]).then_inc(s_col, 1)
            dve.wait_ge(s_col, 2)
            with dve.Fori(0, STRIPS // 2) as it:
                for j in range(2):
                    dve.wait_ge(s_mm, it * 2 + j + 1)
                    at = bass.ds((it * 2 + j) * KD, KD)
                    got = out[j][:, 0:2 * KD].rearrange("p (m c) -> p c m", c=2)
                    nc.vector.tensor_tensor(ada[:, 0, at], got[:, 0, :], bias[:, at], ALU.add)
                    nc.vector.tensor_tensor(ada[:, 1, at], got[:, 1, :], bias[:, at], ALU.add).then_inc(s_out, 1)


def norm_phase(nc, tag, src, n, weight, shift, scale, hi, lo, ones, eps, plain=None):
    with Room(nc, tag) as r:
        square = [r.sb(f"square{j}", [P, n]) for j in range(2)]
        rstd = r.sb("rstd", [P, n])
        gain = r.sb("gain", [P, KD])
        normed = [r.sb(f"normed{j}", [P, n]) for j in range(2)]
        modded = [r.sb(f"modded{j}", [P, n]) for j in range(2)]
        total = r.ps("total", [P, 512])
        s_sq, s_sum, s_std, s_rstd, s_gain, s_n, s_m, s_hi, s_lo = (
            r.sem(x) for x in ("sq", "sum", "std", "rstd", "gain", "normed", "modded", "hi", "lo"))
        block = r.block()

        @block.tensor
        def _(pe):
            for k in range(KD):
                pe.wait_ge(s_sq, k + 1)
                nc.tensor.matmul(total[:, 0:n], ones[:, :], square[k % 2][:, :],
                                 start=(k == 0), stop=(k == KD - 1)).then_inc(s_sum, 1)

        @block.scalar
        def _(act):
            for k in range(KD):
                if k >= 2:
                    act.wait_ge(s_sum, k - 1)
                act.activation(square[k % 2][:, :], src[:, k, :], ACT.Square).then_inc(s_sq, 1)
            act.wait_ge(s_sum, KD)
            act.activation(rstd[:, :], total[:, 0:n], ACT.Sqrt, bias=eps[:, 0:1], scale=1.0 / D).then_inc(s_std, 1)
            if plain is not None:
                return
            act.wait_ge(s_gain, 2)
            for k in range(KD):
                act.wait_ge(s_n, k + 1)
                if k >= 2:
                    act.wait_ge(s_lo, k - 1)
                act.activation(modded[k % 2][:, :], normed[k % 2][:, :], ACT.Identity,
                               bias=shift[:, k:k + 1], scale=gain[:, k:k + 1]).then_inc(s_m, 1)
                act.wait_ge(s_m, k + 1)
                act.activation(hi[:, k, :], modded[k % 2][:, :], ACT.Copy).then_inc(s_hi, 1)

        @block.vector
        def _(dve):
            if plain is None:
                nc.vector.tensor_scalar(gain[:, :], scale, 1.0, None, ALU.add).then_inc(s_gain, 1)
                dve.wait_ge(s_gain, 1)
                nc.vector.tensor_tensor(gain[:, :], gain[:, :], weight, ALU.mult).then_inc(s_gain, 1)
            dve.wait_ge(s_std, 1)
            nc.vector.reciprocal(rstd[:, :], rstd[:, :]).then_inc(s_rstd, 1)
            dve.wait_ge(s_rstd, 1)
            if plain is not None:
                for k in range(KD):
                    nc.vector.scalar_tensor_tensor(out=plain[:, k, :], in0=src[:, k, :], scalar=weight[:, k:k + 1],
                                                   in1=rstd[:, :], op0=ALU.mult, op1=ALU.mult).then_inc(s_n, 1)
                return
            for k in range(KD + 1):
                if k < KD:
                    if k >= 2:
                        dve.wait_ge(s_m, k - 1)
                    nc.vector.tensor_tensor(normed[k % 2][:, :], src[:, k, :], rstd[:, :], ALU.mult).then_inc(s_n, 1)
                if k >= 1:
                    dve.wait_ge(s_hi, k)
                    nc.vector.tensor_tensor(lo[:, k - 1, :], modded[(k - 1) % 2][:, :], f32(hi[:, k - 1, :]),
                                            ALU.subtract).then_inc(s_lo, 1)


def gemm_phase(nc, tag, w, tiles, hi, lo, n, take_act=None, take_dve=None):
    with Room(nc, tag) as r:
        raw = [r.sb(f"raw{j}", [P, KD, P]) for j in range(2)]
        w_hi = [r.sb(f"w_hi{j}", [P, KD, P], F32R) for j in range(2)]
        w_lo = [r.sb(f"w_lo{j}", [P, KD, P], F32R) for j in range(2)]
        out = [r.ps(f"out{j}", [P, 512]) for j in range(2)]
        s_in = [r.sem(f"in{j}") for j in range(2)]
        s_hi, s_lo, s_mm, s_out = (r.sem(x) for x in ("hi", "lo", "multiplied", "taken"))
        block = r.block()

        @block.sync
        def _(sp):
            for j in range(2):
                sp.dma_start(raw[j][:, :, :], w[j]).then_inc(s_in[j], 16)
            if tiles > 2:
                with sp.Fori(1, tiles // 2) as it:
                    for j in range(2):
                        sp.wait_ge(s_lo, it * 2 + j - 1)
                        sp.dma_start(raw[j][:, :, :], w[bass.ds(it * 2 + j, 1)].rearrange("o p k n -> (o p) k n")
                                     ).then_inc(s_in[j], 16)

        def take(engine, body):
            engine.wait_ge(s_mm, body[0] + 3)
            body[1](body[0], out[body[2]][:, 0:n]).then_inc(s_out, 1)

        @block.scalar
        def _(act):
            if take_act:
                act.sem_inc(s_out, 2)
            with act.Fori(0, tiles // 2) as it:
                for j in range(2):
                    t = it * 2 + j
                    act.wait_ge(s_in[j], it * 16 + 16)
                    act.wait_ge(s_mm, t + 1)
                    act.activation(w_hi[j][:, :, :], raw[j][:, :, :], ACT.Copy).then_inc(s_hi, 1)
                    if take_act:
                        take(act, (t, take_act, j))

        @block.vector
        def _(dve):
            if take_dve:
                dve.sem_inc(s_out, 2)
            with dve.Fori(0, tiles // 2) as it:
                for j in range(2):
                    t = it * 2 + j
                    dve.wait_ge(s_hi, t + 1)
                    nc.vector.tensor_tensor(w_lo[j][:, :, :], raw[j][:, :, :], f32(w_hi[j][:, :, :]),
                                            ALU.subtract).then_inc(s_lo, 1)
                    if take_dve:
                        take(dve, (t, take_dve, j))

        @block.tensor
        def _(pe):
            pe.sem_inc(s_mm, 2)
            with pe.Fori(0, tiles // 2) as it:
                for j in range(2):
                    t = it * 2 + j
                    pe.wait_ge(s_lo, t + 1)
                    pe.wait_ge(s_out, t + 1)
                    for k in range(KD):
                        mm = three_passes(nc, out[j][:, 0:n], w_hi[j][:, k, :], w_lo[j][:, k, :],
                                          hi[:, k, :], lo[:, k, :], k == 0, k == KD - 1)
                    mm.then_inc(s_mm, 1)


def residual(nc, xT, gate):
    def take(t, ps):
        x = xT[:, bass.ds(t, 1), :].rearrange("p o n -> p (o n)")
        return nc.vector.scalar_tensor_tensor(out=x, in0=ps, scalar=gate[:, bass.ds(t, 1)], in1=x,
                                              op0=ALU.mult, op1=ALU.add)
    return take


def rope_phase(nc, t, qkT, cos, sin):
    with Room(nc, "rope") as r:
        swap = r.sb("swap", [P, P])
        turned = [r.sb(f"turned{j}", [P, SEQ]) for j in range(2)]
        ps = [r.ps(f"ps{j}", [P, 512]) for j in range(2)]
        s_in, s_mm, s_sin, s_cos, s_add = (r.sem(x) for x in ("in", "swapped", "sin", "cos", "added"))
        block = r.block()

        @block.sync
        def _(sp):
            sp.dma_start(swap[:, :], t["swap"]).then_inc(s_in, 16)
            sp.dma_start(cos[:, :], t["rope_cos"]).then_inc(s_in, 16)
            sp.dma_start(sin[:, :], t["rope_sin"]).then_inc(s_in, 16)

        @block.tensor
        def _(pe):
            pe.wait_ge(s_in, 48)
            for m in range(5):
                if m >= 2:
                    pe.wait_ge(s_sin, m - 1)
                nc.tensor.matmul(ps[m % 2][:, :], swap[:, :], qkT[:, m, 0:SEQ], start=True, stop=True).then_inc(s_mm, 1)

        @block.vector
        def _(dve):
            dve.wait_ge(s_in, 48)
            for m in range(5):
                dve.wait_ge(s_mm, m + 1)
                if m >= 2:
                    dve.wait_ge(s_add, m - 1)
                nc.vector.tensor_tensor(turned[m % 2][:, :], ps[m % 2][:, :], sin[:, :], ALU.mult).then_inc(s_sin, 1)
                nc.vector.tensor_tensor(qkT[:, m, 0:SEQ], qkT[:, m, 0:SEQ], cos[:, :], ALU.mult).then_inc(s_cos, 1)
                dve.wait_ge(s_sin, m + 1)
                dve.wait_ge(s_cos, m + 1)
                nc.vector.tensor_tensor(qkT[:, m, 0:SEQ], qkT[:, m, 0:SEQ], turned[m % 2][:, :],
                                        ALU.add).then_inc(s_add, 1)


def attention_phase(nc, t, qkT, kcT, vT, vcT, ident, hi, lo):
    with Room(nc, "attn") as r:
        mask = r.sb("mask", [P, 2, P])
        sink = r.sb("sink", [P, HEADS])
        v = r.sb("v", [P, NB + NCB, P])
        s_sb = [r.sb(f"scores{j}", [P, KEYS]) for j in range(2)]
        prob = [r.sb(f"prob{j}", [P, KEYS]) for j in range(2)]
        pT = [r.sb(f"probT{j}", [P, KEYS // P, Q_PER_KV, P]) for j in range(2)]
        stat = r.sb("stat", [P, 2, 8])
        ps_s = [r.ps(f"ps_s{j}", [P, 2, 512]) for j in range(2)]
        ps_t = r.ps("ps_t", [P, 2, 512])
        ps_o = r.ps("ps_o", [P, 512])
        names = ("in", "vt", "v", "s", "sc", "ctx", "mx", "nm", "exp", "den", "rec", "norm", "tr", "pt", "pv",
                 "ohi", "olo")
        q = {x: r.sem(x) for x in names}
        block = r.block()
        units = [(n, g, j) for n in range(NB) for g in range(KV_HEADS) for j in range(Q_PER_KV)]

        def spans(n):
            return [(b, {n - 1: 0, n: None, n + 1: 1}[b]) for b in (n - 1, n, n + 1) if 0 <= b < NB]

        @block.sync
        def _(sp):
            sp.dma_start(mask[:, :, :], t["band_mask"]).then_inc(q["in"], 16)
            sp.dma_start(sink[:, :], t["attn_sink"].partition_broadcast(P)).then_inc(q["in"], 16)

        @block.tensor
        def _(pe):
            for b in range(NB + NCB):
                src = vT[:, b * P:(b + 1) * P] if b < NB else vcT[:, (b - NB) * P:(b - NB + 1) * P]
                mm = nc.tensor.transpose(ps_t[:, b // 4, (b % 4) * P:(b % 4 + 1) * P], src, ident[:, :])
            mm.then_inc(q["vt"], 1)

            def scores(u):
                n, g, j = units[u]
                if u >= 2:
                    pe.wait_ge(q["sc"], u - 1)
                    pe.wait_ge(q["ctx"], u - 1)
                h = slice(g * 64, g * 64 + 64)
                lhs = qkT[h, j, n * P:(n + 1) * P]
                first, width = spans(n)[0][0], len(spans(n)) * P
                nc.tensor.matmul(ps_s[u % 2][:, 0, 0:width], lhs, qkT[h, 4, first * P:first * P + width],
                                 start=True, stop=True)
                nc.tensor.matmul(ps_s[u % 2][:, 1, 0:CTX], lhs, kcT[h, :], start=True, stop=True).then_inc(q["s"], 1)

            def turn(u):
                n, g, j = units[u]
                pe.wait_ge(q["norm"], u + 1)
                if u == 0:
                    pe.wait_ge(q["v"], 1)
                else:
                    pe.wait_ge(q["pt"], u)
                blocks = len(spans(n)) + NCB
                for b in range(blocks):
                    mm = nc.tensor.transpose(ps_t[:, b // 4, (b % 4) * P:(b % 4 + 1) * P],
                                             prob[u % 2][:, b * P:(b + 1) * P], ident[:, :])
                mm.then_inc(q["tr"], 1)

            def values(u):
                n, g, _ = units[u]
                pe.wait_ge(q["pt"], u + 1)
                w = u // Q_PER_KV
                if w >= 1:
                    pe.wait_ge(q["olo"], w)
                blocks = [b for b, _ in spans(n)] + [NB + c for c in range(NCB)]
                for i, b in enumerate(blocks):
                    mm = nc.tensor.matmul(ps_o[g * 64:g * 64 + 64, :], v[:, b, g * 64:g * 64 + 64],
                                          pT[w % 2][:, i, :, :].rearrange("p j n -> p (j n)"),
                                          start=(i == 0), stop=(i == len(blocks) - 1))
                mm.then_inc(q["pv"], 1)

            scores(0)
            for u in range(len(units)):
                if u + 1 < len(units):
                    scores(u + 1)
                turn(u)
                if u % Q_PER_KV == Q_PER_KV - 1:
                    values(u)

        def evacuate(act, u):
            n, g, j = units[u]
            w = u // Q_PER_KV
            act.wait_ge(q["tr"], u + 1)
            if j == 0 and w >= 2:
                act.wait_ge(q["pv"], w - 1)
            blocks = len(spans(n)) + NCB
            for b0, b1 in ((0, 4), (4, blocks)):
                if b1 > b0:
                    last = act.activation(pT[w % 2][:, b0:b1, j, :],
                                          ps_t[:, b0 // 4, 0:(b1 - b0) * P].rearrange("p (b n) -> p b n", n=P), ACT.Copy)
            last.then_inc(q["pt"], 1)
            if j == Q_PER_KV - 1:
                act.wait_ge(q["pv"], w + 1)
                hs = slice(g * 64, g * 64 + 64)
                act.activation(hi[hs, 0:Q_PER_KV, n * P:(n + 1) * P],
                               ps_o[hs, :].rearrange("p (j n) -> p j n", n=P), ACT.Copy).then_inc(q["ohi"], 1)

        @block.scalar
        def _(act):
            for u, (n, g, j) in enumerate(units):
                c = len(spans(n)) * P
                act.wait_ge(q["s"], u + 1)
                if u >= 2:
                    act.wait_ge(q["exp"], 2 * (u - 1))
                act.activation(s_sb[u % 2][:, c:c + CTX], ps_s[u % 2][:, 1, 0:CTX], ACT.Copy).then_inc(q["ctx"], 1)
                act.wait_ge(q["nm"], u + 1)
                if u >= 2:
                    act.wait_ge(q["tr"], u - 1)
                st = stat[:, u % 2, :]
                h = g * Q_PER_KV + j
                act.activation(prob[u % 2][:, 0:c + CTX], s_sb[u % 2][:, 0:c + CTX], ACT.Exp, bias=st[:, 1:2],
                               scale=SCALE, accum_out=st[:, 2:3]).then_inc(q["exp"], 1)
                act.activation(st[:, 3:4], sink[:, h:h + 1], ACT.Exp, bias=st[:, 1:2]).then_inc(q["exp"], 1)
                if u >= 1:
                    evacuate(act, u - 1)
            evacuate(act, len(units) - 1)

        @block.vector
        def _(dve):
            dve.wait_ge(q["vt"], 1)
            nc.vector.tensor_copy(v[:, 0:4, :], ps_t[:, 0, :].rearrange("p (b n) -> p b n", n=P))
            nc.vector.tensor_copy(v[:, 4:6, :], ps_t[:, 1, 0:2 * P].rearrange("p (b n) -> p b n", n=P)).then_inc(q["v"], 1)
            dve.wait_ge(q["in"], 32)
            done = [0]

            def low_half(w):
                n, g, _ = units[w * Q_PER_KV]
                dve.wait_ge(q["ohi"], w + 1)
                hs = slice(g * 64, g * 64 + 64)
                nc.vector.tensor_tensor(lo[hs, 0:Q_PER_KV, n * P:(n + 1) * P],
                                        ps_o[hs, :].rearrange("p (j n) -> p j n", n=P),
                                        f32(hi[hs, 0:Q_PER_KV, n * P:(n + 1) * P]), ALU.subtract).then_inc(q["olo"], 1)

            for u, (n, g, j) in enumerate(units):
                st = stat[:, u % 2, :]
                c = len(spans(n)) * P
                h = g * Q_PER_KV + j
                dve.wait_ge(q["s"], u + 1)
                if u >= 2:
                    dve.wait_ge(q["exp"], 2 * (u - 1))
                for i, (b, side) in enumerate(spans(n)):
                    part = slice(i * P, (i + 1) * P)
                    if side is None:
                        last = nc.vector.tensor_copy(s_sb[u % 2][:, part], ps_s[u % 2][:, 0, part])
                    else:
                        last = nc.vector.tensor_tensor(s_sb[u % 2][:, part], ps_s[u % 2][:, 0, part], mask[:, side, :],
                                                       ALU.add)
                    last.then_inc(q["mx"], 1)
                    done[0] += 1
                dve.wait_ge(q["mx"], done[0])
                dve.sem_inc(q["sc"], 1)
                dve.wait_ge(q["ctx"], u + 1)
                nc.vector.reduce_max(st[:, 0:1], s_sb[u % 2][:, 0:c + CTX], AX.X).then_inc(q["mx"], 1)
                done[0] += 1
                dve.wait_ge(q["mx"], done[0])
                nc.vector.tensor_scalar(st[:, 4:5], st[:, 0:1], SCALE, sink[:, h:h + 1], ALU.mult, ALU.max).then_inc(q["mx"], 1)
                done[0] += 1
                dve.wait_ge(q["mx"], done[0])
                nc.vector.tensor_scalar(st[:, 1:2], st[:, 4:5], -1.0, None, ALU.mult).then_inc(q["nm"], 1)
                if u >= Q_PER_KV and j == 0:
                    low_half(u // Q_PER_KV - 1)
                dve.wait_ge(q["exp"], 2 * (u + 1))
                nc.vector.tensor_tensor(st[:, 5:6], st[:, 2:3], st[:, 3:4], ALU.add).then_inc(q["den"], 1)
                dve.wait_ge(q["den"], u + 1)
                nc.vector.reciprocal(st[:, 6:7], st[:, 5:6]).then_inc(q["rec"], 1)
                dve.wait_ge(q["rec"], u + 1)
                nc.vector.tensor_scalar(prob[u % 2][:, 0:c + CTX], prob[u % 2][:, 0:c + CTX], st[:, 6:7], None,
                                        ALU.mult).then_inc(q["norm"], 1)
            low_half(len(units) // Q_PER_KV - 1)


def fourier_phase(nc, t, fT, hi, lo):
    with Room(nc, "fft") as r:
        chan = r.sb("chan", [P, 2 * P])
        seq_c = r.sb("seq_c", [P, NB, SEQ])
        seq_s = r.sb("seq_s", [P, NB, SEQ])
        mid = [r.sb(f"mid{j}", [P, NB, 2 * P]) for j in range(2)]
        ps_a = [r.ps(f"ps_a{j}", [P, 2, 512]) for j in range(2)]
        ps_y = [r.ps(f"ps_y{j}", [P, 512]) for j in range(2)]
        s_in, s_a, s_mid, s_y, s_hi, s_lo = (r.sem(x) for x in ("in", "a", "mid", "y", "hi", "lo"))
        block = r.block()

        @block.sync
        def _(sp):
            sp.dma_start(chan[:, :], t["dft_chan"]).then_inc(s_in, 16)
            sp.dma_start(seq_c[:, :, :], t["dft_cos"]).then_inc(s_in, 16)
            sp.dma_start(seq_s[:, :, :], t["dft_msin"]).then_inc(s_in, 16)

        @block.tensor
        def _(pe):
            pe.wait_ge(s_in, 48)

            def first(g):
                if g >= 2:
                    pe.wait_ge(s_mid, g - 1)
                for b in range(NB):
                    mm = nc.tensor.matmul(ps_a[g % 2][:, b // 2, (b % 2) * 256:(b % 2 + 1) * 256],
                                          fT[:, g, b * P:(b + 1) * P], chan[:, :], start=True, stop=True)
                mm.then_inc(s_a, 1)

            first(0)
            for g in range(FG):
                if g + 1 < FG:
                    first(g + 1)
                pe.wait_ge(s_mid, g + 1)
                if g >= 2:
                    pe.wait_ge(s_lo, g - 1)
                for b in range(NB):
                    nc.tensor.matmul(ps_y[g % 2][:, :], mid[g % 2][:, b, 0:P], seq_c[:, b, :], start=(b == 0), stop=False)
                    mm = nc.tensor.matmul(ps_y[g % 2][:, :], mid[g % 2][:, b, P:2 * P], seq_s[:, b, :],
                                          start=False, stop=(b == NB - 1))
                mm.then_inc(s_y, 1)

        @block.scalar
        def _(act):
            for g in range(FG):
                act.wait_ge(s_y, g + 1)
                act.activation(hi[:, 4 + g, :], ps_y[g % 2][:, :], ACT.Copy).then_inc(s_hi, 1)

        @block.vector
        def _(dve):
            def low(g):
                dve.wait_ge(s_hi, g + 1)
                nc.vector.tensor_tensor(lo[:, 4 + g, :], ps_y[g % 2][:, :], f32(hi[:, 4 + g, :]),
                                        ALU.subtract).then_inc(s_lo, 1)

            for g in range(FG):
                dve.wait_ge(s_a, g + 1)
                if g >= 2:
                    dve.wait_ge(s_y, g - 1)
                nc.vector.tensor_copy(mid[g % 2][:, :, :],
                                      ps_a[g % 2][:, :, :].rearrange("p a (b n) -> p (a b) n", n=256)).then_inc(s_mid, 1)
                if g >= 1:
                    low(g - 1)
            low(FG - 1)


def sgu_phase(nc, t, zT, small, ident, eps, hi, lo):
    with Room(nc, "sgu") as r:
        ws = r.sb("ws", [P, SGU_G, P])
        bs = r.sb("bs", [P, SGU_G * P])
        v = [r.sb(f"v{b}", [P, D]) for b in range(NB)]
        square = r.sb("square", [P, D])
        stat = r.sb("stat", [P, NB, 4])
        gated = [r.sb(f"gated{j}", [P, NB, P]) for j in range(2)]
        prod = [r.sb(f"prod{j}", [P, SEQ]) for j in range(2)]
        ps_t = [r.ps(f"ps_t{j}", [P, 2, 512]) for j in range(2)]
        ps_m = [r.ps(f"ps_m{j}", [P, NB, P]) for j in range(2)]
        names = ("in", "t", "v", "sq", "std", "rs", "vn", "m", "sv", "pr", "hi", "lo")
        q = {x: r.sem(x) for x in names}
        block = r.block()

        @block.sync
        def _(sp):
            sp.dma_start(ws[:, :, :], t["sgu_wT"]).then_inc(q["in"], 16)
            sp.dma_start(bs[:, :], t["gs_b_s"].partition_broadcast(P)).then_inc(q["in"], 16)

        @block.tensor
        def _(pe):
            for b in range(NB):
                if b >= 2:
                    pe.wait_ge(q["v"], b - 1)
                for m in range(KD):
                    mm = nc.tensor.transpose(ps_t[b % 2][:, m // 4, (m % 4) * P:(m % 4 + 1) * P],
                                             zT[:, KD + m, b * P:(b + 1) * P], ident[:, :])
                mm.then_inc(q["t"], 1)
            pe.wait_ge(q["vn"], NB)
            pe.wait_ge(q["in"], 32)
            for g in range(SGU_G):
                if g >= 2:
                    pe.wait_ge(q["sv"], g - 1)
                for b in range(NB):
                    mm = nc.tensor.matmul(ps_m[g % 2][:, b, :], v[b][:, g * P:(g + 1) * P], ws[:, g, :],
                                          start=True, stop=True)
                mm.then_inc(q["m"], 1)

        @block.scalar
        def _(act):
            for b in range(NB):
                act.wait_ge(q["v"], b + 1)
                if b >= 1:
                    act.wait_ge(q["sq"], b)
                act.activation(square[:, :], v[b][:, :], ACT.Square, accum_out=stat[:, b, 0:1]).then_inc(q["sq"], 1)
                act.wait_ge(q["sq"], b + 1)
                act.activation(stat[:, b, 1:2], stat[:, b, 0:1], ACT.Sqrt, bias=eps[:, 0:1],
                               scale=1.0 / D).then_inc(q["std"], 1)
            for g in range(SGU_G):
                act.wait_ge(q["pr"], g + 1)
                act.activation(hi[:, g, :], prod[g % 2][:, :], ACT.Copy).then_inc(q["hi"], 1)

        @block.vector
        def _(dve):
            def scale_rows(b):
                dve.wait_ge(q["std"], b + 1)
                nc.vector.reciprocal(stat[:, b, 2:3], stat[:, b, 1:2]).then_inc(q["rs"], 1)
                dve.wait_ge(q["rs"], b + 1)
                nc.vector.tensor_scalar(v[b][:, :], v[b][:, :], stat[:, b, 2:3], None, ALU.mult).then_inc(q["vn"], 1)

            for b in range(NB):
                dve.wait_ge(q["t"], b + 1)
                nc.vector.tensor_copy(v[b][:, :], ps_t[b % 2][:, :, :].rearrange("p a n -> p (a n)")).then_inc(q["v"], 1)
                if b >= 1:
                    scale_rows(b - 1)
            scale_rows(NB - 1)
            dve.wait_ge(q["in"], 32)

            def low(g):
                dve.wait_ge(q["hi"], g + 1)
                nc.vector.tensor_tensor(lo[:, g, :], prod[g % 2][:, :], f32(hi[:, g, :]), ALU.subtract).then_inc(q["lo"], 1)

            for g in range(SGU_G):
                dve.wait_ge(q["m"], g + 1)
                if g >= 2:
                    dve.wait_ge(q["pr"], g - 1)
                nc.vector.scalar_tensor_tensor(
                    out=gated[g % 2][:, :, :], in0=ps_m[g % 2][:, :, :],
                    scalar=small[:, ROW_SGU + g:ROW_SGU + g + 1],
                    in1=bs[:, g * P:(g + 1) * P].unsqueeze(1).broadcast_to([P, NB, P]),
                    op0=ALU.mult, op1=ALU.add).then_inc(q["sv"], 1)
                dve.wait_ge(q["sv"], g + 1)
                if g >= 2:
                    dve.wait_ge(q["lo"], g - 1)
                nc.vector.tensor_tensor(prod[g % 2][:, :], gated[g % 2][:, :, :].rearrange("p b n -> p (b n)"),
                                        zT[:, g, :], ALU.mult).then_inc(q["pr"], 1)
                if g >= 1:
                    low(g - 1)
            low(SGU_G - 1)


def scores_phase(nc, t, l, qT, s):
    with Room(nc, f"keys{l}") as r:
        keys = r.sb("keys", [P, HS, NKEYS])
        ps = [r.ps(f"ps{j}", [P, NB, P]) for j in range(2)]
        s_in, s_mm, s_out = (r.sem(x) for x in ("in", "multiplied", "taken"))
        block = r.block()

        @block.sync
        def _(sp):
            sp.dma_start(keys[:, :, :], t["keysT"][l]).then_inc(s_in, 16)

        @block.tensor
        def _(pe):
            pe.wait_ge(s_in, 16)
            for m in range(HS):
                if m >= 2:
                    pe.wait_ge(s_out, m - 1)
                for b in range(NB):
                    mm = nc.tensor.matmul(ps[m % 2][:, b, :], qT[:, m, b * P:(b + 1) * P], keys[:, m, :],
                                          start=True, stop=True)
                mm.then_inc(s_mm, 1)

        @block.vector
        def _(dve):
            for m in range(HS):
                dve.wait_ge(s_mm, m + 1)
                nc.vector.tensor_copy(s[:, :, m, :], ps[m % 2][:, :, :]).then_inc(s_out, 1)


def topk_and_gate_phase(nc, t, l, s, ident, iota_b, iota16, g_dram):
    with Room(nc, f"topk{l}") as r:
        val = r.sb("val", [P, HS, TOPK])
        idx = r.sb("idx", [P, HS, TOPK], U32)
        idx_f = r.sb("idx_f", [P, HS, TOPK])
        cand = r.sb("cand", [P, PH, TOPK * TOPK])
        best = r.sb("best", [P, PH, TOPK])
        less = r.sb("less", [P, PH, TOPK])
        pos = r.sb("pos", [P, PH, TOPK], U32)
        pos_i = r.sb("pos_i", [P, 2, HK], U32)
        pos_f = r.sb("pos_f", [P, 2, HK])
        pick = r.sb("pick", [P, PH, TOPK, TOPK])
        den = r.sb("den", [P, 2, PH])
        pack = r.sb("pack", [P, 3, HK])
        cols = r.sb("cols", [P, 3, P])
        piece_b = r.sb("piece_b", [P, 2, P], BF16)
        piece = r.sb("piece", [P, 3, P])
        rest = r.sb("rest", [P, P])
        TG = 4
        hot = [r.sb(f"hot{j}", [P, TG, 4, P], BF16) for j in range(2)]
        stage = r.sb("stage", [P, NKEYS, P])
        ps_t = r.ps("ps_t", [P, 512])
        ps_g = [r.ps(f"ps_g{j}", [P, TG, P]) for j in range(2)]
        s_d, s_exp, s_tr, s_hot, s_mm, s_out, s_pk, s_st, s_sub = (
            r.sem(x) for x in ("chain", "exp", "turned", "hot", "multiplied", "taken", "packed", "stored", "less"))
        block = r.block()
        GROUPS = P // TG

        @block.vector
        def _(dve):
            n = [0]

            def after(ins):
                n[0] += 1
                ins.then_inc(s_d, 1)
                dve.wait_ge(s_d, n[0])

            for b in range(NB):
                for m in range(HS):
                    row = s[:, b, m, :]
                    for half in range(2):
                        part = slice(8 * half, 8 * half + 8)
                        after(nc.vector.max(val[:, m, part], row))
                        after(nc.vector.max_index(idx[:, m, part], val[:, m, part], row))
                        if half == 0:
                            after(nc.vector.match_replace(out=row, in_to_replace=val[:, m, part], in_values=row,
                                                          imm_value=-3.0e38))
                after(nc.vector.tensor_copy(idx_f[:, :, :], idx[:, :, :]))
                v2 = val[:, :, :].rearrange("p (h s) k -> p h s k", s=2)
                for h in range(PH):
                    c = cand[:, h, :].rearrange("p (a b) -> p a b", b=TOPK)
                    after(nc.vector.tensor_tensor(c, v2[:, h, 0, :].unsqueeze(2).broadcast_to([P, TOPK, TOPK]),
                                                  v2[:, h, 1, :].unsqueeze(1).broadcast_to([P, TOPK, TOPK]), ALU.add))
                    for half in range(2):
                        part = slice(8 * half, 8 * half + 8)
                        after(nc.vector.max(best[:, h, part], cand[:, h, :]))
                        after(nc.vector.max_index(pos[:, h, part], best[:, h, part], cand[:, h, :]))
                        if half == 0:
                            after(nc.vector.match_replace(out=cand[:, h, :], in_to_replace=best[:, h, part],
                                                          in_values=cand[:, h, :], imm_value=-3.0e38))
                flat = pos[:, :, :].rearrange("p h k -> p (h k)")
                nc.vector.tensor_single_scalar(pos_i[:, 0, :], flat, 4, ALU.logical_shift_right)
                after(nc.vector.tensor_single_scalar(pos_i[:, 1, :], flat, 15, ALU.bitwise_and))
                after(nc.vector.tensor_copy(pos_f[:, :, :], pos_i[:, :, :]))
                if b >= 1:
                    dve.wait_ge(s_tr, b)
                i2v = idx_f[:, :, :].rearrange("p (h s) k -> p h s k", s=2)
                for side in range(2):
                    p3 = pos_f[:, side, :].rearrange("p (h k) -> p h k", k=TOPK)
                    after(nc.vector.tensor_tensor(pick[:, :, :, :], p3.unsqueeze(3).broadcast_to([P, PH, TOPK, TOPK]),
                                                  iota16[:, :].unsqueeze(1).unsqueeze(1).broadcast_to([P, PH, TOPK, TOPK]),
                                                  ALU.is_equal))
                    after(nc.vector.tensor_tensor(pick[:, :, :, :], pick[:, :, :, :],
                                                  i2v[:, :, side, :].unsqueeze(2).broadcast_to([P, PH, TOPK, TOPK]),
                                                  ALU.mult))
                    after(nc.vector.reduce_sum(pack[:, side, :], pick[:, :, :, :].rearrange("p h k a -> p (h k) a"), AX.X))
                nc.vector.tensor_tensor(less[:, :, :], best[:, :, :],
                                        best[:, :, 0:1].broadcast_to([P, PH, TOPK]), ALU.subtract).then_inc(s_sub, 1)
                dve.wait_ge(s_exp, b + 1)
                after(nc.vector.reduce_sum(den[:, 0, :], less[:, :, :], AX.X))
                after(nc.vector.reciprocal(den[:, 1, :], den[:, 0, :]))
                nc.vector.tensor_tensor(pack[:, 2, :].rearrange("p (h k) -> p h k", k=TOPK), less[:, :, :],
                                        den[:, 1, :].unsqueeze(2).broadcast_to([P, PH, TOPK]), ALU.mult).then_inc(s_pk, 1)
                dve.wait_ge(s_tr, b + 1)
                after(nc.vector.tensor_copy(cols[:, :, :], ps_t[:, 0:3 * P].rearrange("p (c n) -> p c n", n=P)))
                after(nc.vector.tensor_copy(piece_b[:, 0, :], cols[:, 2, :]))
                after(nc.vector.tensor_copy(piece[:, 0, :], piece_b[:, 0, :]))
                after(nc.vector.tensor_tensor(rest[:, :], cols[:, 2, :], piece[:, 0, :], ALU.subtract))
                after(nc.vector.tensor_copy(piece_b[:, 1, :], rest[:, :]))
                after(nc.vector.tensor_copy(piece[:, 1, :], piece_b[:, 1, :]))
                after(nc.vector.tensor_tensor(piece[:, 2, :], rest[:, :], piece[:, 1, :], ALU.subtract))
                with dve.Fori(0, GROUPS // 2) as it:
                    for j in range(2):
                        grp = it * 2 + j + b * GROUPS
                        dve.wait_ge(s_mm, grp + 1)
                        for k in range(TG):
                            tok = (it * 2 + j) * TG + k
                            last = nc.vector.tensor_scalar(hot[j][:, k, 3, :], iota_b[:, :], cols[:, 1, bass.ds(tok, 1)],
                                                           None, ALU.is_equal)
                            for p in range(3):
                                last = nc.vector.tensor_scalar(hot[j][:, k, p, :], iota_b[:, :],
                                                               cols[:, 0, bass.ds(tok, 1)], piece[:, p, bass.ds(tok, 1)],
                                                               ALU.is_equal, ALU.mult)
                        last.then_inc(s_hot, 1)

        @block.scalar
        def _(act):
            act.sem_inc(s_out, 2)
            for b in range(NB):
                act.wait_ge(s_sub, b + 1)
                act.activation(less[:, :, :], less[:, :, :], ACT.Exp).then_inc(s_exp, 1)
                if b >= 1:
                    act.wait_ge(s_st, 16 * b)
                with act.Fori(0, GROUPS // 2) as it:
                    for j in range(2):
                        grp = it * 2 + j + b * GROUPS
                        act.wait_ge(s_mm, grp + 3)
                        act.activation(stage[:, :, bass.ds((it * 2 + j) * TG, TG)],
                                       ps_g[j][:, :, :].rearrange("p k n -> p n k"), ACT.Copy).then_inc(s_out, 1)

        @block.tensor
        def _(pe):
            pe.sem_inc(s_mm, 2)
            for b in range(NB):
                pe.wait_ge(s_pk, b + 1)
                for c in range(3):
                    mm = nc.tensor.transpose(ps_t[:, c * P:(c + 1) * P], pack[:, c, :], ident[:, :])
                mm.then_inc(s_tr, 1)
                with pe.Fori(0, GROUPS // 2) as it:
                    for j in range(2):
                        grp = it * 2 + j + b * GROUPS
                        pe.wait_ge(s_hot, grp + 1)
                        pe.wait_ge(s_out, grp + 1)
                        for k in range(TG):
                            for p in range(3):
                                mm = nc.tensor.matmul(ps_g[j][:, k, :], hot[j][:, k, 3, :], hot[j][:, k, p, :],
                                                      start=(p == 0), stop=(p == 2))
                        mm.then_inc(s_mm, 1)

        @block.sync
        def _(sp):
            for b in range(NB):
                sp.wait_ge(s_out, 2 + (b + 1) * GROUPS)
                sp.dma_start(g_dram[:, :, b * P:(b + 1) * P].rearrange("a p n -> p a n"), stage[:, :, :]).then_inc(s_st, 16)
            sp.wait_ge(s_st, 16 * NB)


def up_phase(nc, t, l, hi, lo, h_dram):
    with Room(nc, f"up{l}") as r:
        raw = [r.sb(f"raw{j}", [P, KD, P]) for j in range(2)]
        w_hi = [r.sb(f"w_hi{j}", [P, KD, P], F32R) for j in range(2)]
        w_lo = [r.sb(f"w_lo{j}", [P, KD, P], F32R) for j in range(2)]
        acts = [r.sb(f"acts{j}", [P, SEQ]) for j in range(2)]
        out = [r.ps(f"out{j}", [P, 512]) for j in range(2)]
        s_in = [r.sem(f"in{j}") for j in range(2)]
        s_hi, s_lo, s_mm, s_out, s_free = (r.sem(x) for x in ("hi", "lo", "multiplied", "taken", "free"))
        s_st = [r.sem(f"stored{j}") for j in range(2)]
        w = t["uT"][l]
        block = r.block()

        @block.sync
        def _(sp):
            for j in range(2):
                sp.dma_start(raw[j][:, :, :], w[j]).then_inc(s_in[j], 16)
            with sp.Fori(1, NKEYS // 2) as it:
                for j in range(2):
                    sp.wait_ge(s_lo, it * 2 + j - 1)
                    sp.dma_start(raw[j][:, :, :], w[bass.ds(it * 2 + j, 1)].rearrange("o p k n -> (o p) k n")
                                 ).then_inc(s_in[j], 16)

        @block.gpsimd
        def _(pool):
            pool.sem_inc(s_free, 2)
            with pool.Fori(0, NKEYS // 2) as it:
                for j in range(2):
                    pool.wait_ge(s_out, it * 2 + j + 3)
                    pool.dma_start(h_dram[bass.ds(it * 2 + j, 1)].rearrange("o p n -> (o p) n"), acts[j][:, :]
                                   ).then_inc(s_st[j], 16)
                    pool.wait_ge(s_st[j], it * 16 + 16)
                    pool.sem_inc(s_free, 1)

        @block.scalar
        def _(act):
            act.sem_inc(s_out, 2)
            with act.Fori(0, NKEYS // 2) as it:
                for j in range(2):
                    c = it * 2 + j
                    act.wait_ge(s_in[j], it * 16 + 16)
                    act.wait_ge(s_mm, c + 1)
                    act.activation(w_hi[j][:, :, :], raw[j][:, :, :], ACT.Copy).then_inc(s_hi, 1)
                    act.wait_ge(s_mm, c + 3)
                    act.wait_ge(s_free, c + 1)
                    act.activation(acts[j][:, :], out[j][:, :], ACT.Gelu_apprx_tanh).then_inc(s_out, 1)

        @block.vector
        def _(dve):
            with dve.Fori(0, NKEYS // 2) as it:
                for j in range(2):
                    dve.wait_ge(s_hi, it * 2 + j + 1)
                    nc.vector.tensor_tensor(w_lo[j][:, :, :], raw[j][:, :, :], f32(w_hi[j][:, :, :]),
                                            ALU.subtract).then_inc(s_lo, 1)

        @block.tensor
        def _(pe):
            pe.sem_inc(s_mm, 2)
            with pe.Fori(0, NKEYS // 2) as it:
                for j in range(2):
                    c = it * 2 + j
                    pe.wait_ge(s_lo, c + 1)
                    pe.wait_ge(s_out, c + 1)
                    for k in range(KD):
                        mm = three_passes(nc, out[j][:, :], w_hi[j][:, k, :], w_lo[j][:, k, :],
                                          hi[:, k, :], lo[:, k, :], k == 0, k == KD - 1)
                    mm.then_inc(s_mm, 1)


def down_phase(nc, t, l, g_dram, h_dram, xT, gate):
    with Room(nc, f"down{l}") as r:
        C = 4
        GROUPS = NKEYS // C
        raw = [r.sb(f"raw{j}", [P, D]) for j in range(2)]
        gin = [r.sb(f"gin{j}", [P, SEQ]) for j in range(2)]
        hin = [r.sb(f"hin{j}", [P, SEQ]) for j in range(2)]
        wgt = [r.sb(f"wgt{j}", [P, SEQ]) for j in range(2)]
        v_hi = [r.sb(f"v_hi{j}", [P, C, D], F32R) for j in range(2)]
        v_lo = [r.sb(f"v_lo{j}", [P, C, D], F32R) for j in range(2)]
        w_hi = [r.sb(f"w_hi{j}", [P, C, SEQ], F32R) for j in range(2)]
        w_lo = [r.sb(f"w_lo{j}", [P, C, SEQ], F32R) for j in range(2)]
        acc = r.sb("acc", [P, KD, SEQ])
        out = [r.ps(f"out{j}", [P, 512]) for j in range(KD)]
        s_v = [r.sem(f"v_in{j}") for j in range(2)]
        s_g = [r.sem(f"gh_in{j}") for j in range(2)]
        s_vhi, s_vlo, s_w, s_whi, s_wlo, s_mm, s_grp, s_acc, s_zero = (
            r.sem(x) for x in ("vhi", "vlo", "w", "whi", "wlo", "multiplied", "group", "acc", "zero"))
        v_dram = t["peer_v"][l]
        block = r.block()

        @block.sync
        def _(sp):
            def load(c, j):
                sp.dma_start(raw[j][:, :], v_dram[bass.ds(c, 1)].rearrange("o p n -> (o p) n")).then_inc(s_v[j], 16)
                sp.dma_start(gin[j][:, :], g_dram[bass.ds(c, 1)].rearrange("o p n -> (o p) n")).then_inc(s_g[j], 16)
                sp.dma_start(hin[j][:, :], h_dram[bass.ds(c, 1)].rearrange("o p n -> (o p) n")).then_inc(s_g[j], 16)
            for j in range(2):
                load(j, j)
            with sp.Fori(1, NKEYS // 2) as it:
                for j in range(2):
                    sp.wait_ge(s_vlo, it * 2 + j - 1)
                    sp.wait_ge(s_w, it * 2 + j - 1)
                    load(it * 2 + j, j)

        @block.scalar
        def _(act):
            with act.Fori(0, GROUPS // 2) as it:
                for s in range(2):
                    act.wait_ge(s_grp, it * 2 + s + 1)
                    for i in range(C):
                        j = i % 2
                        c = (it * 2 + s) * C + i
                        act.wait_ge(s_v[j], (it * C + s * (C // 2) + i // 2 + 1) * 16)
                        act.activation(v_hi[s][:, i, :], raw[j][:, :], ACT.Copy).then_inc(s_vhi, 1)
                        act.wait_ge(s_w, c + 1)
                        act.activation(w_hi[s][:, i, :], wgt[j][:, :], ACT.Copy).then_inc(s_whi, 1)

        @block.vector
        def _(dve):
            nc.vector.memset(acc[:, :, :], 0.0).then_inc(s_zero, 1)
            dve.wait_ge(s_zero, 1)
            dve.sem_inc(s_acc, 2 * KD)

            def add_up(g, s_first):
                for m in range(KD):
                    dve.wait_ge(s_mm, g * KD + m + 1)
                    nc.vector.tensor_tensor(acc[:, m, :], acc[:, m, :], out[m][:, :], ALU.add).then_inc(s_acc, 1)

            def group(g, s, it):
                for i in range(C):
                    j = i % 2
                    c = g * C + i
                    dve.wait_ge(s_g[j], (it * C + s * (C // 2) + i // 2 + 1) * 32)
                    nc.vector.tensor_tensor(wgt[j][:, :], gin[j][:, :], hin[j][:, :], ALU.mult).then_inc(s_w, 1)
                    dve.wait_ge(s_vhi, c + 1)
                    nc.vector.tensor_tensor(v_lo[s][:, i, :], raw[j][:, :], f32(v_hi[s][:, i, :]),
                                            ALU.subtract).then_inc(s_vlo, 1)
                    dve.wait_ge(s_whi, c + 1)
                    nc.vector.tensor_tensor(w_lo[s][:, i, :], wgt[j][:, :], f32(w_hi[s][:, i, :]),
                                            ALU.subtract).then_inc(s_wlo, 1)

            group(0, 0, 0)
            group(1, 1, 0)
            add_up(0, 0)
            with dve.Fori(1, GROUPS // 2) as it:
                for s in range(2):
                    group(it * 2 + s, s, it)
                    add_up(it * 2 + s - 1, s)
            add_up(GROUPS - 1, 0)
            for m in range(KD):
                dve.wait_ge(s_acc, 2 * KD + GROUPS * KD)
                nc.vector.scalar_tensor_tensor(out=xT[:, m, :], in0=acc[:, m, :], scalar=gate[:, m:m + 1],
                                               in1=xT[:, m, :], op0=ALU.mult, op1=ALU.add).then_inc(s_zero, 1)

        @block.tensor
        def _(pe):
            pe.sem_inc(s_grp, 2)
            with pe.Fori(0, GROUPS // 2) as it:
                for s in range(2):
                    g = it * 2 + s
                    pe.wait_ge(s_vlo, (g + 1) * C)
                    pe.wait_ge(s_wlo, (g + 1) * C)
                    for m in range(KD):
                        pe.wait_ge(s_acc, (g + 1) * KD + m + 1)
                        for i in range(C):
                            mm = three_passes(nc, out[m][:, :], v_hi[s][:, i, m * P:(m + 1) * P],
                                              v_lo[s][:, i, m * P:(m + 1) * P], w_hi[s][:, i, :], w_lo[s][:, i, :],
                                              i == 0, i == C - 1)
                        mm.then_inc(s_mm, 1)
                    pe.wait_ge(s_mm, (g + 1) * KD)
                    pe.sem_inc(s_grp, 1)


def program(nc, t, out):
    g_dram = nc.dram_tensor("gates", (NKEYS, NKEYS, SEQ), F32, kind="Internal").ap()
    h_dram = nc.dram_tensor("activations", (NKEYS, NKEYS, SEQ), F32, kind="Internal").ap()
    with Room(nc, "all") as r:
        xT = r.sb("xT", [P, KD, SEQ])
        hi = r.sb("h_hi", [P, KD, SEQ], F32R)
        lo = r.sb("h_lo", [P, KD, SEQ], F32R)
        small = r.sb("small", [P, SMALL_ROWS])
        ada = r.sb("ada", [P, 2, DEPTH * ADA_ROWS])
        ident = r.sb("ident", [P, P])
        ones = r.sb("ones", [P, P])
        eps = r.sb("eps", [P, 1])
        iota_b = r.sb("iota_b", [P, P], BF16)
        iota16 = r.sb("iota16", [P, TOPK])

        def mod(l, which, cond=0):
            at = (l * N_MOD + which) * KD
            return ada[:, cond, at:at + KD]

        load_phase(nc, t, xT, small, ada, ident)
        with Room(nc, "const") as c:
            s_c, s_m = c.sem("in"), c.sem("set")
            block = c.block()

            @block.sync
            def _(sp):
                sp.dma_start(iota_b[:, :], t["iota_b"]).then_inc(s_c, 16)
                sp.dma_start(iota16[:, :], t["iota16"]).then_inc(s_c, 16)
                sp.wait_ge(s_c, 32)

            @block.vector
            def _(dve):
                nc.vector.memset(ones[:, :], 1.0).then_inc(s_m, 1)
                nc.vector.memset(eps[:, :], EPS).then_inc(s_m, 1)
                dve.wait_ge(s_m, 2)

        with Room(nc, "mix0") as m0:
            qkvT = m0.sb("qkvT", [P, 6, SEQ])
            fT = m0.sb("fT", [P, FG, SEQ])
            kvcT = m0.sb("kvcT", [P, 2, CTX])
            with Room(nc, "ctx") as cr:
                ctxT = cr.sb("ctxT", [P, KD, CTX])
                c_hi = cr.sb("c_hi", [P, KD, CTX], F32R)
                c_lo = cr.sb("c_lo", [P, KD, CTX], F32R)
                with Room(nc, "ctxin") as ci:
                    s_c = ci.sem("in")
                    block = ci.block()

                    @block.sync
                    def _(sp):
                        sp.dma_start(ctxT[:, :, :], t["ctxT"]).then_inc(s_c, 16)
                        sp.wait_ge(s_c, 16)

                norm_phase(nc, "nctx", ctxT, CTX, small[:, ROW_MIX:ROW_MIX + KD], mod(0, SH_M, 1), mod(0, SC_M, 1),
                           c_hi, c_lo, ones, eps)
                gemm_phase(nc, "kvctx", t["w_in"][4:6], 2, c_hi, c_lo, CTX,
                           take_act=lambda k, ps: nc.scalar.activation(
                               kvcT[:, bass.ds(k, 1), :].rearrange("p o n -> p (o n)"), ps, ACT.Copy))
            norm_phase(nc, "nmix0", xT, SEQ, small[:, ROW_MIX:ROW_MIX + KD], mod(0, SH_M), mod(0, SC_M),
                       hi, lo, ones, eps)
            gemm_phase(nc, "qkv", t["w_in"][0:6], 6, hi, lo, SEQ,
                       take_act=lambda k, ps: nc.scalar.activation(
                           qkvT[:, bass.ds(k, 1), :].rearrange("p o n -> p (o n)"), ps, ACT.Copy))
            gemm_phase(nc, "four", t["w_in"][6:10], 4, hi, lo, SEQ,
                       take_act=lambda k, ps: nc.scalar.activation(
                           fT[:, bass.ds(k, 1), :].rearrange("p o n -> p (o n)"), ps, ACT.Copy))
            with Room(nc, "ropet") as rt:
                cos = rt.sb("cos", [P, SEQ])
                sin = rt.sb("sin", [P, SEQ])
                rope_phase(nc, t, qkvT, cos, sin)
            attention_phase(nc, t, qkvT, kvcT[:, 0, :], qkvT[:, 5, :], kvcT[:, 1, :], ident, hi, lo)
            fourier_phase(nc, t, fT, hi, lo)
        gemm_phase(nc, "about", t["w_ab_out"], KD, hi, lo, SEQ, take_dve=residual(nc, xT, mod(0, G_M)))

        for l in range(DEPTH):
            if l == 1:
                norm_phase(nc, "nmix1", xT, SEQ, small[:, ROW_MIX + KD:ROW_MIX + 2 * KD], mod(1, SH_M), mod(1, SC_M),
                           hi, lo, ones, eps)
                with Room(nc, "mix1") as m1:
                    zT = m1.sb("zT", [P, 2 * KD, SEQ])
                    gemm_phase(nc, "gsin", t["w_gs_in"], 2 * KD, hi, lo, SEQ,
                               take_act=lambda k, ps: nc.scalar.activation(
                                   zT[:, bass.ds(k, 1), :].rearrange("p o n -> p (o n)"), ps, ACT.Gelu_apprx_tanh))
                    sgu_phase(nc, t, zT, small, ident, eps, hi, lo)
                gemm_phase(nc, "gsout", t["w_gs_out"], KD, hi, lo, SEQ, take_dve=residual(nc, xT, mod(1, G_M)))
            ffn_w = small[:, ROW_FFN + l * KD:ROW_FFN + (l + 1) * KD]
            norm_phase(nc, f"nffn{l}", xT, SEQ, ffn_w, mod(l, SH_F), mod(l, SC_F), hi, lo, ones, eps)
            with Room(nc, f"rout{l}") as rr:
                s = rr.sb("s", [P, NB, HS, NKEYS])
                with Room(nc, f"qs{l}") as qr:
                    qT = qr.sb("qT", [P, HS, SEQ])
                    gemm_phase(nc, f"peerq{l}", t["w_peer_q"][l], HS, hi, lo, SEQ,
                               take_act=lambda k, ps: nc.scalar.activation(
                                   qT[:, bass.ds(k, 1), :].rearrange("p o n -> p (o n)"), ps, ACT.Copy))
                    scores_phase(nc, t, l, qT, s)
                topk_and_gate_phase(nc, t, l, s, ident, iota_b, iota16, g_dram)
            up_phase(nc, t, l, hi, lo, h_dram)
            down_phase(nc, t, l, g_dram, h_dram, xT, mod(l, G_F))

        with Room(nc, "final") as fr:
            y = fr.sb("y", [P, KD, SEQ])
            norm_phase(nc, "nout", xT, SEQ, small[:, ROW_OUT:ROW_OUT + KD], None, None, None, None, ones, eps, plain=y)
            s_o = fr.sem("out")
            block = fr.block()

            @block.sync
            def _(sp):
                sp.dma_start(out, y[:, :, :]).then_inc(s_o, 16)
                sp.wait_ge(s_o, 16)


def tiles_of(w):
    k, n = w.shape
    return w.reshape(k // P, P, n // P, P).transpose(2, 1, 0, 3)


def channels_first(x):
    return x.reshape(x.shape[0], KD, P).transpose(2, 1, 0)


def constants():
    half = HEAD_DIM // 2
    inv = np.float32(THETA) ** (-np.arange(0, half, 2, dtype=np.float32) / half)
    tok = np.arange(SEQ)
    row = (tok // GRID_W).astype(np.float32)[:, None] * inv
    col = (tok % GRID_W).astype(np.float32)[:, None] * inv
    cos, sin, swap = np.zeros((P, SEQ)), np.zeros((P, SEQ)), np.zeros((P, P))
    for p in range(P):
        d = p % HEAD_DIM
        ang = (row if d < half else col)[:, d % (half // 2)]
        low = d % half < half // 2
        cos[p] = np.cos(ang)
        sin[p] = -np.sin(ang) if low else np.sin(ang)
        swap[p + (half // 2 if low else -(half // 2)), p] = 1
    i, j = np.arange(P)[:, None], np.arange(P)[None, :]
    mask = np.stack([np.where(j >= i, 0, NEG), np.where(j <= i, 0, NEG)], 1)

    def dft(n):
        a = 2 * np.pi * (np.outer(np.arange(n), np.arange(n)) % n) / n
        return np.cos(a) / np.sqrt(n), np.sin(a) / np.sqrt(n)

    cc, sc = dft(P)
    cn, sn = dft(SEQ)
    blocks = lambda a: a.reshape(NB, P, SEQ).transpose(1, 0, 2)
    out = {
        "identity": np.eye(P), "rope_cos": cos, "rope_sin": sin, "swap": swap, "band_mask": mask,
        "dft_chan": np.concatenate([cc, sc], 1), "dft_cos": blocks(cn), "dft_msin": blocks(-sn),
        "iota16": np.tile(np.arange(TOPK), (P, 1)),
    }
    out = {k: np.ascontiguousarray(v, dtype=np.float32) for k, v in out.items()}
    out["iota_b"] = np.tile(np.arange(P), (P, 1)).astype(mybir.dt.np(BF16))
    return out


def kernel(**inputs):
    import concourse.bacc as bacc
    from concourse.bass_utils import run_bass_kernel_spmd

    a = {k: np.asarray(v) for k, v in inputs.items()}
    w_in = a["ab_w_in"][0]
    wq = w_in[:, :HEADS * HEAD_DIM].reshape(D, KV_HEADS, Q_PER_KV, HEAD_DIM).transpose(0, 2, 1, 3).reshape(D, -1)
    w_in = np.concatenate([wq, w_in[:, HEADS * HEAD_DIM:]], 1)
    w_out = a["ab_w_out"][0]
    wa = w_out[:HEADS * HEAD_DIM].reshape(KV_HEADS, Q_PER_KV, HEAD_DIM, D).transpose(1, 0, 2, 3).reshape(-1, D)
    w_out = np.concatenate([wa, w_out[HEADS * HEAD_DIM:]], 0)
    rows = [a["c"][0], a["c_ctx"], a["norm_mix_w"].reshape(-1), a["norm_ffn_w"].reshape(-1), a["norm_out_w"],
            a["gs_norm_w"][0]]
    arrays = {
        "xT": channels_first(a["x"][0]), "ctxT": channels_first(a["ctx"][0]),
        "small_rows": np.concatenate(rows).reshape(SMALL_ROWS, P),
        "ada_b_rows": a["ada_b"].reshape(DEPTH * ADA_ROWS, P),
        "ada_tiles": a["ada_w"].reshape(DEPTH, KD, P, N_MOD, D).transpose(0, 3, 2, 1, 4).reshape(-1, P, KD, D),
        "w_in": tiles_of(w_in), "w_ab_out": tiles_of(w_out),
        "w_gs_in": tiles_of(a["gs_w_in"][0]), "w_gs_out": tiles_of(a["gs_w_out"][0]),
        "w_peer_q": np.stack([tiles_of(w) for w in a["peer_w_q"]]),
        "attn_sink": a["attn_sink"][0], "gs_b_s": a["gs_b_s"][0].reshape(-1),
        "sgu_wT": a["gs_w_s"][0].transpose(2, 0, 1),
        "keysT": a["peer_keys"].reshape(DEPTH, HS, NKEYS, P).transpose(0, 3, 1, 2),
        "uT": a["peer_u"].reshape(DEPTH, NKEYS, NKEYS, KD, P).transpose(0, 1, 4, 3, 2),
        "peer_v": a["peer_v"].reshape(DEPTH, NKEYS, NKEYS, D),
    }
    arrays.update(constants())
    arrays = {k: np.ascontiguousarray(v) for k, v in arrays.items()}
    nc = bacc.Bacc("TRN2", target_bir_lowering=False, num_devices=1)
    t = {k: nc.dram_tensor(f"in_{k}", v.shape, mybir.dt.from_np(v.dtype), kind="ExternalInput").ap()
         for k, v in arrays.items()}
    out = nc.dram_tensor("out_T", (P, KD, SEQ), F32, kind="ExternalOutput").ap()
    program(nc, t, out)
    r = run_bass_kernel_spmd(nc, [{f"in_{k}": v for k, v in arrays.items()}], core_ids=[0])
    got = r.results[0]["out_T"]
    return np.ascontiguousarray(got.transpose(2, 1, 0)).reshape(1, SEQ, D)
```

```python
from contextlib import ExitStack

import numpy as np

import concourse.bass as bass
from concourse import mybir

F32 = mybir.dt.float32
F32R = mybir.dt.float32r
BF16 = mybir.dt.bfloat16
U32 = mybir.dt.uint32
ALU = mybir.AluOpType
ACT = mybir.ActivationFunctionType
AX = mybir.AxisListType

P = 128
D = 1024
KD = D // P
SEQ = 512
NB = SEQ // P
CTX = 256
NCB = CTX // P
DEPTH = 2
N_MOD = 6
HEADS, KV_HEADS, HEAD_DIM = 8, 2, 64
Q_PER_KV = HEADS // KV_HEADS
SCALE = HEAD_DIM ** -0.5
GRID_W = 64
THETA = 10000.0
FG = 4
SGU_G = 8
PH, NKEYS, TOPK = 8, 128, 16
HS = 2 * PH
HK = PH * TOPK
TG = 8
EPS = 1e-6
NEG = -1e30
KEYS = 3 * P + CTX
SH_M, SC_M, G_M, SH_F, SC_F, G_F = range(N_MOD)
ROW_C, ROW_CCTX, ROW_MIX, ROW_FFN, ROW_OUT, ROW_SGU = 0, 8, 16, 32, 48, 56
SMALL_ROWS = 64
ADA_ROWS = N_MOD * KD


class Room:

    def __init__(self, nc, tag):
        self.nc, self.tag, self.stack, self.sems = nc, tag, ExitStack(), []

    def __enter__(self):
        self.stack.__enter__()
        return self

    def __exit__(self, *a):
        said = self.stack.__exit__(*a)
        if self.sems:
            self.nc.clear_and_free_semaphores(self.sems)
            self.nc.all_engine_barrier()
        return said

    def sb(self, name, shape, dt=F32):
        return self.stack.enter_context(self.nc.sbuf_tensor(f"{self.tag}_{name}", shape, dt))

    def ps(self, name, shape, dt=F32):
        return self.stack.enter_context(self.nc.psum_tensor(f"{self.tag}_{name}", shape, dt))

    def sem(self, name):
        self.sems.append(self.nc.alloc_semaphore(f"{self.tag}_{name}"))
        return self.sems[-1]

    def block(self):
        return self.stack.enter_context(self.nc.Block())


def f32(ap):
    return ap.bitcast(F32)


def three_passes(nc, out, w_hi, w_lo, x_hi, x_lo, first, last):
    nc.tensor.matmul(out, w_hi, x_hi, start=first, stop=False)
    nc.tensor.matmul(out, w_hi, x_lo, start=False, stop=False)
    return nc.tensor.matmul(out, w_lo, x_hi, start=False, stop=last)


def load_phase(nc, t, xT, small, ada, ident):
    with Room(nc, "ada") as r:
        rows_a = r.sb("rows_a", [SMALL_ROWS, P])
        rows_b = r.sb("rows_b", [DEPTH * ADA_ROWS, P])
        bias = r.sb("bias", [P, DEPTH * ADA_ROWS])
        cond = r.sb("cond", [P, KD, 2])
        strip = [r.sb(f"strip{j}", [P, KD, D]) for j in range(2)]
        flat = [r.sb(f"flat{j}", [2, D]) for j in range(2)]
        turned = r.ps("turned", [P, 512])
        out = [r.ps(f"out{j}", [2, 2, 512]) for j in range(2)]
        cols = [r.ps(f"cols{j}", [P, 512]) for j in range(2)]
        s_flat, s_cols = r.sem("flat"), r.sem("cols")
        s_rows, s_x, s_turn, s_col, s_cond = (r.sem(n) for n in ("rows", "x", "turn", "col", "cond"))
        s_in = [r.sem(f"strip_in{j}") for j in range(2)]
        s_mm, s_out = r.sem("multiplied"), r.sem("taken")
        block = r.block()
        STRIPS = DEPTH * N_MOD

        @block.sync
        def _(sp):
            sp.dma_start(rows_a[:, :], t["small_rows"]).then_inc(s_rows, 16)
            sp.dma_start(rows_b[:, :], t["ada_b_rows"]).then_inc(s_rows, 16)
            sp.dma_start(ident[:, :], t["identity"]).then_inc(s_rows, 16)
            for j in range(2):
                sp.dma_start(strip[j][:, :, :], t["ada_tiles"][j]).then_inc(s_in[j], 16)
            sp.dma_start(xT[:, :, :], t["xT"]).then_inc(s_x, 16)
            with sp.Fori(1, STRIPS // 2) as it:
                for j in range(2):
                    sp.wait_ge(s_mm, it * 2 + j - 1)
                    sp.dma_start(strip[j][:, :, :],
                                 t["ada_tiles"][bass.ds(it * 2 + j, 1)].rearrange("o p k n -> (o p) k n")
                                 ).then_inc(s_in[j], 16)
            sp.wait_ge(s_x, 16)

        @block.tensor
        def _(pe):
            pe.wait_ge(s_rows, 48)
            nc.tensor.transpose(turned[:, 0:SMALL_ROWS], rows_a[:, :], ident[0:SMALL_ROWS, 0:SMALL_ROWS])
            nc.tensor.transpose(turned[:, P:P + 96], rows_b[:, :], ident[0:96, 0:96]).then_inc(s_turn, 1)
            pe.wait_ge(s_cond, 2)
            pe.sem_inc(s_cols, 2)
            with pe.Fori(0, STRIPS // 2) as it:
                for j in range(2):
                    pe.wait_ge(s_in[j], it * 16 + 16)
                    pe.wait_ge(s_flat, it * 2 + j + 1)
                    for k in range(KD):
                        for half in range(2):
                            mm = nc.tensor.matmul(out[j][:, half, :], cond[:, k, :],
                                                  strip[j][:, k, half * 512:(half + 1) * 512],
                                                  start=(k == 0), stop=(k == KD - 1))
                    mm.then_inc(s_mm, 1)
                    pe.wait_ge(s_flat, it * 2 + j + 3)
                    pe.wait_ge(s_out, it * 2 + j + 1)
                    for m in range(KD):
                        mm = nc.tensor.matmul(cols[j][:, 2 * m:2 * m + 2], flat[j][:, m * P:(m + 1) * P],
                                              ident[0:2, 0:2], start=True, stop=True)
                    mm.then_inc(s_cols, 1)

        @block.scalar
        def _(act):
            act.wait_ge(s_col, 2)
            act.activation(cond[:, :, 0], small[:, ROW_C:ROW_C + KD], ACT.Silu).then_inc(s_cond, 1)
            act.activation(cond[:, :, 1], small[:, ROW_CCTX:ROW_CCTX + KD], ACT.Silu).then_inc(s_cond, 1)
            act.sem_inc(s_flat, 2)
            with act.Fori(0, STRIPS // 2) as it:
                for j in range(2):
                    act.wait_ge(s_mm, it * 2 + j + 1)
                    act.wait_ge(s_cols, it * 2 + j + 1)
                    act.activation(flat[j][:, :].rearrange("p (h n) -> p h n", h=2), out[j][:, :, :],
                                   ACT.Copy).then_inc(s_flat, 1)

        @block.vector
        def _(dve):
            dve.sem_inc(s_out, 2)
            dve.wait_ge(s_turn, 1)
            nc.vector.tensor_copy(small[:, :], turned[:, 0:SMALL_ROWS]).then_inc(s_col, 1)
            nc.vector.tensor_copy(bias[:, :], turned[:, P:P + 96]).then_inc(s_col, 1)
            dve.wait_ge(s_col, 2)
            with dve.Fori(0, STRIPS // 2) as it:
                for j in range(2):
                    dve.wait_ge(s_cols, it * 2 + j + 3)
                    at = bass.ds((it * 2 + j) * KD, KD)
                    got = cols[j][:, 0:2 * KD].rearrange("p (m c) -> p c m", c=2)
                    nc.vector.tensor_tensor(ada[:, 0, at], got[:, 0, :], bias[:, at], ALU.add)
                    nc.vector.tensor_tensor(ada[:, 1, at], got[:, 1, :], bias[:, at], ALU.add).then_inc(s_out, 1)


def norm_phase(nc, tag, src, n, weight, shift, scale, hi, lo, ones, eps, plain=None):
    with Room(nc, tag) as r:
        square = [r.sb(f"square{j}", [P, n]) for j in range(2)]
        rstd = r.sb("rstd", [P, n])
        gain = r.sb("gain", [P, KD])
        normed = [r.sb(f"normed{j}", [P, n]) for j in range(2)]
        modded = [r.sb(f"modded{j}", [P, n]) for j in range(2)]
        total = r.ps("total", [P, 512])
        s_sq, s_sum, s_std, s_rstd, s_gain, s_n, s_m, s_hi, s_lo = (
            r.sem(x) for x in ("sq", "sum", "std", "rstd", "gain", "normed", "modded", "hi", "lo"))
        block = r.block()

        @block.tensor
        def _(pe):
            for k in range(KD):
                pe.wait_ge(s_sq, k + 1)
                nc.tensor.matmul(total[:, 0:n], ones[:, :], square[k % 2][:, :],
                                 start=(k == 0), stop=(k == KD - 1)).then_inc(s_sum, 1)

        @block.scalar
        def _(act):
            for k in range(KD):
                if k >= 2:
                    act.wait_ge(s_sum, k - 1)
                act.activation(square[k % 2][:, :], src[:, k, :], ACT.Square).then_inc(s_sq, 1)
            act.wait_ge(s_sum, KD)
            act.activation(rstd[:, :], total[:, 0:n], ACT.Sqrt, bias=eps[:, 0:1], scale=1.0 / D).then_inc(s_std, 1)
            if plain is not None:
                return
            act.wait_ge(s_gain, 2)
            for k in range(KD):
                act.wait_ge(s_n, k + 1)
                if k >= 2:
                    act.wait_ge(s_lo, k - 1)
                act.activation(modded[k % 2][:, :], normed[k % 2][:, :], ACT.Identity,
                               bias=shift[:, k:k + 1], scale=gain[:, k:k + 1]).then_inc(s_m, 1)
                act.wait_ge(s_m, k + 1)
                act.activation(hi[:, k, :], modded[k % 2][:, :], ACT.Copy).then_inc(s_hi, 1)

        @block.vector
        def _(dve):
            if plain is None:
                nc.vector.tensor_scalar(gain[:, :], scale, 1.0, None, ALU.add).then_inc(s_gain, 1)
                dve.wait_ge(s_gain, 1)
                nc.vector.tensor_tensor(gain[:, :], gain[:, :], weight, ALU.mult).then_inc(s_gain, 1)
            dve.wait_ge(s_std, 1)
            nc.vector.reciprocal(rstd[:, :], rstd[:, :]).then_inc(s_rstd, 1)
            dve.wait_ge(s_rstd, 1)
            if plain is not None:
                for k in range(KD):
                    nc.vector.scalar_tensor_tensor(out=plain[:, k, :], in0=src[:, k, :], scalar=weight[:, k:k + 1],
                                                   in1=rstd[:, :], op0=ALU.mult, op1=ALU.mult).then_inc(s_n, 1)
                return
            for k in range(KD + 1):
                if k < KD:
                    if k >= 2:
                        dve.wait_ge(s_m, k - 1)
                    nc.vector.tensor_tensor(normed[k % 2][:, :], src[:, k, :], rstd[:, :], ALU.mult).then_inc(s_n, 1)
                if k >= 1:
                    dve.wait_ge(s_hi, k)
                    nc.vector.tensor_tensor(lo[:, k - 1, :], modded[(k - 1) % 2][:, :], f32(hi[:, k - 1, :]),
                                            ALU.subtract).then_inc(s_lo, 1)


def gemm_phase(nc, tag, w, tiles, hi, lo, n, take_act=None, take_dve=None):
    with Room(nc, tag) as r:
        raw = [r.sb(f"raw{j}", [P, KD, P]) for j in range(2)]
        w_hi = [r.sb(f"w_hi{j}", [P, KD, P], F32R) for j in range(2)]
        w_lo = [r.sb(f"w_lo{j}", [P, KD, P], F32R) for j in range(2)]
        out = [r.ps(f"out{j}", [P, 512]) for j in range(2)]
        s_in = [r.sem(f"in{j}") for j in range(2)]
        s_hi, s_lo, s_mm, s_out = (r.sem(x) for x in ("hi", "lo", "multiplied", "taken"))
        block = r.block()

        @block.sync
        def _(sp):
            for j in range(2):
                sp.dma_start(raw[j][:, :, :], w[j]).then_inc(s_in[j], 16)
            if tiles > 2:
                with sp.Fori(1, tiles // 2) as it:
                    for j in range(2):
                        sp.wait_ge(s_lo, it * 2 + j - 1)
                        sp.dma_start(raw[j][:, :, :], w[bass.ds(it * 2 + j, 1)].rearrange("o p k n -> (o p) k n")
                                     ).then_inc(s_in[j], 16)

        def take(engine, body, q, j):
            t = q * 2 + j
            engine.wait_ge(s_mm, t + 3)
            body(t, out[j][:, 0:n]).then_inc(s_out, 1)

        def split_hi(q, j):
            nc.scalar.wait_ge(s_in[j], q * 16 + 16)
            nc.scalar.wait_ge(s_mm, q * 2 + j + 1)
            nc.scalar.activation(w_hi[j][:, :, :], raw[j][:, :, :], ACT.Copy).then_inc(s_hi, 1)

        def split_lo(q, j):
            nc.vector.wait_ge(s_hi, q * 2 + j + 1)
            nc.vector.tensor_tensor(w_lo[j][:, :, :], raw[j][:, :, :], f32(w_hi[j][:, :, :]),
                                    ALU.subtract).then_inc(s_lo, 1)

        def walk(engine, split, body):
            if body:
                engine.sem_inc(s_out, 2)
            split(0, 0)
            if tiles > 2:
                with engine.Fori(0, tiles // 2 - 1) as it:
                    split(it, 1)
                    if body:
                        take(engine, body, it, 0)
                    split(it + 1, 0)
                    if body:
                        take(engine, body, it, 1)
            split(tiles // 2 - 1, 1)
            if body:
                take(engine, body, tiles // 2 - 1, 0)
                take(engine, body, tiles // 2 - 1, 1)

        @block.scalar
        def _(act):
            walk(act, split_hi, take_act)

        @block.vector
        def _(dve):
            walk(dve, split_lo, take_dve)

        @block.tensor
        def _(pe):
            pe.sem_inc(s_mm, 2)
            with pe.Fori(0, tiles // 2) as it:
                for j in range(2):
                    t = it * 2 + j
                    pe.wait_ge(s_lo, t + 1)
                    pe.wait_ge(s_out, t + 1)
                    for k in range(KD):
                        mm = three_passes(nc, out[j][:, 0:n], w_hi[j][:, k, :], w_lo[j][:, k, :],
                                          hi[:, k, :], lo[:, k, :], k == 0, k == KD - 1)
                    mm.then_inc(s_mm, 1)


def residual(nc, xT, gate):
    def take(t, ps):
        x = xT[:, bass.ds(t, 1), :].rearrange("p o n -> p (o n)")
        return nc.vector.scalar_tensor_tensor(out=x, in0=ps, scalar=gate[:, bass.ds(t, 1)], in1=x,
                                              op0=ALU.mult, op1=ALU.add)
    return take


def rope_phase(nc, t, qkT, cos, sin):
    with Room(nc, "rope") as r:
        swap = r.sb("swap", [P, P])
        turned = [r.sb(f"turned{j}", [P, SEQ]) for j in range(2)]
        ps = [r.ps(f"ps{j}", [P, 512]) for j in range(2)]
        s_in, s_mm, s_sin, s_cos, s_add = (r.sem(x) for x in ("in", "swapped", "sin", "cos", "added"))
        block = r.block()

        @block.sync
        def _(sp):
            sp.dma_start(swap[:, :], t["swap"]).then_inc(s_in, 16)
            sp.dma_start(cos[:, :], t["rope_cos"]).then_inc(s_in, 16)
            sp.dma_start(sin[:, :], t["rope_sin"]).then_inc(s_in, 16)

        @block.tensor
        def _(pe):
            pe.wait_ge(s_in, 48)
            for m in range(5):
                if m >= 2:
                    pe.wait_ge(s_sin, m - 1)
                nc.tensor.matmul(ps[m % 2][:, :], swap[:, :], qkT[:, m, 0:SEQ], start=True, stop=True).then_inc(s_mm, 1)

        @block.vector
        def _(dve):
            dve.wait_ge(s_in, 48)
            for m in range(5):
                dve.wait_ge(s_mm, m + 1)
                if m >= 2:
                    dve.wait_ge(s_add, m - 1)
                nc.vector.tensor_tensor(turned[m % 2][:, :], ps[m % 2][:, :], sin[:, :], ALU.mult).then_inc(s_sin, 1)
                nc.vector.tensor_tensor(qkT[:, m, 0:SEQ], qkT[:, m, 0:SEQ], cos[:, :], ALU.mult).then_inc(s_cos, 1)
                dve.wait_ge(s_sin, m + 1)
                dve.wait_ge(s_cos, m + 1)
                nc.vector.tensor_tensor(qkT[:, m, 0:SEQ], qkT[:, m, 0:SEQ], turned[m % 2][:, :],
                                        ALU.add).then_inc(s_add, 1)


def attention_phase(nc, t, qkT, kcT, vT, vcT, ident, hi, lo):
    with Room(nc, "attn") as r:
        mask = r.sb("mask", [P, 2, P])
        sink = r.sb("sink", [P, HEADS])
        v = r.sb("v", [P, NB + NCB, P])
        s_sb = [r.sb(f"scores{j}", [P, KEYS]) for j in range(2)]
        prob = [r.sb(f"prob{j}", [P, KEYS]) for j in range(2)]
        pT = [r.sb(f"probT{j}", [P, KEYS // P, Q_PER_KV, P]) for j in range(2)]
        stat = r.sb("stat", [P, 2, 8])
        ps_s = [r.ps(f"ps_s{j}", [P, 2, 512]) for j in range(2)]
        ps_t = r.ps("ps_t", [P, 2, 512])
        ps_o = r.ps("ps_o", [P, 512])
        names = ("in", "vt", "v", "s", "sc", "ctx", "mx", "nm", "exp", "den", "rec", "norm", "tr", "pt", "pv",
                 "ohi", "olo")
        q = {x: r.sem(x) for x in names}
        block = r.block()
        units = [(n, g, j) for n in range(NB) for g in range(KV_HEADS) for j in range(Q_PER_KV)]

        def spans(n):
            return [(b, {n - 1: 0, n: None, n + 1: 1}[b]) for b in (n - 1, n, n + 1) if 0 <= b < NB]

        @block.sync
        def _(sp):
            sp.dma_start(mask[:, :, :], t["band_mask"]).then_inc(q["in"], 16)
            sp.dma_start(sink[:, :], t["attn_sink"].partition_broadcast(P)).then_inc(q["in"], 16)

        @block.tensor
        def _(pe):
            for b in range(NB + NCB):
                src = vT[:, b * P:(b + 1) * P] if b < NB else vcT[:, (b - NB) * P:(b - NB + 1) * P]
                mm = nc.tensor.transpose(ps_t[:, b // 4, (b % 4) * P:(b % 4 + 1) * P], src, ident[:, :])
            mm.then_inc(q["vt"], 1)

            def scores(u):
                n, g, j = units[u]
                if u >= 2:
                    pe.wait_ge(q["sc"], u - 1)
                    pe.wait_ge(q["ctx"], u - 1)
                h = slice(g * 64, g * 64 + 64)
                lhs = qkT[h, j, n * P:(n + 1) * P]
                first, width = spans(n)[0][0], len(spans(n)) * P
                nc.tensor.matmul(ps_s[u % 2][:, 0, 0:width], lhs, qkT[h, 4, first * P:first * P + width],
                                 start=True, stop=True)
                nc.tensor.matmul(ps_s[u % 2][:, 1, 0:CTX], lhs, kcT[h, :], start=True, stop=True).then_inc(q["s"], 1)

            def turn(u):
                n, g, j = units[u]
                pe.wait_ge(q["norm"], u + 1)
                if u == 0:
                    pe.wait_ge(q["v"], 1)
                else:
                    pe.wait_ge(q["pt"], u)
                blocks = len(spans(n)) + NCB
                for b in range(blocks):
                    mm = nc.tensor.transpose(ps_t[:, b // 4, (b % 4) * P:(b % 4 + 1) * P],
                                             prob[u % 2][:, b * P:(b + 1) * P], ident[:, :])
                mm.then_inc(q["tr"], 1)

            def values(u):
                n, g, _ = units[u]
                pe.wait_ge(q["pt"], u + 1)
                w = u // Q_PER_KV
                if w >= 1:
                    pe.wait_ge(q["olo"], w)
                blocks = [b for b, _ in spans(n)] + [NB + c for c in range(NCB)]
                for i, b in enumerate(blocks):
                    mm = nc.tensor.matmul(ps_o[g * 64:g * 64 + 64, :], v[:, b, g * 64:g * 64 + 64],
                                          pT[w % 2][:, i, :, :].rearrange("p j n -> p (j n)"),
                                          start=(i == 0), stop=(i == len(blocks) - 1))
                mm.then_inc(q["pv"], 1)

            scores(0)
            for u in range(len(units)):
                if u + 1 < len(units):
                    scores(u + 1)
                turn(u)
                if u % Q_PER_KV == Q_PER_KV - 1:
                    values(u)

        def evacuate(act, u):
            n, g, j = units[u]
            w = u // Q_PER_KV
            act.wait_ge(q["tr"], u + 1)
            if j == 0 and w >= 2:
                act.wait_ge(q["pv"], w - 1)
            blocks = len(spans(n)) + NCB
            for b0, b1 in ((0, 4), (4, blocks)):
                if b1 > b0:
                    last = act.activation(pT[w % 2][:, b0:b1, j, :],
                                          ps_t[:, b0 // 4, 0:(b1 - b0) * P].rearrange("p (b n) -> p b n", n=P), ACT.Copy)
            last.then_inc(q["pt"], 1)
            if j == Q_PER_KV - 1:
                act.wait_ge(q["pv"], w + 1)
                hs = slice(g * 64, g * 64 + 64)
                act.activation(hi[hs, 0:Q_PER_KV, n * P:(n + 1) * P],
                               ps_o[hs, :].rearrange("p (j n) -> p j n", n=P), ACT.Copy).then_inc(q["ohi"], 1)

        @block.scalar
        def _(act):
            for u, (n, g, j) in enumerate(units):
                c = len(spans(n)) * P
                act.wait_ge(q["s"], u + 1)
                if u >= 2:
                    act.wait_ge(q["exp"], 2 * (u - 1))
                act.activation(s_sb[u % 2][:, c:c + CTX], ps_s[u % 2][:, 1, 0:CTX], ACT.Copy).then_inc(q["ctx"], 1)
                act.wait_ge(q["nm"], u + 1)
                if u >= 2:
                    act.wait_ge(q["tr"], u - 1)
                st = stat[:, u % 2, :]
                h = g * Q_PER_KV + j
                act.activation(prob[u % 2][:, 0:c + CTX], s_sb[u % 2][:, 0:c + CTX], ACT.Exp, bias=st[:, 1:2],
                               scale=SCALE, accum_out=st[:, 2:3]).then_inc(q["exp"], 1)
                act.activation(st[:, 3:4], sink[:, h:h + 1], ACT.Exp, bias=st[:, 1:2]).then_inc(q["exp"], 1)
                if u >= 1:
                    evacuate(act, u - 1)
            evacuate(act, len(units) - 1)

        @block.vector
        def _(dve):
            dve.wait_ge(q["vt"], 1)
            nc.vector.tensor_copy(v[:, 0:4, :], ps_t[:, 0, :].rearrange("p (b n) -> p b n", n=P))
            nc.vector.tensor_copy(v[:, 4:6, :], ps_t[:, 1, 0:2 * P].rearrange("p (b n) -> p b n", n=P)).then_inc(q["v"], 1)
            dve.wait_ge(q["in"], 32)
            done = [0]

            def low_half(w):
                n, g, _ = units[w * Q_PER_KV]
                dve.wait_ge(q["ohi"], w + 1)
                hs = slice(g * 64, g * 64 + 64)
                nc.vector.tensor_tensor(lo[hs, 0:Q_PER_KV, n * P:(n + 1) * P],
                                        ps_o[hs, :].rearrange("p (j n) -> p j n", n=P),
                                        f32(hi[hs, 0:Q_PER_KV, n * P:(n + 1) * P]), ALU.subtract).then_inc(q["olo"], 1)

            for u, (n, g, j) in enumerate(units):
                st = stat[:, u % 2, :]
                c = len(spans(n)) * P
                h = g * Q_PER_KV + j
                dve.wait_ge(q["s"], u + 1)
                if u >= 2:
                    dve.wait_ge(q["exp"], 2 * (u - 1))
                for i, (b, side) in enumerate(spans(n)):
                    part = slice(i * P, (i + 1) * P)
                    if side is None:
                        last = nc.vector.tensor_copy(s_sb[u % 2][:, part], ps_s[u % 2][:, 0, part])
                    else:
                        last = nc.vector.tensor_tensor(s_sb[u % 2][:, part], ps_s[u % 2][:, 0, part], mask[:, side, :],
                                                       ALU.add)
                    last.then_inc(q["mx"], 1)
                    done[0] += 1
                dve.wait_ge(q["mx"], done[0])
                dve.sem_inc(q["sc"], 1)
                dve.wait_ge(q["ctx"], u + 1)
                nc.vector.reduce_max(st[:, 0:1], s_sb[u % 2][:, 0:c + CTX], AX.X).then_inc(q["mx"], 1)
                done[0] += 1
                dve.wait_ge(q["mx"], done[0])
                nc.vector.tensor_scalar(st[:, 4:5], st[:, 0:1], SCALE, sink[:, h:h + 1], ALU.mult, ALU.max).then_inc(q["mx"], 1)
                done[0] += 1
                dve.wait_ge(q["mx"], done[0])
                nc.vector.tensor_scalar(st[:, 1:2], st[:, 4:5], -1.0, None, ALU.mult).then_inc(q["nm"], 1)
                if u >= Q_PER_KV and j == 0:
                    low_half(u // Q_PER_KV - 1)
                dve.wait_ge(q["exp"], 2 * (u + 1))
                nc.vector.tensor_tensor(st[:, 5:6], st[:, 2:3], st[:, 3:4], ALU.add).then_inc(q["den"], 1)
                dve.wait_ge(q["den"], u + 1)
                nc.vector.reciprocal(st[:, 6:7], st[:, 5:6]).then_inc(q["rec"], 1)
                dve.wait_ge(q["rec"], u + 1)
                nc.vector.tensor_scalar(prob[u % 2][:, 0:c + CTX], prob[u % 2][:, 0:c + CTX], st[:, 6:7], None,
                                        ALU.mult).then_inc(q["norm"], 1)
            low_half(len(units) // Q_PER_KV - 1)


def fourier_phase(nc, t, fT, hi, lo):
    with Room(nc, "fft") as r:
        chan = r.sb("chan", [P, 2 * P])
        seq_c = r.sb("seq_c", [P, NB, SEQ])
        seq_s = r.sb("seq_s", [P, NB, SEQ])
        mid = [r.sb(f"mid{j}", [P, NB, 2 * P]) for j in range(2)]
        ps_a = [r.ps(f"ps_a{j}", [P, 2, 512]) for j in range(2)]
        ps_y = [r.ps(f"ps_y{j}", [P, 512]) for j in range(2)]
        s_in, s_a, s_mid, s_y, s_hi, s_lo = (r.sem(x) for x in ("in", "a", "mid", "y", "hi", "lo"))
        block = r.block()

        @block.sync
        def _(sp):
            sp.dma_start(chan[:, :], t["dft_chan"]).then_inc(s_in, 16)
            sp.dma_start(seq_c[:, :, :], t["dft_cos"]).then_inc(s_in, 16)
            sp.dma_start(seq_s[:, :, :], t["dft_msin"]).then_inc(s_in, 16)

        @block.tensor
        def _(pe):
            pe.wait_ge(s_in, 48)

            def first(g):
                if g >= 2:
                    pe.wait_ge(s_mid, g - 1)
                for b in range(NB):
                    mm = nc.tensor.matmul(ps_a[g % 2][:, b // 2, (b % 2) * 256:(b % 2 + 1) * 256],
                                          fT[:, g, b * P:(b + 1) * P], chan[:, :], start=True, stop=True)
                mm.then_inc(s_a, 1)

            first(0)
            for g in range(FG):
                if g + 1 < FG:
                    first(g + 1)
                pe.wait_ge(s_mid, g + 1)
                if g >= 2:
                    pe.wait_ge(s_lo, g - 1)
                for b in range(NB):
                    nc.tensor.matmul(ps_y[g % 2][:, :], mid[g % 2][:, b, 0:P], seq_c[:, b, :], start=(b == 0), stop=False)
                    mm = nc.tensor.matmul(ps_y[g % 2][:, :], mid[g % 2][:, b, P:2 * P], seq_s[:, b, :],
                                          start=False, stop=(b == NB - 1))
                mm.then_inc(s_y, 1)

        @block.scalar
        def _(act):
            for g in range(FG):
                act.wait_ge(s_y, g + 1)
                act.activation(hi[:, 4 + g, :], ps_y[g % 2][:, :], ACT.Copy).then_inc(s_hi, 1)

        @block.vector
        def _(dve):
            def low(g):
                dve.wait_ge(s_hi, g + 1)
                nc.vector.tensor_tensor(lo[:, 4 + g, :], ps_y[g % 2][:, :], f32(hi[:, 4 + g, :]),
                                        ALU.subtract).then_inc(s_lo, 1)

            for g in range(FG):
                dve.wait_ge(s_a, g + 1)
                if g >= 2:
                    dve.wait_ge(s_y, g - 1)
                nc.vector.tensor_copy(mid[g % 2][:, :, :],
                                      ps_a[g % 2][:, :, :].rearrange("p a (b n) -> p (a b) n", n=256)).then_inc(s_mid, 1)
                if g >= 1:
                    low(g - 1)
            low(FG - 1)


def sgu_phase(nc, t, zT, small, ident, eps, hi, lo):
    with Room(nc, "sgu") as r:
        ws = r.sb("ws", [P, SGU_G, P])
        bs = r.sb("bs", [P, SGU_G * P])
        v = [r.sb(f"v{b}", [P, D]) for b in range(NB)]
        square = r.sb("square", [P, D])
        stat = r.sb("stat", [P, NB, 4])
        gated = [r.sb(f"gated{j}", [P, NB, P]) for j in range(2)]
        prod = [r.sb(f"prod{j}", [P, SEQ]) for j in range(2)]
        ps_t = [r.ps(f"ps_t{j}", [P, 2, 512]) for j in range(2)]
        ps_m = [r.ps(f"ps_m{j}", [P, NB, P]) for j in range(2)]
        names = ("in", "t", "v", "sq", "std", "rs", "vn", "m", "sv", "pr", "hi", "lo")
        q = {x: r.sem(x) for x in names}
        block = r.block()

        @block.sync
        def _(sp):
            sp.dma_start(ws[:, :, :], t["sgu_wT"]).then_inc(q["in"], 16)
            sp.dma_start(bs[:, :], t["gs_b_s"].partition_broadcast(P)).then_inc(q["in"], 16)

        @block.tensor
        def _(pe):
            for b in range(NB):
                if b >= 2:
                    pe.wait_ge(q["v"], b - 1)
                for m in range(KD):
                    mm = nc.tensor.transpose(ps_t[b % 2][:, m // 4, (m % 4) * P:(m % 4 + 1) * P],
                                             zT[:, KD + m, b * P:(b + 1) * P], ident[:, :])
                mm.then_inc(q["t"], 1)
            pe.wait_ge(q["vn"], NB)
            pe.wait_ge(q["in"], 32)
            for g in range(SGU_G):
                if g >= 2:
                    pe.wait_ge(q["sv"], g - 1)
                for b in range(NB):
                    mm = nc.tensor.matmul(ps_m[g % 2][:, b, :], v[b][:, g * P:(g + 1) * P], ws[:, g, :],
                                          start=True, stop=True)
                mm.then_inc(q["m"], 1)

        @block.scalar
        def _(act):
            for b in range(NB):
                act.wait_ge(q["v"], b + 1)
                if b >= 1:
                    act.wait_ge(q["sq"], b)
                act.activation(square[:, :], v[b][:, :], ACT.Square, accum_out=stat[:, b, 0:1]).then_inc(q["sq"], 1)
                act.wait_ge(q["sq"], b + 1)
                act.activation(stat[:, b, 1:2], stat[:, b, 0:1], ACT.Sqrt, bias=eps[:, 0:1],
                               scale=1.0 / D).then_inc(q["std"], 1)
            for g in range(SGU_G):
                act.wait_ge(q["pr"], g + 1)
                act.activation(hi[:, g, :], prod[g % 2][:, :], ACT.Copy).then_inc(q["hi"], 1)

        @block.vector
        def _(dve):
            def scale_rows(b):
                dve.wait_ge(q["std"], b + 1)
                nc.vector.reciprocal(stat[:, b, 2:3], stat[:, b, 1:2]).then_inc(q["rs"], 1)
                dve.wait_ge(q["rs"], b + 1)
                nc.vector.tensor_scalar(v[b][:, :], v[b][:, :], stat[:, b, 2:3], None, ALU.mult).then_inc(q["vn"], 1)

            for b in range(NB):
                dve.wait_ge(q["t"], b + 1)
                nc.vector.tensor_copy(v[b][:, :], ps_t[b % 2][:, :, :].rearrange("p a n -> p (a n)")).then_inc(q["v"], 1)
                if b >= 1:
                    scale_rows(b - 1)
            scale_rows(NB - 1)
            dve.wait_ge(q["in"], 32)

            def low(g):
                dve.wait_ge(q["hi"], g + 1)
                nc.vector.tensor_tensor(lo[:, g, :], prod[g % 2][:, :], f32(hi[:, g, :]), ALU.subtract).then_inc(q["lo"], 1)

            for g in range(SGU_G):
                dve.wait_ge(q["m"], g + 1)
                if g >= 2:
                    dve.wait_ge(q["pr"], g - 1)
                nc.vector.scalar_tensor_tensor(
                    out=gated[g % 2][:, :, :], in0=ps_m[g % 2][:, :, :],
                    scalar=small[:, ROW_SGU + g:ROW_SGU + g + 1],
                    in1=bs[:, g * P:(g + 1) * P].unsqueeze(1).broadcast_to([P, NB, P]),
                    op0=ALU.mult, op1=ALU.add).then_inc(q["sv"], 1)
                dve.wait_ge(q["sv"], g + 1)
                if g >= 2:
                    dve.wait_ge(q["lo"], g - 1)
                nc.vector.tensor_tensor(prod[g % 2][:, :], gated[g % 2][:, :, :].rearrange("p b n -> p (b n)"),
                                        zT[:, g, :], ALU.mult).then_inc(q["pr"], 1)
                if g >= 1:
                    low(g - 1)
            low(SGU_G - 1)


def scores_phase(nc, t, l, qT, s):
    with Room(nc, f"keys{l}") as r:
        keys = r.sb("keys", [P, HS, NKEYS])
        ps = [r.ps(f"ps{j}", [P, NB, P]) for j in range(2)]
        s_in, s_mm, s_out = (r.sem(x) for x in ("in", "multiplied", "taken"))
        block = r.block()

        @block.sync
        def _(sp):
            sp.dma_start(keys[:, :, :], t["keysT"][l]).then_inc(s_in, 16)

        @block.tensor
        def _(pe):
            pe.wait_ge(s_in, 16)
            for m in range(HS):
                if m >= 2:
                    pe.wait_ge(s_out, m - 1)
                for b in range(NB):
                    mm = nc.tensor.matmul(ps[m % 2][:, b, :], qT[:, m, b * P:(b + 1) * P], keys[:, m, :],
                                          start=True, stop=True)
                mm.then_inc(s_mm, 1)

        @block.vector
        def _(dve):
            for m in range(HS):
                dve.wait_ge(s_mm, m + 1)
                nc.vector.tensor_copy(s[:, :, m, :], ps[m % 2][:, :, :]).then_inc(s_out, 1)


def route_and_up_phase(nc, t, l, s, hi, lo, ident, iota, iota16, g_dram, h_dram):
    with Room(nc, f"up{l}") as r:
        raw = [r.sb(f"raw{j}", [P, KD, P]) for j in range(2)]
        w_hi = [r.sb(f"w_hi{j}", [P, KD, P], F32R) for j in range(2)]
        w_lo = [r.sb(f"w_lo{j}", [P, KD, P], F32R) for j in range(2)]
        acts = [r.sb(f"acts{j}", [P, SEQ]) for j in range(2)]
        val = r.sb("val", [P, HS, TOPK])
        idx = r.sb("idx", [P, HS, TOPK], U32)
        idx_f = r.sb("idx_f", [P, HS, TOPK])
        cand = r.sb("cand", [P, PH, TOPK * TOPK])
        best = r.sb("best", [P, PH, TOPK])
        less = r.sb("less", [P, PH, TOPK])
        pos = r.sb("pos", [P, HK], U32)
        pos_i = r.sb("pos_i", [P, 2, HK], U32)
        pos_f = r.sb("pos_f", [P, 2, HK])
        den = r.sb("den", [P, 2, PH])
        pack = r.sb("pack", [P, 3, HK])
        index = r.sb("index", [P, 2, P], BF16)
        piece = r.sb("piece", [P, 3, P], BF16)
        rest = r.sb("rest", [P, 2, P])
        hot1 = r.sb("hot1", [P, 4, NKEYS, TG], BF16)
        hot0 = cand[:, :, :].rearrange("p h n -> p (h n)").bitcast(BF16).rearrange(
            "p (c i k) -> p c i k", c=4, k=TG)
        hot = [hot0, hot1[:, :, :, :]]
        stage = r.sb("stage", [P, NKEYS, P])
        out = [r.ps(f"out{j}", [P, 512]) for j in range(2)]
        ps_t = r.ps("ps_t", [P, 512])
        ps_g = [r.ps(f"ps_g{j}", [P, TG, P]) for j in range(2)]
        s_in = [r.sem(f"in{j}") for j in range(2)]
        s_store = [r.sem(f"act_stored{j}") for j in range(2)]
        s_hi, s_lo, s_mm, s_out, s_free = (r.sem(x) for x in ("hi", "lo", "multiplied", "taken", "free"))
        s_d, s_less, s_exp, s_pack, s_turn, s_one, s_hot, s_gmm, s_gout, s_gst = (
            r.sem(x) for x in ("chain", "less", "exp", "packed", "turned", "onehot", "hot", "gates_multiplied",
                               "gates_taken", "gates_stored"))
        w = t["uT"][l]
        block = r.block()
        PART = NKEYS // NB // 2
        PAIRS = PART // 2

        @block.sync
        def _(sp):
            def loads(first, last):
                with sp.Fori(first // 2, last // 2) as it:
                    for j in range(2):
                        sp.wait_ge(s_lo, it * 2 + j - 1)
                        sp.dma_start(raw[j][:, :, :], w[bass.ds(it * 2 + j, 1)].rearrange("o p k n -> (o p) k n")
                                     ).then_inc(s_in[j], 16)

            for j in range(2):
                sp.dma_start(raw[j][:, :, :], w[j]).then_inc(s_in[j], 16)
            at = 2
            for b in range(NB):
                upto = min((b + 1) * 2 * PART + 6, NKEYS)
                loads(at, upto)
                at = upto
                sp.wait_ge(s_gout, 2 + (b + 1) * PART)
                sp.dma_start(g_dram[:, :, b * P:(b + 1) * P].rearrange("a p n -> p a n"), stage[:, :, :]
                             ).then_inc(s_gst, 16)
            sp.wait_ge(s_gst, 16 * NB)

        @block.gpsimd
        def _(pool):
            pool.sem_inc(s_free, 2)
            with pool.Fori(0, NKEYS // 2) as it:
                for j in range(2):
                    pool.wait_ge(s_out, it * 2 + j + 3)
                    pool.dma_start(h_dram[bass.ds(it * 2 + j, 1)].rearrange("o p n -> (o p) n"), acts[j][:, :]
                                   ).then_inc(s_store[j], 16)
                    pool.wait_ge(s_store[j], it * 16 + 16)
                    pool.sem_inc(s_free, 1)

        @block.scalar
        def _(act):
            act.sem_inc(s_out, 2)
            act.sem_inc(s_gout, 2)

            def split_hi(q, j):
                act.wait_ge(s_in[j], q * 16 + 16)
                act.wait_ge(s_mm, q * 2 + j + 1)
                act.activation(w_hi[j][:, :, :], raw[j][:, :, :], ACT.Copy).then_inc(s_hi, 1)

            def gelu(q, j):
                act.wait_ge(s_mm, q * 2 + j + 3)
                act.wait_ge(s_free, q * 2 + j + 1)
                act.activation(acts[j][:, :], out[j][:, :], ACT.Gelu_apprx_tanh).then_inc(s_out, 1)

            def take_gates(b, k, j):
                act.wait_ge(s_gmm, b * PART + k + 3)
                act.activation(stage[:, :, bass.ds(k * TG, TG)], ps_g[j][:, :, :].rearrange("p k n -> p n k"),
                               ACT.Copy).then_inc(s_gout, 1)

            def pair(q, b=None, k=None, last=False):
                split_hi(q, 1)
                gelu(q, 0)
                if b is not None:
                    take_gates(b, k, 0)
                if not last:
                    split_hi(q + 1, 0)
                gelu(q, 1)
                if b is not None:
                    take_gates(b, k + 1, 1)

            split_hi(0, 0)
            for b in range(NB):
                q0 = b * PART
                with act.Fori(0, PAIRS - 1) as it:
                    pair(it + q0)
                act.wait_ge(s_less, b + 1)
                act.activation(less[:, :, :], less[:, :, :], ACT.Exp).then_inc(s_exp, 1)
                pair(q0 + PAIRS - 1)
                if b >= 1:
                    act.wait_ge(s_gst, 16 * b)
                with act.Fori(0, PAIRS - (b == NB - 1)) as it:
                    pair(it + (q0 + PAIRS), b, it * 2)
                if b == NB - 1:
                    pair(q0 + 2 * PAIRS - 1, b, PART - 2, last=True)

        @block.tensor
        def _(pe):
            pe.sem_inc(s_mm, 2)
            pe.sem_inc(s_gmm, 2)

            def up(q, j):
                pe.wait_ge(s_lo, q * 2 + j + 1)
                pe.wait_ge(s_out, q * 2 + j + 1)
                for k in range(KD):
                    mm = three_passes(nc, out[j][:, :], w_hi[j][:, k, :], w_lo[j][:, k, :],
                                      hi[:, k, :], lo[:, k, :], k == 0, k == KD - 1)
                mm.then_inc(s_mm, 1)

            for b in range(NB):
                with pe.Fori(b * PART, b * PART + PAIRS) as it:
                    up(it, 0)
                    up(it, 1)
                pe.wait_ge(s_pack, b + 1)
                for c in range(3):
                    mm = nc.tensor.transpose(ps_t[:, c * P:(c + 1) * P], pack[:, c, :], ident[:, :])
                mm.then_inc(s_turn, 1)
                with pe.Fori(0, PAIRS) as it:
                    for j in range(2):
                        up(it + (b * PART + PAIRS), j)
                        grp = it * 2 + (b * PART + j)
                        pe.wait_ge(s_hot, grp + 1)
                        pe.wait_ge(s_gout, grp + 1)
                        for k in range(TG):
                            for p in range(3):
                                mm = nc.tensor.matmul(ps_g[j][:, k, :], hot[j][:, 3, :, k], hot[j][:, p, :, k],
                                                      start=(p == 0), stop=(p == 2))
                        mm.then_inc(s_gmm, 1)

        @block.vector
        def _(dve):
            n = [0]

            def after(ins):
                n[0] += 1
                ins.then_inc(s_d, 1)
                dve.wait_ge(s_d, n[0])

            def split_lo(q, j):
                dve.wait_ge(s_hi, q * 2 + j + 1)
                nc.vector.tensor_tensor(w_lo[j][:, :, :], raw[j][:, :, :], f32(w_hi[j][:, :, :]),
                                        ALU.subtract).then_inc(s_lo, 1)

            def top16(values, indices, row):
                for half in range(2):
                    part = slice(8 * half, 8 * half + 8)
                    after(nc.vector.max(values[:, part], row))
                    after(nc.vector.max_index(indices[:, part], values[:, part], row))
                    if half == 0:
                        after(nc.vector.match_replace(out=row, in_to_replace=values[:, part], in_values=row,
                                                      imm_value=-3.0e38))

            v2 = val[:, :, :].rearrange("p (h s) k -> p h s k", s=2)
            i2v = idx_f[:, :, :].rearrange("p (h s) k -> p h s k", s=2)
            pick = cand[:, :, :].rearrange("p h (k a) -> p h k a", a=TOPK)
            grid = [P, PH, TOPK, TOPK]

            def candidates(b, h):
                if b >= 1 and h == 0:
                    dve.wait_ge(s_gmm, 2 + b * PART)
                c = cand[:, h, :].rearrange("p (a b) -> p a b", b=TOPK)
                after(nc.vector.tensor_tensor(c, v2[:, h, 0, :].unsqueeze(2).broadcast_to([P, TOPK, TOPK]),
                                              v2[:, h, 1, :].unsqueeze(1).broadcast_to([P, TOPK, TOPK]), ALU.add))
                top16(best[:, h, :], pos[:, h * TOPK:(h + 1) * TOPK], cand[:, h, :])

            def positions(b):
                nc.vector.tensor_tensor(less[:, :, :], best[:, :, :], best[:, :, 0:1].broadcast_to([P, PH, TOPK]),
                                        ALU.subtract).then_inc(s_less, 1)
                nc.vector.tensor_single_scalar(pos_i[:, 0, :], pos[:, :], 4, ALU.logical_shift_right)
                after(nc.vector.tensor_single_scalar(pos_i[:, 1, :], pos[:, :], 15, ALU.bitwise_and))
                after(nc.vector.tensor_copy(pos_f[:, :, :], pos_i[:, :, :]))
                after(nc.vector.tensor_copy(idx_f[:, :, :], idx[:, :, :]))

            def pick_where(side):
                p3 = pos_f[:, side, :].rearrange("p (h k) -> p h k", k=TOPK)
                after(nc.vector.tensor_tensor(pick, p3.unsqueeze(3).broadcast_to(grid),
                                              iota16[:, :].unsqueeze(1).unsqueeze(1).broadcast_to(grid), ALU.is_equal))

            def pick_times(side):
                after(nc.vector.tensor_tensor(pick, pick, i2v[:, :, side, :].unsqueeze(2).broadcast_to(grid), ALU.mult))

            def pick_sum(side):
                after(nc.vector.reduce_sum(pack[:, side, :], pick.rearrange("p h k a -> p (h k) a"), AX.X))

            def softmax(b):
                dve.wait_ge(s_exp, b + 1)
                after(nc.vector.reduce_sum(den[:, 0, :], less[:, :, :], AX.X))
                after(nc.vector.reciprocal(den[:, 1, :], den[:, 0, :]))
                nc.vector.tensor_tensor(pack[:, 2, :].rearrange("p (h k) -> p h k", k=TOPK), less[:, :, :],
                                        den[:, 1, :].unsqueeze(2).broadcast_to([P, PH, TOPK]),
                                        ALU.mult).then_inc(s_pack, 1)

            def columns(b):
                dve.wait_ge(s_turn, b + 1)
                nc.vector.tensor_copy(index[:, :, :], ps_t[:, 0:2 * P].rearrange("p (c n) -> p c n", n=P))
                gate = ps_t[:, 2 * P:3 * P]
                after(nc.vector.tensor_copy(piece[:, 0, :], gate))
                after(nc.vector.tensor_tensor(rest[:, 0, :], gate, piece[:, 0, :], ALU.subtract))
                after(nc.vector.tensor_copy(piece[:, 1, :], rest[:, 0, :]))
                after(nc.vector.tensor_tensor(rest[:, 1, :], rest[:, 0, :], piece[:, 1, :], ALU.subtract))
                after(nc.vector.tensor_copy(piece[:, 2, :], rest[:, 1, :]))

            def one_hots(b, k, j):
                grp = k + b * PART
                dve.wait_ge(s_gmm, grp + 1)
                at = bass.ds(k * TG, TG)
                shape = [P, NKEYS, TG]
                nc.vector.tensor_tensor(hot[j][:, 0, :, :], iota[:, :, :],
                                        index[:, 0, at].unsqueeze(1).broadcast_to(shape), ALU.is_equal).then_inc(s_one, 1)
                nc.vector.tensor_tensor(hot[j][:, 3, :, :], iota[:, :, :],
                                        index[:, 1, at].unsqueeze(1).broadcast_to(shape), ALU.is_equal)
                dve.wait_ge(s_one, grp + 1)
                for p in (2, 1, 0):
                    last = nc.vector.tensor_tensor(hot[j][:, p, :, :], hot[j][:, 0, :, :],
                                                   piece[:, p, at].unsqueeze(1).broadcast_to(shape), ALU.mult)
                last.then_inc(s_hot, 1)

            split_lo(0, 0)
            for b in range(NB):
                beside = [[(top16, (val[:, m, :], idx[:, m, :], s[:, b, m, :])) for m in (2 * i, 2 * i + 1)]
                          for i in range(HS // 2)]
                beside += [[(candidates, (b, 2 * i)), (candidates, (b, 2 * i + 1))] for i in range(PH // 2)]
                beside += [[(positions, (b,)), (pick_where, (0,))], [(pick_times, (0,)), (pick_sum, (0,))],
                           [(pick_where, (1,)), (pick_times, (1,))], [(pick_sum, (1,)), (softmax, (b,))]]
                for c, work in enumerate(beside):
                    split_lo(b * PART + (c + 1) // 2, (c + 1) % 2)
                    for f, args in work:
                        f(*args)
                columns(b)
                q0 = b * PART + PAIRS
                with dve.Fori(0, PAIRS - (b == NB - 1)) as it:
                    one_hots(b, it * 2, 0)
                    split_lo(it + q0, 1)
                    one_hots(b, it * 2 + 1, 1)
                    split_lo(it + (q0 + 1), 0)
                if b == NB - 1:
                    one_hots(b, PART - 2, 0)
                    split_lo(q0 + PAIRS - 1, 1)
                    one_hots(b, PART - 1, 1)


def down_phase(nc, t, l, g_dram, h_dram, xT, gate):
    with Room(nc, f"down{l}") as r:
        C = 4
        GROUPS = NKEYS // C
        raw = [r.sb(f"raw{j}", [P, D]) for j in range(2)]
        gin = [r.sb(f"gin{j}", [P, SEQ]) for j in range(2)]
        hin = [r.sb(f"hin{j}", [P, SEQ]) for j in range(2)]
        wgt = [r.sb(f"wgt{j}", [P, SEQ]) for j in range(2)]
        v_hi = [r.sb(f"v_hi{j}", [P, C, D], F32R) for j in range(2)]
        v_lo = [r.sb(f"v_lo{j}", [P, C, D], F32R) for j in range(2)]
        w_hi = [r.sb(f"w_hi{j}", [P, C, SEQ], F32R) for j in range(2)]
        w_lo = [r.sb(f"w_lo{j}", [P, C, SEQ], F32R) for j in range(2)]
        acc = r.sb("acc", [P, KD, SEQ])
        out = [r.ps(f"out{j}", [P, 512]) for j in range(KD)]
        s_v = [r.sem(f"v_in{j}") for j in range(2)]
        s_g = [r.sem(f"gh_in{j}") for j in range(2)]
        s_vhi, s_vlo, s_w, s_whi, s_wlo, s_mm, s_grp, s_acc, s_zero = (
            r.sem(x) for x in ("vhi", "vlo", "w", "whi", "wlo", "multiplied", "group", "acc", "zero"))
        v_dram = t["peer_v"][l]
        block = r.block()

        @block.sync
        def _(sp):
            def load(c, j):
                sp.dma_start(raw[j][:, :], v_dram[bass.ds(c, 1)].rearrange("o p n -> (o p) n")).then_inc(s_v[j], 16)
                sp.dma_start(gin[j][:, :], g_dram[bass.ds(c, 1)].rearrange("o p n -> (o p) n")).then_inc(s_g[j], 16)
                sp.dma_start(hin[j][:, :], h_dram[bass.ds(c, 1)].rearrange("o p n -> (o p) n")).then_inc(s_g[j], 16)
            for j in range(2):
                load(j, j)
            with sp.Fori(1, NKEYS // 2) as it:
                for j in range(2):
                    sp.wait_ge(s_vlo, it * 2 + j - 1)
                    sp.wait_ge(s_w, it * 2 + j - 1)
                    load(it * 2 + j, j)

        @block.scalar
        def _(act):
            with act.Fori(0, GROUPS // 2) as it:
                for s in range(2):
                    act.wait_ge(s_grp, it * 2 + s + 1)
                    for i in range(C):
                        j = i % 2
                        c = (it * 2 + s) * C + i
                        act.wait_ge(s_v[j], (it * C + s * (C // 2) + i // 2 + 1) * 16)
                        act.activation(v_hi[s][:, i, :], raw[j][:, :], ACT.Copy).then_inc(s_vhi, 1)
                        act.wait_ge(s_w, c + 1)
                        act.activation(w_hi[s][:, i, :], wgt[j][:, :], ACT.Copy).then_inc(s_whi, 1)

        @block.vector
        def _(dve):
            nc.vector.memset(acc[:, :, :], 0.0).then_inc(s_zero, 1)
            dve.wait_ge(s_zero, 1)
            dve.sem_inc(s_acc, 2 * KD)

            def add_up(g, s_first):
                for m in range(KD):
                    dve.wait_ge(s_mm, g * KD + m + 1)
                    nc.vector.tensor_tensor(acc[:, m, :], acc[:, m, :], out[m][:, :], ALU.add).then_inc(s_acc, 1)

            def group(g, s, it):
                for i in range(C):
                    j = i % 2
                    c = g * C + i
                    dve.wait_ge(s_g[j], (it * C + s * (C // 2) + i // 2 + 1) * 32)
                    nc.vector.tensor_tensor(wgt[j][:, :], gin[j][:, :], hin[j][:, :], ALU.mult).then_inc(s_w, 1)
                    dve.wait_ge(s_vhi, c + 1)
                    nc.vector.tensor_tensor(v_lo[s][:, i, :], raw[j][:, :], f32(v_hi[s][:, i, :]),
                                            ALU.subtract).then_inc(s_vlo, 1)
                    dve.wait_ge(s_whi, c + 1)
                    nc.vector.tensor_tensor(w_lo[s][:, i, :], wgt[j][:, :], f32(w_hi[s][:, i, :]),
                                            ALU.subtract).then_inc(s_wlo, 1)

            group(0, 0, 0)
            group(1, 1, 0)
            add_up(0, 0)
            with dve.Fori(1, GROUPS // 2) as it:
                for s in range(2):
                    group(it * 2 + s, s, it)
                    add_up(it * 2 + s - 1, s)
            add_up(GROUPS - 1, 0)
            for m in range(KD):
                dve.wait_ge(s_acc, 2 * KD + GROUPS * KD)
                nc.vector.scalar_tensor_tensor(out=xT[:, m, :], in0=acc[:, m, :], scalar=gate[:, m:m + 1],
                                               in1=xT[:, m, :], op0=ALU.mult, op1=ALU.add).then_inc(s_zero, 1)

        @block.tensor
        def _(pe):
            pe.sem_inc(s_grp, 2)
            with pe.Fori(0, GROUPS // 2) as it:
                for s in range(2):
                    g = it * 2 + s
                    pe.wait_ge(s_vlo, (g + 1) * C)
                    pe.wait_ge(s_wlo, (g + 1) * C)
                    for m in range(KD):
                        pe.wait_ge(s_acc, (g + 1) * KD + m + 1)
                        for i in range(C):
                            mm = three_passes(nc, out[m][:, :], v_hi[s][:, i, m * P:(m + 1) * P],
                                              v_lo[s][:, i, m * P:(m + 1) * P], w_hi[s][:, i, :], w_lo[s][:, i, :],
                                              i == 0, i == C - 1)
                        mm.then_inc(s_mm, 1)
                    pe.wait_ge(s_mm, (g + 1) * KD)
                    pe.sem_inc(s_grp, 1)


def program(nc, t, out):
    g_dram = nc.dram_tensor("gates", (NKEYS, NKEYS, SEQ), F32, kind="Internal").ap()
    h_dram = nc.dram_tensor("activations", (NKEYS, NKEYS, SEQ), F32, kind="Internal").ap()
    with Room(nc, "all") as r:
        xT = r.sb("xT", [P, KD, SEQ])
        hi = r.sb("h_hi", [P, KD, SEQ], F32R)
        lo = r.sb("h_lo", [P, KD, SEQ], F32R)
        small = r.sb("small", [P, SMALL_ROWS])
        ada = r.sb("ada", [P, 2, DEPTH * ADA_ROWS])
        ident = r.sb("ident", [P, P])
        ones = r.sb("ones", [P, P])
        eps = r.sb("eps", [P, 1])
        iota_b = r.sb("iota_b", [P, NKEYS, TG], BF16)
        iota16 = r.sb("iota16", [P, TOPK])

        def mod(l, which, cond=0):
            at = (l * N_MOD + which) * KD
            return ada[:, cond, at:at + KD]

        load_phase(nc, t, xT, small, ada, ident)
        with Room(nc, "const") as c:
            s_c, s_m = c.sem("in"), c.sem("set")
            block = c.block()

            @block.sync
            def _(sp):
                sp.dma_start(iota_b[:, :, :], t["iota_b"]).then_inc(s_c, 16)
                sp.dma_start(iota16[:, :], t["iota16"]).then_inc(s_c, 16)
                sp.wait_ge(s_c, 32)

            @block.vector
            def _(dve):
                nc.vector.memset(ones[:, :], 1.0).then_inc(s_m, 1)
                nc.vector.memset(eps[:, :], EPS).then_inc(s_m, 1)
                dve.wait_ge(s_m, 2)

        with Room(nc, "mix0") as m0:
            qkvT = m0.sb("qkvT", [P, 6, SEQ])
            fT = m0.sb("fT", [P, FG, SEQ])
            kvcT = m0.sb("kvcT", [P, 2, CTX])
            with Room(nc, "ctx") as cr:
                ctxT = cr.sb("ctxT", [P, KD, CTX])
                c_hi = cr.sb("c_hi", [P, KD, CTX], F32R)
                c_lo = cr.sb("c_lo", [P, KD, CTX], F32R)
                with Room(nc, "ctxin") as ci:
                    s_c = ci.sem("in")
                    block = ci.block()

                    @block.sync
                    def _(sp):
                        sp.dma_start(ctxT[:, :, :], t["ctxT"]).then_inc(s_c, 16)
                        sp.wait_ge(s_c, 16)

                norm_phase(nc, "nctx", ctxT, CTX, small[:, ROW_MIX:ROW_MIX + KD], mod(0, SH_M, 1), mod(0, SC_M, 1),
                           c_hi, c_lo, ones, eps)
                gemm_phase(nc, "kvctx", t["w_in"][4:6], 2, c_hi, c_lo, CTX,
                           take_act=lambda k, ps: nc.scalar.activation(
                               kvcT[:, bass.ds(k, 1), :].rearrange("p o n -> p (o n)"), ps, ACT.Copy))
            norm_phase(nc, "nmix0", xT, SEQ, small[:, ROW_MIX:ROW_MIX + KD], mod(0, SH_M), mod(0, SC_M),
                       hi, lo, ones, eps)
            gemm_phase(nc, "qkv", t["w_in"][0:6], 6, hi, lo, SEQ,
                       take_act=lambda k, ps: nc.scalar.activation(
                           qkvT[:, bass.ds(k, 1), :].rearrange("p o n -> p (o n)"), ps, ACT.Copy))
            gemm_phase(nc, "four", t["w_in"][6:10], 4, hi, lo, SEQ,
                       take_act=lambda k, ps: nc.scalar.activation(
                           fT[:, bass.ds(k, 1), :].rearrange("p o n -> p (o n)"), ps, ACT.Copy))
            with Room(nc, "ropet") as rt:
                cos = rt.sb("cos", [P, SEQ])
                sin = rt.sb("sin", [P, SEQ])
                rope_phase(nc, t, qkvT, cos, sin)
            attention_phase(nc, t, qkvT, kvcT[:, 0, :], qkvT[:, 5, :], kvcT[:, 1, :], ident, hi, lo)
            fourier_phase(nc, t, fT, hi, lo)
        gemm_phase(nc, "about", t["w_ab_out"], KD, hi, lo, SEQ, take_dve=residual(nc, xT, mod(0, G_M)))

        for l in range(DEPTH):
            if l == 1:
                norm_phase(nc, "nmix1", xT, SEQ, small[:, ROW_MIX + KD:ROW_MIX + 2 * KD], mod(1, SH_M), mod(1, SC_M),
                           hi, lo, ones, eps)
                with Room(nc, "mix1") as m1:
                    zT = m1.sb("zT", [P, 2 * KD, SEQ])
                    gemm_phase(nc, "gsin", t["w_gs_in"], 2 * KD, hi, lo, SEQ,
                               take_act=lambda k, ps: nc.scalar.activation(
                                   zT[:, bass.ds(k, 1), :].rearrange("p o n -> p (o n)"), ps, ACT.Gelu_apprx_tanh))
                    sgu_phase(nc, t, zT, small, ident, eps, hi, lo)
                gemm_phase(nc, "gsout", t["w_gs_out"], KD, hi, lo, SEQ, take_dve=residual(nc, xT, mod(1, G_M)))
            ffn_w = small[:, ROW_FFN + l * KD:ROW_FFN + (l + 1) * KD]
            norm_phase(nc, f"nffn{l}", xT, SEQ, ffn_w, mod(l, SH_F), mod(l, SC_F), hi, lo, ones, eps)
            with Room(nc, f"rout{l}") as rr:
                s = rr.sb("s", [P, NB, HS, NKEYS])
                with Room(nc, f"qs{l}") as qr:
                    qT = qr.sb("qT", [P, HS, SEQ])
                    gemm_phase(nc, f"peerq{l}", t["w_peer_q"][l], HS, hi, lo, SEQ,
                               take_act=lambda k, ps: nc.scalar.activation(
                                   qT[:, bass.ds(k, 1), :].rearrange("p o n -> p (o n)"), ps, ACT.Copy))
                    scores_phase(nc, t, l, qT, s)
                route_and_up_phase(nc, t, l, s, hi, lo, ident, iota_b, iota16, g_dram, h_dram)
            down_phase(nc, t, l, g_dram, h_dram, xT, mod(l, G_F))

        with Room(nc, "final") as fr:
            y = fr.sb("y", [P, KD, SEQ])
            norm_phase(nc, "nout", xT, SEQ, small[:, ROW_OUT:ROW_OUT + KD], None, None, None, None, ones, eps, plain=y)
            s_o = fr.sem("out")
            block = fr.block()

            @block.sync
            def _(sp):
                sp.dma_start(out, y[:, :, :]).then_inc(s_o, 16)
                sp.wait_ge(s_o, 16)


def tiles_of(w):
    k, n = w.shape
    return w.reshape(k // P, P, n // P, P).transpose(2, 1, 0, 3)


def channels_first(x):
    return x.reshape(x.shape[0], KD, P).transpose(2, 1, 0)


def constants():
    half = HEAD_DIM // 2
    inv = np.float32(THETA) ** (-np.arange(0, half, 2, dtype=np.float32) / half)
    tok = np.arange(SEQ)
    row = (tok // GRID_W).astype(np.float32)[:, None] * inv
    col = (tok % GRID_W).astype(np.float32)[:, None] * inv
    cos, sin, swap = np.zeros((P, SEQ)), np.zeros((P, SEQ)), np.zeros((P, P))
    for p in range(P):
        d = p % HEAD_DIM
        ang = (row if d < half else col)[:, d % (half // 2)]
        low = d % half < half // 2
        cos[p] = np.cos(ang)
        sin[p] = -np.sin(ang) if low else np.sin(ang)
        swap[p + (half // 2 if low else -(half // 2)), p] = 1
    i, j = np.arange(P)[:, None], np.arange(P)[None, :]
    mask = np.stack([np.where(j >= i, 0, NEG), np.where(j <= i, 0, NEG)], 1)

    def dft(n):
        a = 2 * np.pi * (np.outer(np.arange(n), np.arange(n)) % n) / n
        return np.cos(a) / np.sqrt(n), np.sin(a) / np.sqrt(n)

    cc, sc = dft(P)
    cn, sn = dft(SEQ)
    blocks = lambda a: a.reshape(NB, P, SEQ).transpose(1, 0, 2)
    out = {
        "identity": np.eye(P), "rope_cos": cos, "rope_sin": sin, "swap": swap, "band_mask": mask,
        "dft_chan": np.concatenate([cc, sc], 1), "dft_cos": blocks(cn), "dft_msin": blocks(-sn),
        "iota16": np.tile(np.arange(TOPK), (P, 1)),
    }
    out = {k: np.ascontiguousarray(v, dtype=np.float32) for k, v in out.items()}
    out["iota_b"] = np.broadcast_to(np.arange(NKEYS)[None, :, None], (P, NKEYS, TG)).astype(mybir.dt.np(BF16))
    return out


def kernel(**inputs):
    import concourse.bacc as bacc
    from concourse.bass_utils import run_bass_kernel_spmd

    a = {k: np.asarray(v) for k, v in inputs.items()}
    w_in = a["ab_w_in"][0]
    wq = w_in[:, :HEADS * HEAD_DIM].reshape(D, KV_HEADS, Q_PER_KV, HEAD_DIM).transpose(0, 2, 1, 3).reshape(D, -1)
    w_in = np.concatenate([wq, w_in[:, HEADS * HEAD_DIM:]], 1)
    w_out = a["ab_w_out"][0]
    wa = w_out[:HEADS * HEAD_DIM].reshape(KV_HEADS, Q_PER_KV, HEAD_DIM, D).transpose(1, 0, 2, 3).reshape(-1, D)
    w_out = np.concatenate([wa, w_out[HEADS * HEAD_DIM:]], 0)
    rows = [a["c"][0], a["c_ctx"], a["norm_mix_w"].reshape(-1), a["norm_ffn_w"].reshape(-1), a["norm_out_w"],
            a["gs_norm_w"][0]]
    arrays = {
        "xT": channels_first(a["x"][0]), "ctxT": channels_first(a["ctx"][0]),
        "small_rows": np.concatenate(rows).reshape(SMALL_ROWS, P),
        "ada_b_rows": a["ada_b"].reshape(DEPTH * ADA_ROWS, P),
        "ada_tiles": a["ada_w"].reshape(DEPTH, KD, P, N_MOD, D).transpose(0, 3, 2, 1, 4).reshape(-1, P, KD, D),
        "w_in": tiles_of(w_in), "w_ab_out": tiles_of(w_out),
        "w_gs_in": tiles_of(a["gs_w_in"][0]), "w_gs_out": tiles_of(a["gs_w_out"][0]),
        "w_peer_q": np.stack([tiles_of(w) for w in a["peer_w_q"]]),
        "attn_sink": a["attn_sink"][0], "gs_b_s": a["gs_b_s"][0].reshape(-1),
        "sgu_wT": a["gs_w_s"][0].transpose(2, 0, 1),
        "keysT": a["peer_keys"].reshape(DEPTH, HS, NKEYS, P).transpose(0, 3, 1, 2),
        "uT": a["peer_u"].reshape(DEPTH, NKEYS, NKEYS, KD, P).transpose(0, 1, 4, 3, 2),
        "peer_v": a["peer_v"].reshape(DEPTH, NKEYS, NKEYS, D),
    }
    arrays.update(constants())
    arrays = {k: np.ascontiguousarray(v) for k, v in arrays.items()}
    nc = bacc.Bacc("TRN2", target_bir_lowering=False, num_devices=1)
    t = {k: nc.dram_tensor(f"in_{k}", v.shape, mybir.dt.from_np(v.dtype), kind="ExternalInput").ap()
         for k, v in arrays.items()}
    out = nc.dram_tensor("out_T", (P, KD, SEQ), F32, kind="ExternalOutput").ap()
    program(nc, t, out)
    r = run_bass_kernel_spmd(nc, [{f"in_{k}": v for k, v in arrays.items()}], core_ids=[0])
    got = r.results[0]["out_T"]
    return np.ascontiguousarray(got.transpose(2, 1, 0)).reshape(1, SEQ, D)
```

```python
from contextlib import ExitStack

import numpy as np

import concourse.bass as bass
from concourse import mybir

F32 = mybir.dt.float32
F32R = mybir.dt.float32r
BF16 = mybir.dt.bfloat16
U32 = mybir.dt.uint32
ALU = mybir.AluOpType
ACT = mybir.ActivationFunctionType
AX = mybir.AxisListType

P = 128
D = 1024
KD = D // P
SEQ = 512
NB = SEQ // P
CTX = 256
NCB = CTX // P
DEPTH = 2
N_MOD = 6
HEADS, KV_HEADS, HEAD_DIM = 8, 2, 64
Q_PER_KV = HEADS // KV_HEADS
SCALE = HEAD_DIM ** -0.5
GRID_W = 64
THETA = 10000.0
FG = 4
SGU_G = 8
PH, NKEYS, TOPK = 8, 128, 16
HS = 2 * PH
HK = PH * TOPK
TG = 8
EPS = 1e-6
NEG = -1e30
KEYS = 3 * P + CTX
SH_M, SC_M, G_M, SH_F, SC_F, G_F = range(N_MOD)
ROW_C, ROW_CCTX, ROW_MIX, ROW_FFN, ROW_OUT, ROW_SGU = 0, 8, 16, 32, 48, 56
SMALL_ROWS = 64
ADA_ROWS = N_MOD * KD


class Room:

    def __init__(self, nc, tag):
        self.nc, self.tag, self.stack, self.sems = nc, tag, ExitStack(), []

    def __enter__(self):
        self.stack.__enter__()
        return self

    def __exit__(self, *a):
        said = self.stack.__exit__(*a)
        if self.sems:
            self.nc.clear_and_free_semaphores(self.sems)
            self.nc.all_engine_barrier()
        return said

    def sb(self, name, shape, dt=F32):
        return self.stack.enter_context(self.nc.sbuf_tensor(f"{self.tag}_{name}", shape, dt))

    def ps(self, name, shape, dt=F32):
        return self.stack.enter_context(self.nc.psum_tensor(f"{self.tag}_{name}", shape, dt))

    def sem(self, name):
        self.sems.append(self.nc.alloc_semaphore(f"{self.tag}_{name}"))
        return self.sems[-1]

    def block(self):
        return self.stack.enter_context(self.nc.Block())


def preload(r, sp, ring, w):
    s = r.sem("ahead")
    for j in range(2):
        sp.dma_start(ring[j][:, :, :], w[j]).then_inc(s, 16)
    sp.wait_ge(s, 32)


def f32(ap):
    return ap.bitcast(F32)


def three_passes(nc, out, w_hi, w_lo, x_hi, x_lo, first, last):
    nc.tensor.matmul(out, w_hi, x_hi, start=first, stop=False)
    nc.tensor.matmul(out, w_hi, x_lo, start=False, stop=False)
    return nc.tensor.matmul(out, w_lo, x_hi, start=False, stop=last)


def load_phase(nc, t, xT, small, ada, ident, also):
    with Room(nc, "ada") as r:
        Q = 4
        QK = KD // Q
        PAIR = P // 2
        rows_a = r.sb("rows_a", [SMALL_ROWS, P])
        rows_b = r.sb("rows_b", [DEPTH * ADA_ROWS, P])
        bias = r.sb("bias", [P, DEPTH * ADA_ROWS])
        cond = r.sb("cond", [P, KD, 2])
        wide = r.sb("wide", [P, KD, P])
        c_hi = r.sb("c_hi", [P, KD, P], F32R)
        c_lo = r.sb("c_lo", [P, KD, P], F32R)
        raw = [r.sb(f"raw{j}", [P, QK, D]) for j in range(Q)]
        w_hi = [r.sb(f"w_hi{j}", [P, QK, D], F32R) for j in range(Q)]
        w_lo = [r.sb(f"w_lo{j}", [P, QK, D], F32R) for j in range(Q)]
        flat = r.sb("flat", [P, D])
        turned = r.ps("turned", [P, 512])
        out = [[r.ps(f"out{u}{j}", [P, 512]) for j in range(2)] for u in range(2)]
        cols = r.ps("cols", [P, 512])
        s_rows, s_x, s_turn, s_col, s_cond, s_wide, s_chi, s_clo = (
            r.sem(n) for n in ("rows", "x", "turn", "col", "cond", "wide", "chi", "clo"))
        s_in = [r.sem(f"strip_in{j}") for j in range(Q)]
        s_hi, s_lo, s_mm, s_flat, s_cols, s_out = (
            r.sem(n) for n in ("hi", "lo", "multiplied", "flat", "cols", "taken"))
        block = r.block()
        VECTORS = DEPTH * N_MOD

        def strip(v, j):
            return t["ada_tiles"][bass.ds(v, 1), :, j * QK:(j + 1) * QK, :].rearrange("o p k n -> (o p) k n")

        def walk(engine, body):
            body(0, 0)
            body(1, 1)
            with engine.Fori(1, VECTORS // 2) as it:
                for u in range(2):
                    body(it * 2 + u, u)

        @block.sync
        def _(sp):
            sp.dma_start(rows_a[:, :], t["small_rows"]).then_inc(s_rows, 16)
            sp.dma_start(rows_b[:, :], t["ada_b_rows"]).then_inc(s_rows, 16)
            sp.dma_start(ident[:, :], t["identity"]).then_inc(s_rows, 16)
            for j in range(Q):
                sp.dma_start(raw[j][:, :, :], strip(0, j)).then_inc(s_in[j], 16)
            sp.dma_start(xT[:, :, :], t["xT"]).then_inc(s_x, 16)
            with sp.Fori(1, VECTORS) as it:
                for j in range(Q):
                    sp.wait_ge(s_lo, it * Q + (j + 1 - Q))
                    sp.dma_start(raw[j][:, :, :], strip(it, j)).then_inc(s_in[j], 16)
            for to, source in also:
                sp.dma_start(to, source).then_inc(s_x, 16)
            sp.wait_ge(s_x, 16 * (1 + len(also)))

        @block.tensor
        def _(pe):
            pe.wait_ge(s_rows, 48)
            nc.tensor.transpose(turned[:, 0:SMALL_ROWS], rows_a[:, :], ident[0:SMALL_ROWS, 0:SMALL_ROWS])
            nc.tensor.transpose(turned[:, P:P + 96], rows_b[:, :], ident[0:96, 0:96]).then_inc(s_turn, 1)
            pe.wait_ge(s_clo, 1)
            pe.sem_inc(s_mm, Q)
            pe.sem_inc(s_cols, 1)

            def columns(v):
                pe.wait_ge(s_flat, v + 3)
                pe.wait_ge(s_out, v + 1)
                for m in range(KD):
                    mm = nc.tensor.matmul(cols[:, 2 * m:2 * m + 2], flat[:, m * P:(m + 1) * P],
                                          ident[:, 0:P:PAIR], start=True, stop=True)
                mm.then_inc(s_cols, 1)

            def vector(v, u):
                pe.wait_ge(s_flat, v + 1)
                for j in range(Q):
                    pe.wait_ge(s_lo, v * Q + (j + 1))
                    for half in range(2):
                        cut = slice(half * 512, (half + 1) * 512)
                        for i in range(QK):
                            k = j * QK + i
                            mm = three_passes(nc, out[u][half][:, :], c_hi[:, k, :], c_lo[:, k, :],
                                              w_hi[j][:, i, cut], w_lo[j][:, i, cut], k == 0, k == KD - 1)
                    mm.then_inc(s_mm, 1)
                    if j == 1 and (u == 1 or not isinstance(v, int)):
                        columns(v - 1)

            walk(pe, vector)
            columns(VECTORS - 1)

        @block.scalar
        def _(act):
            act.wait_ge(s_col, 2)
            act.activation(cond[:, :, 0], small[:, ROW_C:ROW_C + KD], ACT.Silu).then_inc(s_cond, 1)
            act.activation(cond[:, :, 1], small[:, ROW_CCTX:ROW_CCTX + KD], ACT.Silu).then_inc(s_cond, 1)
            act.wait_ge(s_wide, 2)
            act.activation(c_hi[:, :, :], wide[:, :, :], ACT.Copy).then_inc(s_chi, 1)
            act.sem_inc(s_flat, 2)

            def split_hi(v, j):
                act.wait_ge(s_in[j], v * 16 + 16)
                act.wait_ge(s_mm, v * Q + (j + 1))
                act.activation(w_hi[j][:, :, :], raw[j][:, :, :], ACT.Copy).then_inc(s_hi, 1)

            def take(v, u):
                act.wait_ge(s_mm, v * Q + 2 * Q)
                act.wait_ge(s_cols, v + 1)
                act.activation(flat[:, 0:512], out[u][0][:, :], ACT.Copy)
                act.activation(flat[:, 512:D], out[u][1][:, :], ACT.Copy).then_inc(s_flat, 1)

            def vector(v, u):
                for j in range(Q - 1):
                    split_hi(v, j)
                if u == 1 or not isinstance(v, int):
                    take(v - 1, 1 - u)
                split_hi(v, Q - 1)

            walk(act, vector)
            take(VECTORS - 1, 1)

        @block.vector
        def _(dve):
            dve.sem_inc(s_out, 1)
            dve.wait_ge(s_turn, 1)
            nc.vector.tensor_copy(small[:, :], turned[:, 0:SMALL_ROWS]).then_inc(s_col, 1)
            nc.vector.tensor_copy(bias[:, :], turned[:, P:P + 96]).then_inc(s_col, 1)
            dve.wait_ge(s_cond, 2)
            for c in range(2):
                nc.vector.tensor_copy(wide[:, :, c * PAIR:(c + 1) * PAIR],
                                      cond[:, :, c:c + 1].broadcast_to([P, KD, PAIR])).then_inc(s_wide, 1)
            dve.wait_ge(s_chi, 1)
            nc.vector.tensor_tensor(c_lo[:, :, :], wide[:, :, :], f32(c_hi[:, :, :]), ALU.subtract).then_inc(s_clo, 1)

            def split_lo(v, j):
                dve.wait_ge(s_hi, v * Q + (j + 1))
                nc.vector.tensor_tensor(w_lo[j][:, :, :], raw[j][:, :, :], f32(w_hi[j][:, :, :]),
                                        ALU.subtract).then_inc(s_lo, 1)

            def take(v):
                dve.wait_ge(s_cols, v + 2)
                at = bass.ds(v * KD, KD)
                got = cols[:, 0:2 * KD].rearrange("p (m c) -> p c m", c=2)
                nc.vector.tensor_tensor(ada[:, 0, at], got[:, 0, :], bias[:, at], ALU.add)
                nc.vector.tensor_tensor(ada[:, 1, at], got[:, 1, :], bias[:, at], ALU.add).then_inc(s_out, 1)

            def low_halves(v):
                for j in range(Q):
                    split_lo(v, j)
                    if j == 1 and not (isinstance(v, int) and v < 2):
                        take(v - 2)

            walk(dve, lambda v, u: low_halves(v))
            take(VECTORS - 2)
            take(VECTORS - 1)


def norm_phase(nc, tag, src, n, weight, shift, scale, hi, lo, ones, eps, plain=None, ring=None, next_w=None):
    with Room(nc, tag) as r:
        square = r.sb("square", [P, KD, n])
        rstd = r.sb("rstd", [P, n])
        gain = r.sb("gain", [P, KD])
        S = 4
        normed = [r.sb(f"normed{j}", [P, n]) for j in range(S)]
        modded = [r.sb(f"modded{j}", [P, n]) for j in range(S)]
        total = r.ps("total", [P, 512])
        s_sq, s_pair, s_sum, s_std, s_rstd, s_gain, s_n, s_m, s_hi, s_lo = (
            r.sem(x) for x in ("sq", "pair", "sum", "std", "rstd", "gain", "normed", "modded", "hi", "lo"))
        block = r.block()

        if next_w is not None:
            @block.sync
            def _(sp):
                preload(r, sp, ring, next_w)

        @block.tensor
        def _(pe):
            for i in range(KD // 2):
                pe.wait_ge(s_pair, i + 1)
                mm = nc.tensor.matmul(total[:, 0:n], ones[:, :], square[:, 2 * i, :],
                                      start=(i == 0), stop=(i == KD // 2 - 1))
            mm.then_inc(s_sum, 1)

        @block.scalar
        def _(act):
            for k in range(KD):
                act.activation(square[:, k, :], src[:, k, :], ACT.Square).then_inc(s_sq, 1)
            act.wait_ge(s_sum, 1)
            act.activation(rstd[:, :], total[:, 0:n], ACT.Sqrt, bias=eps[:, 0:1], scale=1.0 / D).then_inc(s_std, 1)
            if plain is not None:
                return
            act.wait_ge(s_gain, 2)
            for k in range(KD + 1):
                if k < KD:
                    act.wait_ge(s_n, k + 1)
                    if k >= S:
                        act.wait_ge(s_lo, k - S + 1)
                    act.activation(modded[k % S][:, :], normed[k % S][:, :], ACT.Identity,
                                   bias=shift[:, k:k + 1], scale=gain[:, k:k + 1]).then_inc(s_m, 1)
                if k >= 1:
                    act.wait_ge(s_m, k)
                    act.activation(hi[:, k - 1, :], modded[(k - 1) % S][:, :], ACT.Copy).then_inc(s_hi, 1)

        @block.vector
        def _(dve):
            for i in range(KD // 2):
                dve.wait_ge(s_sq, 2 * i + 2)
                nc.vector.tensor_tensor(square[:, 2 * i, :], square[:, 2 * i, :], square[:, 2 * i + 1, :],
                                        ALU.add).then_inc(s_pair, 1)
            if plain is None:
                nc.vector.tensor_scalar(gain[:, :], scale, 1.0, None, ALU.add).then_inc(s_gain, 1)
                dve.wait_ge(s_gain, 1)
                nc.vector.tensor_tensor(gain[:, :], gain[:, :], weight, ALU.mult).then_inc(s_gain, 1)
            dve.wait_ge(s_std, 1)
            nc.vector.reciprocal(rstd[:, :], rstd[:, :]).then_inc(s_rstd, 1)
            dve.wait_ge(s_rstd, 1)
            if plain is not None:
                for k in range(KD):
                    nc.vector.scalar_tensor_tensor(out=plain[:, k, :], in0=src[:, k, :], scalar=weight[:, k:k + 1],
                                                   in1=rstd[:, :], op0=ALU.mult, op1=ALU.mult).then_inc(s_n, 1)
                return
            for k in range(KD + 2):
                if k < KD:
                    if k >= S:
                        dve.wait_ge(s_m, k - S + 1)
                    nc.vector.tensor_tensor(normed[k % S][:, :], src[:, k, :], rstd[:, :], ALU.mult).then_inc(s_n, 1)
                if k >= 2:
                    dve.wait_ge(s_hi, k - 1)
                    nc.vector.tensor_tensor(lo[:, k - 2, :], modded[(k - 2) % S][:, :], f32(hi[:, k - 2, :]),
                                            ALU.subtract).then_inc(s_lo, 1)


def gemm_phase(nc, tag, ring, w, tiles, hi, lo, n, take_act=None, take_dve=None, also=()):
    with Room(nc, tag) as r:
        raw = ring
        w_hi = [r.sb(f"w_hi{j}", [P, KD, P], F32R) for j in range(2)]
        w_lo = [r.sb(f"w_lo{j}", [P, KD, P], F32R) for j in range(2)]
        out = [r.ps(f"out{j}", [P, 512]) for j in range(2)]
        s_in = [r.sem(f"in{j}") for j in range(2)]
        s_hi, s_lo, s_mm, s_out = (r.sem(x) for x in ("hi", "lo", "multiplied", "taken"))
        block = r.block()

        @block.sync
        def _(sp):
            for j in range(2):
                sp.sem_inc(s_in[j], 16)
            s_also = r.sem("also")
            for to, source in also:
                sp.dma_start(to, source).then_inc(s_also, 16)
            if tiles > 2:
                with sp.Fori(1, tiles // 2) as it:
                    for j in range(2):
                        sp.wait_ge(s_lo, it * 2 + j - 1)
                        sp.dma_start(raw[j][:, :, :], w[bass.ds(it * 2 + j, 1)].rearrange("o p k n -> (o p) k n")
                                     ).then_inc(s_in[j], 16)
            if also:
                sp.wait_ge(s_also, 16 * len(also))

        def take(engine, body, q, j):
            t = q * 2 + j
            engine.wait_ge(s_mm, t + 3)
            body(t, out[j][:, 0:n]).then_inc(s_out, 1)

        def split_hi(q, j):
            nc.scalar.wait_ge(s_in[j], q * 16 + 16)
            nc.scalar.wait_ge(s_mm, q * 2 + j + 1)
            nc.scalar.activation(w_hi[j][:, :, :], raw[j][:, :, :], ACT.Copy).then_inc(s_hi, 1)

        def split_lo(q, j):
            nc.vector.wait_ge(s_hi, q * 2 + j + 1)
            nc.vector.tensor_tensor(w_lo[j][:, :, :], raw[j][:, :, :], f32(w_hi[j][:, :, :]),
                                    ALU.subtract).then_inc(s_lo, 1)

        def walk(engine, split, body):
            if body:
                engine.sem_inc(s_out, 2)
            split(0, 0)
            if tiles > 2:
                with engine.Fori(0, tiles // 2 - 1) as it:
                    split(it, 1)
                    if body:
                        take(engine, body, it, 0)
                    split(it + 1, 0)
                    if body:
                        take(engine, body, it, 1)
            split(tiles // 2 - 1, 1)
            if body:
                take(engine, body, tiles // 2 - 1, 0)
                take(engine, body, tiles // 2 - 1, 1)

        @block.scalar
        def _(act):
            walk(act, split_hi, take_act)

        @block.vector
        def _(dve):
            walk(dve, split_lo, take_dve)

        @block.tensor
        def _(pe):
            pe.sem_inc(s_mm, 2)
            with pe.Fori(0, tiles // 2) as it:
                for j in range(2):
                    t = it * 2 + j
                    pe.wait_ge(s_lo, t + 1)
                    pe.wait_ge(s_out, t + 1)
                    for k in range(KD):
                        mm = three_passes(nc, out[j][:, 0:n], w_hi[j][:, k, :], w_lo[j][:, k, :],
                                          hi[:, k, :], lo[:, k, :], k == 0, k == KD - 1)
                    mm.then_inc(s_mm, 1)


def residual(nc, xT, gate):
    def take(t, ps):
        x = xT[:, bass.ds(t, 1), :].rearrange("p o n -> p (o n)")
        return nc.vector.scalar_tensor_tensor(out=x, in0=ps, scalar=gate[:, bass.ds(t, 1)], in1=x,
                                              op0=ALU.mult, op1=ALU.add)
    return take


def rope_phase(nc, qkT, swap, cos, sin):
    with Room(nc, "rope") as r:
        turned = [r.sb(f"turned{j}", [P, SEQ]) for j in range(2)]
        ps = [r.ps(f"ps{j}", [P, 512]) for j in range(2)]
        s_mm, s_sin, s_cos, s_add = (r.sem(x) for x in ("swapped", "sin", "cos", "added"))
        block = r.block()

        @block.tensor
        def _(pe):
            for m in range(5):
                if m >= 2:
                    pe.wait_ge(s_sin, m - 1)
                nc.tensor.matmul(ps[m % 2][:, :], swap[:, :], qkT[:, m, 0:SEQ], start=True, stop=True).then_inc(s_mm, 1)

        @block.vector
        def _(dve):
            for m in range(5):
                dve.wait_ge(s_mm, m + 1)
                if m >= 2:
                    dve.wait_ge(s_add, m - 1)
                nc.vector.tensor_tensor(turned[m % 2][:, :], ps[m % 2][:, :], sin[:, :], ALU.mult).then_inc(s_sin, 1)
                nc.vector.tensor_tensor(qkT[:, m, 0:SEQ], qkT[:, m, 0:SEQ], cos[:, :], ALU.mult).then_inc(s_cos, 1)
                dve.wait_ge(s_sin, m + 1)
                dve.wait_ge(s_cos, m + 1)
                nc.vector.tensor_tensor(qkT[:, m, 0:SEQ], qkT[:, m, 0:SEQ], turned[m % 2][:, :],
                                        ALU.add).then_inc(s_add, 1)


def attention_phase(nc, t, qkT, kcT, vT, vcT, ident, hi, lo, tables):
    with Room(nc, "attn") as r:
        mask = r.sb("mask", [P, 2, P])
        sink = r.sb("sink", [P, HEADS])
        v = r.sb("v", [P, NB + NCB, P])
        s_sb = [r.sb(f"scores{j}", [P, KEYS]) for j in range(2)]
        prob = [r.sb(f"prob{j}", [P, KEYS]) for j in range(2)]
        pT = [r.sb(f"probT{j}", [P, KEYS // P, Q_PER_KV, P]) for j in range(2)]
        stat = r.sb("stat", [P, 2, 8])
        ps_s = [r.ps(f"ps_s{j}", [P, 2, 512]) for j in range(2)]
        ps_t = r.ps("ps_t", [P, 2, 512])
        ps_o = r.ps("ps_o", [P, 512])
        names = ("in", "vt", "v", "s", "sc", "ctx", "mx", "nm", "exp", "den", "rec", "norm", "tr", "pt", "pv",
                 "ohi", "olo", "dft")
        q = {x: r.sem(x) for x in names}
        block = r.block()
        units = [(n, g, j) for n in range(NB) for g in range(KV_HEADS) for j in range(Q_PER_KV)]

        def spans(n):
            return [(b, {n - 1: 0, n: None, n + 1: 1}[b]) for b in (n - 1, n, n + 1) if 0 <= b < NB]

        @block.sync
        def _(sp):
            sp.dma_start(mask[:, :, :], t["band_mask"]).then_inc(q["in"], 16)
            sp.dma_start(sink[:, :], t["attn_sink"].partition_broadcast(P)).then_inc(q["in"], 16)
            chan, seq_c, seq_s = tables
            sp.dma_start(chan[:, :], t["dft_chan"]).then_inc(q["dft"], 16)
            sp.dma_start(seq_c[:, :, :], t["dft_cos"]).then_inc(q["dft"], 16)
            sp.dma_start(seq_s[:, :, :], t["dft_msin"]).then_inc(q["dft"], 16)
            sp.wait_ge(q["dft"], 48)

        @block.tensor
        def _(pe):
            for b in range(NB + NCB):
                src = vT[:, b * P:(b + 1) * P] if b < NB else vcT[:, (b - NB) * P:(b - NB + 1) * P]
                mm = nc.tensor.transpose(ps_t[:, b // 4, (b % 4) * P:(b % 4 + 1) * P], src, ident[:, :])
            mm.then_inc(q["vt"], 1)

            def scores(u):
                n, g, j = units[u]
                if u >= 2:
                    pe.wait_ge(q["sc"], u - 1)
                    pe.wait_ge(q["ctx"], u - 1)
                h = slice(g * 64, g * 64 + 64)
                lhs = qkT[h, j, n * P:(n + 1) * P]
                first, width = spans(n)[0][0], len(spans(n)) * P
                nc.tensor.matmul(ps_s[u % 2][:, 0, 0:width], lhs, qkT[h, 4, first * P:first * P + width],
                                 start=True, stop=True)
                nc.tensor.matmul(ps_s[u % 2][:, 1, 0:CTX], lhs, kcT[h, :], start=True, stop=True).then_inc(q["s"], 1)

            def turn(u):
                n, g, j = units[u]
                pe.wait_ge(q["norm"], u + 1)
                if u == 0:
                    pe.wait_ge(q["v"], 1)
                else:
                    pe.wait_ge(q["pt"], u)
                blocks = len(spans(n)) + NCB
                for b in range(blocks):
                    mm = nc.tensor.transpose(ps_t[:, b // 4, (b % 4) * P:(b % 4 + 1) * P],
                                             prob[u % 2][:, b * P:(b + 1) * P], ident[:, :])
                mm.then_inc(q["tr"], 1)

            def values(u):
                n, g, _ = units[u]
                pe.wait_ge(q["pt"], u + 1)
                w = u // Q_PER_KV
                if w >= 1:
                    pe.wait_ge(q["olo"], w)
                blocks = [b for b, _ in spans(n)] + [NB + c for c in range(NCB)]
                for i, b in enumerate(blocks):
                    mm = nc.tensor.matmul(ps_o[g * 64:g * 64 + 64, :], v[:, b, g * 64:g * 64 + 64],
                                          pT[w % 2][:, i, :, :].rearrange("p j n -> p (j n)"),
                                          start=(i == 0), stop=(i == len(blocks) - 1))
                mm.then_inc(q["pv"], 1)

            scores(0)
            scores(1)
            for u in range(len(units)):
                if u + 2 < len(units):
                    scores(u + 2)
                turn(u)
                if u >= Q_PER_KV and u % Q_PER_KV == 0:
                    values(u - 1)
            values(len(units) - 1)

        def evacuate(act, u):
            n, g, j = units[u]
            w = u // Q_PER_KV
            act.wait_ge(q["tr"], u + 1)
            if j == 0 and w >= 2:
                act.wait_ge(q["pv"], w - 1)
            blocks = len(spans(n)) + NCB
            for b0, b1 in ((0, 4), (4, blocks)):
                if b1 > b0:
                    last = act.activation(pT[w % 2][:, b0:b1, j, :],
                                          ps_t[:, b0 // 4, 0:(b1 - b0) * P].rearrange("p (b n) -> p b n", n=P), ACT.Copy)
            last.then_inc(q["pt"], 1)

        def high_half(act, w):
            n, g, _ = units[w * Q_PER_KV]
            act.wait_ge(q["pv"], w + 1)
            hs = slice(g * 64, g * 64 + 64)
            act.activation(hi[hs, 0:Q_PER_KV, n * P:(n + 1) * P],
                           ps_o[hs, :].rearrange("p (j n) -> p j n", n=P), ACT.Copy).then_inc(q["ohi"], 1)

        @block.scalar
        def _(act):
            def context(u):
                c = len(spans(units[u][0])) * P
                act.wait_ge(q["s"], u + 1)
                if u >= 2:
                    act.wait_ge(q["exp"], 2 * (u - 1))
                act.activation(s_sb[u % 2][:, c:c + CTX], ps_s[u % 2][:, 1, 0:CTX], ACT.Copy).then_inc(q["ctx"], 1)

            def exponentials(u):
                n, g, j = units[u]
                c = len(spans(n)) * P
                act.wait_ge(q["nm"], u + 1)
                if u >= 2:
                    act.wait_ge(q["tr"], u - 1)
                st = stat[:, u % 2, :]
                h = g * Q_PER_KV + j
                act.activation(prob[u % 2][:, 0:c + CTX], s_sb[u % 2][:, 0:c + CTX], ACT.Exp, bias=st[:, 1:2],
                               scale=SCALE, accum_out=st[:, 2:3]).then_inc(q["exp"], 1)
                act.activation(st[:, 3:4], sink[:, h:h + 1], ACT.Exp, bias=st[:, 1:2]).then_inc(q["exp"], 1)

            context(0)
            for u in range(len(units)):
                if u + 1 < len(units):
                    context(u + 1)
                exponentials(u)
                if u >= 1:
                    evacuate(act, u - 1)
                if u > Q_PER_KV and u % Q_PER_KV == 1:
                    high_half(act, u // Q_PER_KV - 1)
            evacuate(act, len(units) - 1)
            high_half(act, len(units) // Q_PER_KV - 1)

        @block.vector
        def _(dve):
            dve.wait_ge(q["vt"], 1)
            nc.vector.tensor_copy(v[:, 0:4, :], ps_t[:, 0, :].rearrange("p (b n) -> p b n", n=P))
            nc.vector.tensor_copy(v[:, 4:6, :], ps_t[:, 1, 0:2 * P].rearrange("p (b n) -> p b n", n=P)).then_inc(q["v"], 1)
            dve.wait_ge(q["in"], 32)
            done = [0]

            def low_half(w):
                n, g, _ = units[w * Q_PER_KV]
                dve.wait_ge(q["ohi"], w + 1)
                hs = slice(g * 64, g * 64 + 64)
                nc.vector.tensor_tensor(lo[hs, 0:Q_PER_KV, n * P:(n + 1) * P],
                                        ps_o[hs, :].rearrange("p (j n) -> p j n", n=P),
                                        f32(hi[hs, 0:Q_PER_KV, n * P:(n + 1) * P]), ALU.subtract).then_inc(q["olo"], 1)

            def front(u):
                n, g, j = units[u]
                st = stat[:, u % 2, :]
                c = len(spans(n)) * P
                h = g * Q_PER_KV + j
                dve.wait_ge(q["s"], u + 1)
                if u >= 2:
                    dve.wait_ge(q["exp"], 2 * (u - 1))
                for i, (b, side) in enumerate(spans(n)):
                    part = slice(i * P, (i + 1) * P)
                    if side is None:
                        last = nc.vector.tensor_copy(s_sb[u % 2][:, part], ps_s[u % 2][:, 0, part])
                    else:
                        last = nc.vector.tensor_tensor(s_sb[u % 2][:, part], ps_s[u % 2][:, 0, part], mask[:, side, :],
                                                       ALU.add)
                    last.then_inc(q["mx"], 1)
                    done[0] += 1
                dve.wait_ge(q["mx"], done[0])
                dve.sem_inc(q["sc"], 1)
                dve.wait_ge(q["ctx"], u + 1)
                nc.vector.reduce_max(st[:, 0:1], s_sb[u % 2][:, 0:c + CTX], AX.X).then_inc(q["mx"], 1)
                done[0] += 1
                dve.wait_ge(q["mx"], done[0])
                nc.vector.tensor_scalar(st[:, 4:5], st[:, 0:1], SCALE, sink[:, h:h + 1], ALU.mult, ALU.max).then_inc(q["mx"], 1)
                done[0] += 1
                dve.wait_ge(q["mx"], done[0])
                nc.vector.tensor_scalar(st[:, 1:2], st[:, 4:5], -1.0, None, ALU.mult).then_inc(q["nm"], 1)

            def back(u):
                n, g, j = units[u]
                st = stat[:, u % 2, :]
                c = len(spans(n)) * P
                dve.wait_ge(q["exp"], 2 * (u + 1))
                nc.vector.tensor_tensor(st[:, 5:6], st[:, 2:3], st[:, 3:4], ALU.add).then_inc(q["den"], 1)
                dve.wait_ge(q["den"], u + 1)
                nc.vector.reciprocal(st[:, 6:7], st[:, 5:6]).then_inc(q["rec"], 1)
                dve.wait_ge(q["rec"], u + 1)
                nc.vector.tensor_scalar(prob[u % 2][:, 0:c + CTX], prob[u % 2][:, 0:c + CTX], st[:, 6:7], None,
                                        ALU.mult).then_inc(q["norm"], 1)

            front(0)
            for u in range(len(units)):
                if u + 1 < len(units):
                    front(u + 1)
                back(u)
                if u >= Q_PER_KV and u % Q_PER_KV == 2:
                    low_half(u // Q_PER_KV - 1)
            low_half(len(units) // Q_PER_KV - 1)


def fourier_phase(nc, t, fT, tables, hi, lo, ring):
    with Room(nc, "fft") as r:
        chan, seq_c, seq_s = tables
        mid = [r.sb(f"mid{j}", [P, NB, 2 * P]) for j in range(2)]
        ps_a = [r.ps(f"ps_a{j}", [P, 2, 512]) for j in range(2)]
        ps_y = [r.ps(f"ps_y{j}", [P, 512]) for j in range(2)]
        s_a, s_mid, s_y, s_hi, s_lo = (r.sem(x) for x in ("a", "mid", "y", "hi", "lo"))
        block = r.block()

        @block.sync
        def _(sp):
            preload(r, sp, ring, t["w_ab_out"])

        @block.tensor
        def _(pe):
            def first(g):
                if g >= 2:
                    pe.wait_ge(s_mid, g - 1)
                for b in range(NB):
                    mm = nc.tensor.matmul(ps_a[g % 2][:, b // 2, (b % 2) * 256:(b % 2 + 1) * 256],
                                          fT[:, g, b * P:(b + 1) * P], chan[:, :], start=True, stop=True)
                mm.then_inc(s_a, 1)

            first(0)
            for g in range(FG):
                if g + 1 < FG:
                    first(g + 1)
                pe.wait_ge(s_mid, g + 1)
                if g >= 2:
                    pe.wait_ge(s_lo, g - 1)
                for b in range(NB):
                    nc.tensor.matmul(ps_y[g % 2][:, :], mid[g % 2][:, b, 0:P], seq_c[:, b, :], start=(b == 0), stop=False)
                    mm = nc.tensor.matmul(ps_y[g % 2][:, :], mid[g % 2][:, b, P:2 * P], seq_s[:, b, :],
                                          start=False, stop=(b == NB - 1))
                mm.then_inc(s_y, 1)

        @block.scalar
        def _(act):
            for g in range(FG):
                act.wait_ge(s_y, g + 1)
                act.activation(hi[:, 4 + g, :], ps_y[g % 2][:, :], ACT.Copy).then_inc(s_hi, 1)

        @block.vector
        def _(dve):
            def low(g):
                dve.wait_ge(s_hi, g + 1)
                nc.vector.tensor_tensor(lo[:, 4 + g, :], ps_y[g % 2][:, :], f32(hi[:, 4 + g, :]),
                                        ALU.subtract).then_inc(s_lo, 1)

            for g in range(FG):
                dve.wait_ge(s_a, g + 1)
                if g >= 2:
                    dve.wait_ge(s_y, g - 1)
                nc.vector.tensor_copy(mid[g % 2][:, :, :],
                                      ps_a[g % 2][:, :, :].rearrange("p a (b n) -> p (a b) n", n=256)).then_inc(s_mid, 1)
                if g >= 1:
                    low(g - 1)
            low(FG - 1)


def sgu_phase(nc, t, zT, small, ident, eps, hi, lo, ring):
    with Room(nc, "sgu") as r:
        ws = r.sb("ws", [P, SGU_G, P])
        bs = r.sb("bs", [P, SGU_G * P])
        v = [r.sb(f"v{b}", [P, D]) for b in range(NB)]
        square = r.sb("square", [P, D])
        stat = r.sb("stat", [P, NB, 4])
        gated = [r.sb(f"gated{j}", [P, NB, P]) for j in range(2)]
        prod = [r.sb(f"prod{j}", [P, SEQ]) for j in range(2)]
        ps_t = [r.ps(f"ps_t{j}", [P, 2, 512]) for j in range(2)]
        ps_m = [r.ps(f"ps_m{j}", [P, NB, P]) for j in range(2)]
        names = ("in", "t", "v", "sq", "std", "rs", "vn", "m", "sv", "pr", "hi", "lo")
        q = {x: r.sem(x) for x in names}
        block = r.block()

        @block.sync
        def _(sp):
            sp.dma_start(ws[:, :, :], t["sgu_wT"]).then_inc(q["in"], 16)
            sp.dma_start(bs[:, :], t["gs_b_s"].partition_broadcast(P)).then_inc(q["in"], 16)
            preload(r, sp, ring, t["w_gs_out"])

        @block.tensor
        def _(pe):
            for b in range(NB):
                if b >= 2:
                    pe.wait_ge(q["v"], b - 1)
                for m in range(KD):
                    mm = nc.tensor.transpose(ps_t[b % 2][:, m // 4, (m % 4) * P:(m % 4 + 1) * P],
                                             zT[:, KD + m, b * P:(b + 1) * P], ident[:, :])
                mm.then_inc(q["t"], 1)
            pe.wait_ge(q["vn"], NB)
            pe.wait_ge(q["in"], 32)
            for g in range(SGU_G):
                if g >= 2:
                    pe.wait_ge(q["sv"], g - 1)
                for b in range(NB):
                    mm = nc.tensor.matmul(ps_m[g % 2][:, b, :], v[b][:, g * P:(g + 1) * P], ws[:, g, :],
                                          start=True, stop=True)
                mm.then_inc(q["m"], 1)

        @block.scalar
        def _(act):
            for b in range(NB):
                act.wait_ge(q["v"], b + 1)
                if b >= 1:
                    act.wait_ge(q["sq"], b)
                act.activation(square[:, :], v[b][:, :], ACT.Square, accum_out=stat[:, b, 0:1]).then_inc(q["sq"], 1)
                act.wait_ge(q["sq"], b + 1)
                act.activation(stat[:, b, 1:2], stat[:, b, 0:1], ACT.Sqrt, bias=eps[:, 0:1],
                               scale=1.0 / D).then_inc(q["std"], 1)
            for g in range(SGU_G):
                act.wait_ge(q["pr"], g + 1)
                act.activation(hi[:, g, :], prod[g % 2][:, :], ACT.Copy).then_inc(q["hi"], 1)

        @block.vector
        def _(dve):
            def scale_rows(b):
                dve.wait_ge(q["std"], b + 1)
                nc.vector.reciprocal(stat[:, b, 2:3], stat[:, b, 1:2]).then_inc(q["rs"], 1)
                dve.wait_ge(q["rs"], b + 1)
                nc.vector.tensor_scalar(v[b][:, :], v[b][:, :], stat[:, b, 2:3], None, ALU.mult).then_inc(q["vn"], 1)

            for b in range(NB):
                dve.wait_ge(q["t"], b + 1)
                nc.vector.tensor_copy(v[b][:, :], ps_t[b % 2][:, :, :].rearrange("p a n -> p (a n)")).then_inc(q["v"], 1)
                if b >= 1:
                    scale_rows(b - 1)
            scale_rows(NB - 1)
            dve.wait_ge(q["in"], 32)

            def low(g):
                dve.wait_ge(q["hi"], g + 1)
                nc.vector.tensor_tensor(lo[:, g, :], prod[g % 2][:, :], f32(hi[:, g, :]), ALU.subtract).then_inc(q["lo"], 1)

            for g in range(SGU_G):
                dve.wait_ge(q["m"], g + 1)
                if g >= 2:
                    dve.wait_ge(q["pr"], g - 1)
                nc.vector.scalar_tensor_tensor(
                    out=gated[g % 2][:, :, :], in0=ps_m[g % 2][:, :, :],
                    scalar=small[:, ROW_SGU + g:ROW_SGU + g + 1],
                    in1=bs[:, g * P:(g + 1) * P].unsqueeze(1).broadcast_to([P, NB, P]),
                    op0=ALU.mult, op1=ALU.add).then_inc(q["sv"], 1)
                dve.wait_ge(q["sv"], g + 1)
                if g >= 2:
                    dve.wait_ge(q["lo"], g - 1)
                nc.vector.tensor_tensor(prod[g % 2][:, :], gated[g % 2][:, :, :].rearrange("p b n -> p (b n)"),
                                        zT[:, g, :], ALU.mult).then_inc(q["pr"], 1)
                if g >= 1:
                    low(g - 1)
            low(SGU_G - 1)


def scores_phase(nc, t, l, qT, keys, s, ring):
    with Room(nc, f"keys{l}") as r:
        ps = [r.ps(f"ps{j}", [P, NB, P]) for j in range(2)]
        s_mm, s_out = (r.sem(x) for x in ("multiplied", "taken"))
        block = r.block()

        @block.sync
        def _(sp):
            preload(r, sp, ring, t["uT"][l])

        @block.tensor
        def _(pe):
            for m in range(HS):
                if m >= 2:
                    pe.wait_ge(s_out, m - 1)
                for b in range(NB):
                    mm = nc.tensor.matmul(ps[m % 2][:, b, :], qT[:, m, b * P:(b + 1) * P], keys[:, m, :],
                                          start=True, stop=True)
                mm.then_inc(s_mm, 1)

        @block.vector
        def _(dve):
            for m in range(HS):
                dve.wait_ge(s_mm, m + 1)
                nc.vector.tensor_copy(s[:, :, m, :], ps[m % 2][:, :, :]).then_inc(s_out, 1)


def route_and_up_phase(nc, t, l, s, ring, hi, lo, ident, iota, iota16, g_dram, h_dram):
    with Room(nc, f"up{l}") as r:
        raw = ring
        w_hi = [r.sb(f"w_hi{j}", [P, KD, P], F32R) for j in range(2)]
        w_lo = [r.sb(f"w_lo{j}", [P, KD, P], F32R) for j in range(2)]
        acts = [r.sb(f"acts{j}", [P, SEQ]) for j in range(2)]
        val = r.sb("val", [P, HS, TOPK])
        idx = r.sb("idx", [P, HS, TOPK], U32)
        idx_f = r.sb("idx_f", [P, HS, TOPK])
        cand = r.sb("cand", [P, PH, TOPK * TOPK])
        best = r.sb("best", [P, PH, TOPK])
        less = r.sb("less", [P, PH, TOPK])
        pos = r.sb("pos", [P, HK], U32)
        pos_i = r.sb("pos_i", [P, 2, HK], U32)
        pos_f = r.sb("pos_f", [P, 2, HK])
        den = r.sb("den", [P, 2, PH])
        pack = r.sb("pack", [P, 3, HK])
        index = r.sb("index", [P, 2, P], BF16)
        piece = r.sb("piece", [P, 3, P], BF16)
        rest = r.sb("rest", [P, 2, P])
        hot1 = r.sb("hot1", [P, 4, NKEYS, TG], BF16)
        hot0 = cand[:, :, :].rearrange("p h n -> p (h n)").bitcast(BF16).rearrange(
            "p (c i k) -> p c i k", c=4, k=TG)
        hot = [hot0, hot1[:, :, :, :]]
        stage = r.sb("stage", [P, NKEYS, P])
        out = [r.ps(f"out{j}", [P, 512]) for j in range(2)]
        ps_t = r.ps("ps_t", [P, 512])
        ps_g = [r.ps(f"ps_g{j}", [P, TG, P]) for j in range(2)]
        s_in = [r.sem(f"in{j}") for j in range(2)]
        s_store = [r.sem(f"act_stored{j}") for j in range(2)]
        s_hi, s_lo, s_mm, s_out, s_free = (r.sem(x) for x in ("hi", "lo", "multiplied", "taken", "free"))
        s_d, s_less, s_exp, s_pack, s_turn, s_one, s_hot, s_gmm, s_gout, s_gst = (
            r.sem(x) for x in ("chain", "less", "exp", "packed", "turned", "onehot", "hot", "gates_multiplied",
                               "gates_taken", "gates_stored"))
        w = t["uT"][l]
        block = r.block()
        PART = P // TG
        PAIRS = PART // 2
        FIRST = [20] + [12] * (NB - 1)
        START = [sum(FIRST[:b]) + b * PART for b in range(NB + 1)]
        SHARES = 8
        SHARE = NKEYS // SHARES

        @block.sync
        def _(sp):
            def loads(first, last):
                with sp.Fori(first // 2, last // 2) as it:
                    for j in range(2):
                        sp.wait_ge(s_lo, it * 2 + j - 1)
                        sp.dma_start(raw[j][:, :, :], w[bass.ds(it * 2 + j, 1)].rearrange("o p k n -> (o p) k n")
                                     ).then_inc(s_in[j], 16)

            for j in range(2):
                sp.sem_inc(s_in[j], 16)
            def store_gates(b, part):
                sp.dma_start(g_dram[bass.ds(part * SHARE, SHARE), :, b * P:(b + 1) * P].rearrange("a p n -> p a n"),
                             stage[:, bass.ds(part * SHARE, SHARE), :]).then_inc(s_gst, 16)

            at = 2
            for b in range(NB):
                loads(at, START[b + 1] + 2)
                at = START[b + 1] + 2
                sp.wait_ge(s_gout, 2 + (b + 1) * PART)
                beside = min(SHARES, NKEYS - at)
                with sp.Fori(0, beside // 2) as it:
                    for j in range(2):
                        sp.wait_ge(s_lo, it * 2 + (at + j - 1))
                        sp.dma_start(raw[j][:, :, :], w[bass.ds(it * 2 + (at + j), 1)].rearrange(
                            "o p k n -> (o p) k n")).then_inc(s_in[j], 16)
                        store_gates(b, it * 2 + j)
                for part in range(beside, SHARES):
                    store_gates(b, part)
                at += beside
            if at < NKEYS:
                loads(at, NKEYS)
            sp.wait_ge(s_gst, 16 * SHARES * NB)

        @block.gpsimd
        def _(pool):
            pool.sem_inc(s_free, 2)
            with pool.Fori(0, NKEYS // 2) as it:
                for j in range(2):
                    pool.wait_ge(s_out, it * 2 + j + 3)
                    pool.dma_start(h_dram[bass.ds(it * 2 + j, 1)].rearrange("o p n -> (o p) n"), acts[j][:, :]
                                   ).then_inc(s_store[j], 16)
                    pool.wait_ge(s_store[j], it * 16 + 16)
                    pool.sem_inc(s_free, 1)

        @block.scalar
        def _(act):
            act.sem_inc(s_out, 2)
            act.sem_inc(s_gout, 2)

            def split_hi(q, j):
                act.wait_ge(s_in[j], q * 16 + 16)
                act.wait_ge(s_mm, q * 2 + j + 1)
                act.activation(w_hi[j][:, :, :], raw[j][:, :, :], ACT.Copy).then_inc(s_hi, 1)

            def gelu(q, j):
                act.wait_ge(s_mm, q * 2 + j + 3)
                act.wait_ge(s_free, q * 2 + j + 1)
                act.activation(acts[j][:, :], out[j][:, :], ACT.Gelu_apprx_tanh).then_inc(s_out, 1)

            def take_gates(b, k, j):
                act.wait_ge(s_gmm, b * PART + k + 3)
                act.activation(stage[:, :, bass.ds(k * TG, TG)], ps_g[j][:, :, :].rearrange("p k n -> p n k"),
                               ACT.Copy).then_inc(s_gout, 1)

            def pair(q, b=None, k=None, last=False):
                split_hi(q, 1)
                gelu(q, 0)
                if b is not None:
                    take_gates(b, k, 0)
                if not last:
                    split_hi(q + 1, 0)
                gelu(q, 1)
                if b is not None:
                    take_gates(b, k + 1, 1)

            split_hi(0, 0)
            for b in range(NB):
                q0, q1 = START[b] // 2, (START[b] + FIRST[b]) // 2
                with act.Fori(q0, q1 - 1) as it:
                    pair(it)
                act.wait_ge(s_less, b + 1)
                act.activation(less[:, :, :], less[:, :, :], ACT.Exp).then_inc(s_exp, 1)
                pair(q1 - 1)
                if b >= 1:
                    act.wait_ge(s_gst, 16 * SHARES * b)
                with act.Fori(0, PAIRS) as it:
                    pair(it + q1, b, it * 2)
            with act.Fori(START[NB] // 2, NKEYS // 2 - 1) as it:
                pair(it)
            pair(NKEYS // 2 - 1, last=True)

        @block.tensor
        def _(pe):
            pe.sem_inc(s_mm, 2)
            pe.sem_inc(s_gmm, 2)

            def up(q, j):
                pe.wait_ge(s_lo, q * 2 + j + 1)
                pe.wait_ge(s_out, q * 2 + j + 1)
                for k in range(KD):
                    mm = three_passes(nc, out[j][:, :], w_hi[j][:, k, :], w_lo[j][:, k, :],
                                      hi[:, k, :], lo[:, k, :], k == 0, k == KD - 1)
                mm.then_inc(s_mm, 1)

            for b in range(NB):
                with pe.Fori(START[b] // 2, (START[b] + FIRST[b]) // 2) as it:
                    up(it, 0)
                    up(it, 1)
                pe.wait_ge(s_pack, b + 1)
                for c in range(3):
                    mm = nc.tensor.transpose(ps_t[:, c * P:(c + 1) * P], pack[:, c, :], ident[:, :])
                mm.then_inc(s_turn, 1)
                with pe.Fori(0, PAIRS) as it:
                    for j in range(2):
                        up(it + (START[b] + FIRST[b]) // 2, j)
                        grp = it * 2 + (b * PART + j)
                        pe.wait_ge(s_hot, grp + 1)
                        pe.wait_ge(s_gout, grp + 1)
                        for k in range(TG):
                            for p in range(3):
                                mm = nc.tensor.matmul(ps_g[j][:, k, :], hot[j][:, 3, :, k], hot[j][:, p, :, k],
                                                      start=(p == 0), stop=(p == 2))
                        mm.then_inc(s_gmm, 1)
            with pe.Fori(START[NB] // 2, NKEYS // 2) as it:
                up(it, 0)
                up(it, 1)

        @block.vector
        def _(dve):
            n = [0]

            def after(ins):
                n[0] += 1
                ins.then_inc(s_d, 1)
                dve.wait_ge(s_d, n[0])

            def split_lo(q, j):
                dve.wait_ge(s_hi, q * 2 + j + 1)
                nc.vector.tensor_tensor(w_lo[j][:, :, :], raw[j][:, :, :], f32(w_hi[j][:, :, :]),
                                        ALU.subtract).then_inc(s_lo, 1)

            def top16(values, indices, row):
                for half in range(2):
                    part = slice(8 * half, 8 * half + 8)
                    after(nc.vector.max(values[:, part], row))
                    after(nc.vector.max_index(indices[:, part], values[:, part], row))
                    if half == 0:
                        after(nc.vector.match_replace(out=row, in_to_replace=values[:, part], in_values=row,
                                                      imm_value=-3.0e38))

            v2 = val[:, :, :].rearrange("p (h s) k -> p h s k", s=2)
            i2v = idx_f[:, :, :].rearrange("p (h s) k -> p h s k", s=2)
            pick = cand[:, :, :].rearrange("p h (k a) -> p h k a", a=TOPK)
            grid = [P, PH, TOPK, TOPK]

            def candidates(b, h):
                if b >= 1 and h == 0:
                    dve.wait_ge(s_gmm, 2 + b * PART)
                c = cand[:, h, :].rearrange("p (a b) -> p a b", b=TOPK)
                after(nc.vector.tensor_tensor(c, v2[:, h, 0, :].unsqueeze(2).broadcast_to([P, TOPK, TOPK]),
                                              v2[:, h, 1, :].unsqueeze(1).broadcast_to([P, TOPK, TOPK]), ALU.add))
                top16(best[:, h, :], pos[:, h * TOPK:(h + 1) * TOPK], cand[:, h, :])

            def positions(b):
                nc.vector.tensor_tensor(less[:, :, :], best[:, :, :], best[:, :, 0:1].broadcast_to([P, PH, TOPK]),
                                        ALU.subtract).then_inc(s_less, 1)
                nc.vector.tensor_single_scalar(pos_i[:, 0, :], pos[:, :], 4, ALU.logical_shift_right)
                after(nc.vector.tensor_single_scalar(pos_i[:, 1, :], pos[:, :], 15, ALU.bitwise_and))
                after(nc.vector.tensor_copy(pos_f[:, :, :], pos_i[:, :, :]))
                after(nc.vector.tensor_copy(idx_f[:, :, :], idx[:, :, :]))

            def pick_where(side):
                p3 = pos_f[:, side, :].rearrange("p (h k) -> p h k", k=TOPK)
                after(nc.vector.tensor_tensor(pick, p3.unsqueeze(3).broadcast_to(grid),
                                              iota16[:, :].unsqueeze(1).unsqueeze(1).broadcast_to(grid), ALU.is_equal))

            def pick_times(side):
                after(nc.vector.tensor_tensor(pick, pick, i2v[:, :, side, :].unsqueeze(2).broadcast_to(grid), ALU.mult))

            def pick_sum(side):
                after(nc.vector.reduce_sum(pack[:, side, :], pick.rearrange("p h k a -> p (h k) a"), AX.X))

            def softmax(b):
                dve.wait_ge(s_exp, b + 1)
                after(nc.vector.reduce_sum(den[:, 0, :], less[:, :, :], AX.X))
                after(nc.vector.reciprocal(den[:, 1, :], den[:, 0, :]))
                nc.vector.tensor_tensor(pack[:, 2, :].rearrange("p (h k) -> p h k", k=TOPK), less[:, :, :],
                                        den[:, 1, :].unsqueeze(2).broadcast_to([P, PH, TOPK]),
                                        ALU.mult).then_inc(s_pack, 1)

            def columns(b):
                dve.wait_ge(s_turn, b + 1)
                nc.vector.tensor_copy(index[:, :, :], ps_t[:, 0:2 * P].rearrange("p (c n) -> p c n", n=P))
                gate = ps_t[:, 2 * P:3 * P]
                after(nc.vector.tensor_copy(piece[:, 0, :], gate))
                after(nc.vector.tensor_tensor(rest[:, 0, :], gate, piece[:, 0, :], ALU.subtract))
                after(nc.vector.tensor_copy(piece[:, 1, :], rest[:, 0, :]))
                after(nc.vector.tensor_tensor(rest[:, 1, :], rest[:, 0, :], piece[:, 1, :], ALU.subtract))
                after(nc.vector.tensor_copy(piece[:, 2, :], rest[:, 1, :]))

            def one_hots(b, k, j):
                grp = k + b * PART
                dve.wait_ge(s_gmm, grp + 1)
                at = bass.ds(k * TG, TG)
                shape = [P, NKEYS, TG]
                nc.vector.tensor_tensor(hot[j][:, 0, :, :], iota[:, :, :],
                                        index[:, 0, at].unsqueeze(1).broadcast_to(shape), ALU.is_equal).then_inc(s_one, 1)
                nc.vector.tensor_tensor(hot[j][:, 3, :, :], iota[:, :, :],
                                        index[:, 1, at].unsqueeze(1).broadcast_to(shape), ALU.is_equal)
                dve.wait_ge(s_one, grp + 1)
                for p in (2, 1, 0):
                    last = nc.vector.tensor_tensor(hot[j][:, p, :, :], hot[j][:, 0, :, :],
                                                   piece[:, p, at].unsqueeze(1).broadcast_to(shape), ALU.mult)
                last.then_inc(s_hot, 1)

            def keys(b, m):
                top16(val[:, m, :], idx[:, m, :], s[:, b, m, :])

            def next_split(c):
                if c + 1 < NKEYS:
                    split_lo((c + 1) // 2, (c + 1) % 2)

            split_lo(0, 0)
            for b in range(NB):
                beside = [[(candidates, (b, h)) for h in heads] for heads in ((0,), (1, 2), (3,), (4, 5), (6,), (7,))]
                beside[-1].append((positions, (b,)))
                beside += [[(pick_where, (0,))], [(pick_times, (0,))], [(pick_sum, (0,)), (pick_where, (1,))],
                           [(pick_times, (1,))], [(pick_sum, (1,)), (softmax, (b,))], []]
                if b == 0:
                    beside = [[(keys, (0, m)) for m in range(2 * i, 2 * i + 2)] for i in range(HS // 2)] + beside
                assert len(beside) == FIRST[b]
                for c, work in enumerate(beside):
                    next_split(START[b] + c)
                    for f, args in work:
                        f(*args)
                columns(b)
                for k in range(PART):
                    one_hots(b, k, k % 2)
                    next_split(START[b] + FIRST[b] + k)
                    if b + 1 < NB:
                        keys(b + 1, k)
            with dve.Fori(START[NB] // 2, NKEYS // 2 - 1) as it:
                split_lo(it, 1)
                split_lo(it + 1, 0)
            split_lo(NKEYS // 2 - 1, 1)


def down_phase(nc, t, l, ring, g_dram, h_dram, xT, gate):
    with Room(nc, f"down{l}") as r:
        C = 4
        GROUPS = NKEYS // C
        raw = [x[:, :, :].rearrange("p k n -> p (k n)") for x in ring]
        gin = [r.sb(f"gin{j}", [P, SEQ]) for j in range(2)]
        hin = [r.sb(f"hin{j}", [P, SEQ]) for j in range(2)]
        wgt = [r.sb(f"wgt{j}", [P, SEQ]) for j in range(2)]
        v_hi = [r.sb(f"v_hi{j}", [P, C, D], F32R) for j in range(2)]
        v_lo = [r.sb(f"v_lo{j}", [P, C, D], F32R) for j in range(2)]
        w_hi = [r.sb(f"w_hi{j}", [P, C, SEQ], F32R) for j in range(2)]
        w_lo = [r.sb(f"w_lo{j}", [P, C, SEQ], F32R) for j in range(2)]
        acc = r.sb("acc", [P, KD, SEQ])
        out = [r.ps(f"out{j}", [P, 512]) for j in range(KD)]
        s_v = [r.sem(f"v_in{j}") for j in range(2)]
        s_g = [r.sem(f"gh_in{j}") for j in range(2)]
        s_vhi, s_vlo, s_w, s_whi, s_wlo, s_mm, s_acc, s_out = (
            r.sem(x) for x in ("vhi", "vlo", "w", "whi", "wlo", "multiplied", "acc", "residual_added"))
        v_dram = t["peer_v"][l]
        block = r.block()

        @block.sync
        def _(sp):
            def load(c, j):
                sp.dma_start(raw[j], v_dram[bass.ds(c, 1)].rearrange("o p n -> (o p) n")).then_inc(s_v[j], 16)
                sp.dma_start(gin[j][:, :], g_dram[bass.ds(c, 1)].rearrange("o p n -> (o p) n")).then_inc(s_g[j], 16)
                sp.dma_start(hin[j][:, :], h_dram[bass.ds(c, 1)].rearrange("o p n -> (o p) n")).then_inc(s_g[j], 16)
            for j in range(2):
                load(j, j)
            with sp.Fori(1, NKEYS // 2) as it:
                for j in range(2):
                    sp.wait_ge(s_vlo, it * 2 + j - 1)
                    sp.wait_ge(s_w, it * 2 + j - 1)
                    load(it * 2 + j, j)

        @block.scalar
        def _(act):
            with act.Fori(0, GROUPS // 2) as it:
                for s in range(2):
                    act.wait_ge(s_mm, (it * 2 + s + 1) * KD)
                    for i in range(C):
                        j = i % 2
                        c = (it * 2 + s) * C + i
                        act.wait_ge(s_v[j], (it * C + s * (C // 2) + i // 2 + 1) * 16)
                        act.activation(v_hi[s][:, i, :], raw[j], ACT.Copy).then_inc(s_vhi, 1)
                        act.wait_ge(s_w, c + 1)
                        act.activation(w_hi[s][:, i, :], wgt[j][:, :], ACT.Copy).then_inc(s_whi, 1)

        @block.vector
        def _(dve):
            dve.sem_inc(s_acc, 2 * KD)

            def add_up(g):
                for m in range(KD):
                    dve.wait_ge(s_mm, g * KD + (2 * KD + m + 1))
                    nc.vector.tensor_tensor(acc[:, m, :], acc[:, m, :], out[m][:, :], ALU.add).then_inc(s_acc, 1)

            def group(g, s, it):
                for i in range(C):
                    j = i % 2
                    c = g * C + i
                    dve.wait_ge(s_g[j], (it * C + s * (C // 2) + i // 2 + 1) * 32)
                    nc.vector.tensor_tensor(wgt[j][:, :], gin[j][:, :], hin[j][:, :], ALU.mult).then_inc(s_w, 1)
                    dve.wait_ge(s_vhi, c + 1)
                    nc.vector.tensor_tensor(v_lo[s][:, i, :], raw[j], f32(v_hi[s][:, i, :]),
                                            ALU.subtract).then_inc(s_vlo, 1)
                    dve.wait_ge(s_whi, c + 1)
                    nc.vector.tensor_tensor(w_lo[s][:, i, :], wgt[j][:, :], f32(w_hi[s][:, i, :]),
                                            ALU.subtract).then_inc(s_wlo, 1)

            group(0, 0, 0)
            group(1, 1, 0)
            for m in range(KD):
                dve.wait_ge(s_mm, 2 * KD + m + 1)
                nc.vector.tensor_copy(acc[:, m, :], out[m][:, :]).then_inc(s_acc, 1)
            with dve.Fori(1, GROUPS // 2) as it:
                for s in range(2):
                    group(it * 2 + s, s, it)
                    add_up(it * 2 + s - 1)
            g = GROUPS - 1
            for m in range(KD + 1):
                if m < KD:
                    dve.wait_ge(s_mm, g * KD + (2 * KD + m + 1))
                    nc.vector.tensor_tensor(acc[:, m, :], acc[:, m, :], out[m][:, :], ALU.add).then_inc(s_acc, 1)
                if m >= 1:
                    dve.wait_ge(s_acc, 2 * KD + g * KD + m)
                    nc.vector.scalar_tensor_tensor(out=xT[:, m - 1, :], in0=acc[:, m - 1, :], scalar=gate[:, m - 1:m],
                                                   in1=xT[:, m - 1, :], op0=ALU.mult, op1=ALU.add).then_inc(s_out, 1)

        @block.tensor
        def _(pe):
            pe.sem_inc(s_mm, 2 * KD)

            def halves(g, i):
                pe.wait_ge(s_vlo, g * C + i + 1)
                pe.wait_ge(s_wlo, g * C + i + 1)

            def chunk(s, m, i):
                return three_passes(nc, out[m][:, :], v_hi[s][:, i, m * P:(m + 1) * P],
                                    v_lo[s][:, i, m * P:(m + 1) * P], w_hi[s][:, i, :], w_lo[s][:, i, :],
                                    i == 0, i == C - 1)

            def group(g, s):
                for m in range(KD):
                    pe.wait_ge(s_acc, (g + 1) * KD + m + 1)
                    for i in range(C):
                        if m == 0:
                            halves(g, i)
                        mm = chunk(s, m, i)
                    mm.then_inc(s_mm, 1)

            pe.wait_ge(s_acc, 2 * KD)
            for i in range(C):
                halves(0, i)
                for m in range(KD):
                    mm = chunk(0, m, i)
                    if i == C - 1:
                        mm.then_inc(s_mm, 1)
            group(1, 1)
            with pe.Fori(1, GROUPS // 2) as it:
                for s in range(2):
                    group(it * 2 + s, s)


def program(nc, t, out):
    g_dram = nc.dram_tensor("gates", (NKEYS, NKEYS, SEQ), F32, kind="Internal").ap()
    h_dram = nc.dram_tensor("activations", (NKEYS, NKEYS, SEQ), F32, kind="Internal").ap()
    with Room(nc, "all") as r:
        xT = r.sb("xT", [P, KD, SEQ])
        hi = r.sb("h_hi", [P, KD, SEQ], F32R)
        lo = r.sb("h_lo", [P, KD, SEQ], F32R)
        small = r.sb("small", [P, SMALL_ROWS])
        ada = r.sb("ada", [P, 2, DEPTH * ADA_ROWS])
        ident = r.sb("ident", [P, P])
        ones = r.sb("ones", [P, P])
        eps = r.sb("eps", [P, 1])
        iota_b = r.sb("iota_b", [P, NKEYS, TG], BF16)
        iota16 = r.sb("iota16", [P, TOPK])
        ring = [r.sb(f"ring{j}", [P, KD, P]) for j in range(2)]

        def mod(l, which, cond=0):
            at = (l * N_MOD + which) * KD
            return ada[:, cond, at:at + KD]

        with Room(nc, "mix0") as m0:
            kvcT = m0.sb("kvcT", [P, 2, CTX])
            with Room(nc, "ctx") as cr:
                ctxT = cr.sb("ctxT", [P, KD, CTX])
                load_phase(nc, t, xT, small, ada, ident,
                           [(ctxT[:, :, :], t["ctxT"]), (iota_b[:, :, :], t["iota_b"]), (iota16[:, :], t["iota16"])])
                with Room(nc, "const") as c:
                    s_m = c.sem("set")
                    block = c.block()

                    @block.vector
                    def _(dve):
                        nc.vector.memset(ones[:, :], 1.0).then_inc(s_m, 1)
                        nc.vector.memset(eps[:, :], EPS).then_inc(s_m, 1)
                        dve.wait_ge(s_m, 2)

                c_hi = cr.sb("c_hi", [P, KD, CTX], F32R)
                c_lo = cr.sb("c_lo", [P, KD, CTX], F32R)
                norm_phase(nc, "nctx", ctxT, CTX, small[:, ROW_MIX:ROW_MIX + KD], mod(0, SH_M, 1), mod(0, SC_M, 1),
                           c_hi, c_lo, ones, eps, ring=ring, next_w=t["w_in"][4:6])
                gemm_phase(nc, "kvctx", ring, t["w_in"][4:6], 2, c_hi, c_lo, CTX,
                           take_act=lambda k, ps: nc.scalar.activation(
                               kvcT[:, bass.ds(k, 1), :].rearrange("p o n -> p (o n)"), ps, ACT.Copy))
            mixT = m0.sb("mixT", [P, 6 + FG, SEQ])
            with Room(nc, "ropet") as rt:
                swap = rt.sb("swap", [P, P])
                cos = rt.sb("cos", [P, SEQ])
                sin = rt.sb("sin", [P, SEQ])
                norm_phase(nc, "nmix0", xT, SEQ, small[:, ROW_MIX:ROW_MIX + KD], mod(0, SH_M), mod(0, SC_M),
                           hi, lo, ones, eps, ring=ring, next_w=t["w_in"])
                gemm_phase(nc, "in", ring, t["w_in"], 6 + FG, hi, lo, SEQ,
                           take_act=lambda k, ps: nc.scalar.activation(
                               mixT[:, bass.ds(k, 1), :].rearrange("p o n -> p (o n)"), ps, ACT.Copy),
                           also=[(swap[:, :], t["swap"]), (cos[:, :], t["rope_cos"]), (sin[:, :], t["rope_sin"])])
                rope_phase(nc, mixT, swap, cos, sin)
            tables = (m0.sb("chan", [P, 2 * P]), m0.sb("seq_c", [P, NB, SEQ]), m0.sb("seq_s", [P, NB, SEQ]))
            attention_phase(nc, t, mixT, kvcT[:, 0, :], mixT[:, 5, :], kvcT[:, 1, :], ident, hi, lo, tables)
            fourier_phase(nc, t, mixT[:, 6:6 + FG, :], tables, hi, lo, ring)
        gemm_phase(nc, "about", ring, t["w_ab_out"], KD, hi, lo, SEQ, take_dve=residual(nc, xT, mod(0, G_M)))

        for l in range(DEPTH):
            if l == 1:
                norm_phase(nc, "nmix1", xT, SEQ, small[:, ROW_MIX + KD:ROW_MIX + 2 * KD], mod(1, SH_M), mod(1, SC_M),
                           hi, lo, ones, eps, ring=ring, next_w=t["w_gs_in"])
                with Room(nc, "mix1") as m1:
                    zT = m1.sb("zT", [P, 2 * KD, SEQ])
                    gemm_phase(nc, "gsin", ring, t["w_gs_in"], 2 * KD, hi, lo, SEQ,
                               take_act=lambda k, ps: nc.scalar.activation(
                                   zT[:, bass.ds(k, 1), :].rearrange("p o n -> p (o n)"), ps, ACT.Gelu_apprx_tanh))
                    sgu_phase(nc, t, zT, small, ident, eps, hi, lo, ring)
                gemm_phase(nc, "gsout", ring, t["w_gs_out"], KD, hi, lo, SEQ, take_dve=residual(nc, xT, mod(1, G_M)))
            ffn_w = small[:, ROW_FFN + l * KD:ROW_FFN + (l + 1) * KD]
            norm_phase(nc, f"nffn{l}", xT, SEQ, ffn_w, mod(l, SH_F), mod(l, SC_F), hi, lo, ones, eps,
                       ring=ring, next_w=t["w_peer_q"][l])
            with Room(nc, f"rout{l}") as rr:
                s = rr.sb("s", [P, NB, HS, NKEYS])
                with Room(nc, f"qs{l}") as qr:
                    qT = qr.sb("qT", [P, HS, SEQ])
                    keys = qr.sb("keys", [P, HS, NKEYS])
                    gemm_phase(nc, f"peerq{l}", ring, t["w_peer_q"][l], HS, hi, lo, SEQ,
                               take_act=lambda k, ps: nc.scalar.activation(
                                   qT[:, bass.ds(k, 1), :].rearrange("p o n -> p (o n)"), ps, ACT.Copy),
                               also=[(keys[:, :, :], t["keysT"][l])])
                    scores_phase(nc, t, l, qT, keys, s, ring)
                route_and_up_phase(nc, t, l, s, ring, hi, lo, ident, iota_b, iota16, g_dram, h_dram)
            down_phase(nc, t, l, ring, g_dram, h_dram, xT, mod(l, G_F))

        with Room(nc, "final") as fr:
            y = fr.sb("y", [P, KD, SEQ])
            norm_phase(nc, "nout", xT, SEQ, small[:, ROW_OUT:ROW_OUT + KD], None, None, None, None, ones, eps, plain=y)
            s_o = fr.sem("out")
            block = fr.block()

            @block.sync
            def _(sp):
                sp.dma_start(out, y[:, :, :]).then_inc(s_o, 16)
                sp.wait_ge(s_o, 16)


def tiles_of(w):
    k, n = w.shape
    return w.reshape(k // P, P, n // P, P).transpose(2, 1, 0, 3)


def channels_first(x):
    return x.reshape(x.shape[0], KD, P).transpose(2, 1, 0)


def constants():
    half = HEAD_DIM // 2
    inv = np.float32(THETA) ** (-np.arange(0, half, 2, dtype=np.float32) / half)
    tok = np.arange(SEQ)
    row = (tok // GRID_W).astype(np.float32)[:, None] * inv
    col = (tok % GRID_W).astype(np.float32)[:, None] * inv
    cos, sin, swap = np.zeros((P, SEQ)), np.zeros((P, SEQ)), np.zeros((P, P))
    for p in range(P):
        d = p % HEAD_DIM
        ang = (row if d < half else col)[:, d % (half // 2)]
        low = d % half < half // 2
        cos[p] = np.cos(ang)
        sin[p] = -np.sin(ang) if low else np.sin(ang)
        swap[p + (half // 2 if low else -(half // 2)), p] = 1
    i, j = np.arange(P)[:, None], np.arange(P)[None, :]
    mask = np.stack([np.where(j >= i, 0, NEG), np.where(j <= i, 0, NEG)], 1)

    def dft(n):
        a = 2 * np.pi * (np.outer(np.arange(n), np.arange(n)) % n) / n
        return np.cos(a) / np.sqrt(n), np.sin(a) / np.sqrt(n)

    cc, sc = dft(P)
    cn, sn = dft(SEQ)
    blocks = lambda a: a.reshape(NB, P, SEQ).transpose(1, 0, 2)
    out = {
        "identity": np.eye(P), "rope_cos": cos, "rope_sin": sin, "swap": swap, "band_mask": mask,
        "dft_chan": np.concatenate([cc, sc], 1), "dft_cos": blocks(cn), "dft_msin": blocks(-sn),
        "iota16": np.tile(np.arange(TOPK), (P, 1)),
    }
    out = {k: np.ascontiguousarray(v, dtype=np.float32) for k, v in out.items()}
    out["iota_b"] = np.broadcast_to(np.arange(NKEYS)[None, :, None], (P, NKEYS, TG)).astype(mybir.dt.np(BF16))
    return out


def kernel(**inputs):
    import concourse.bacc as bacc
    from concourse.bass_utils import run_bass_kernel_spmd

    a = {k: np.asarray(v) for k, v in inputs.items()}
    w_in = a["ab_w_in"][0]
    wq = w_in[:, :HEADS * HEAD_DIM].reshape(D, KV_HEADS, Q_PER_KV, HEAD_DIM).transpose(0, 2, 1, 3).reshape(D, -1)
    w_in = np.concatenate([wq, w_in[:, HEADS * HEAD_DIM:]], 1)
    w_out = a["ab_w_out"][0]
    wa = w_out[:HEADS * HEAD_DIM].reshape(KV_HEADS, Q_PER_KV, HEAD_DIM, D).transpose(1, 0, 2, 3).reshape(-1, D)
    w_out = np.concatenate([wa, w_out[HEADS * HEAD_DIM:]], 0)
    rows = [a["c"][0], a["c_ctx"], a["norm_mix_w"].reshape(-1), a["norm_ffn_w"].reshape(-1), a["norm_out_w"],
            a["gs_norm_w"][0]]
    arrays = {
        "xT": channels_first(a["x"][0]), "ctxT": channels_first(a["ctx"][0]),
        "small_rows": np.concatenate(rows).reshape(SMALL_ROWS, P),
        "ada_b_rows": a["ada_b"].reshape(DEPTH * ADA_ROWS, P),
        "ada_tiles": a["ada_w"].reshape(DEPTH, KD, P, N_MOD, D).transpose(0, 3, 2, 1, 4).reshape(-1, P, KD, D),
        "w_in": tiles_of(w_in), "w_ab_out": tiles_of(w_out),
        "w_gs_in": tiles_of(a["gs_w_in"][0]), "w_gs_out": tiles_of(a["gs_w_out"][0]),
        "w_peer_q": np.stack([tiles_of(w) for w in a["peer_w_q"]]),
        "attn_sink": a["attn_sink"][0], "gs_b_s": a["gs_b_s"][0].reshape(-1),
        "sgu_wT": a["gs_w_s"][0].transpose(2, 0, 1),
        "keysT": a["peer_keys"].reshape(DEPTH, HS, NKEYS, P).transpose(0, 3, 1, 2),
        "uT": a["peer_u"].reshape(DEPTH, NKEYS, NKEYS, KD, P).transpose(0, 1, 4, 3, 2),
        "peer_v": a["peer_v"].reshape(DEPTH, NKEYS, NKEYS, D),
    }
    arrays.update(constants())
    arrays = {k: np.ascontiguousarray(v) for k, v in arrays.items()}
    nc = bacc.Bacc("TRN2", target_bir_lowering=False, num_devices=1)
    t = {k: nc.dram_tensor(f"in_{k}", v.shape, mybir.dt.from_np(v.dtype), kind="ExternalInput").ap()
         for k, v in arrays.items()}
    out = nc.dram_tensor("out_T", (P, KD, SEQ), F32, kind="ExternalOutput").ap()
    program(nc, t, out)
    r = run_bass_kernel_spmd(nc, [{f"in_{k}": v for k, v in arrays.items()}], core_ids=[0])
    got = r.results[0]["out_T"]
    return np.ascontiguousarray(got.transpose(2, 1, 0)).reshape(1, SEQ, D)
```
